# Optimizing a Trainium2 kernel written in Bass

```python
import jax, jax.numpy as jnp
from jax import lax
import numpy as np

D_MODEL = 1024
BATCH = 1
SEQ = 512
DEPTH = 2

GRID_W = 64
CTX_LEN = 256
N_EVEN = (DEPTH + 1) // 2
N_ODD = DEPTH // 2
HEAD_DIM = 64
BLK = 128
POOL_WINDOWS = (2, 4, 8, 16)
POOL_GROUPS = 4
POOL_CH = D_MODEL // 2
POOL_GC = POOL_CH // POOL_GROUPS
B_HEADS = (D_MODEL // 2) // HEAD_DIM
B_KV = B_HEADS // 4
WINDOW = 128
AB_IN = POOL_CH + (B_HEADS + 2 * B_KV) * HEAD_DIM
C_HEADS = D_MODEL // HEAD_DIM
C_KV = C_HEADS // 4
C_IN = (C_HEADS + 2 * C_KV) * HEAD_DIM
D_FF = (8 * D_MODEL // 3) // 128 * 128
ROPE_BASE = 10000.0
EPS = 1e-6
NEG = -1e30

kernel_name = "hybrid_pool_window_global_convffn_dit"

def rms_norm(x, g):
    xf = x.astype(jnp.float32)
    y = xf * lax.rsqrt(jnp.mean(xf * xf, axis=-1, keepdims=True) + EPS)
    return (y * g.astype(jnp.float32)).astype(x.dtype)

def rope_tables(T):
    rows = T // GRID_W
    row = jnp.repeat(jnp.arange(rows), GRID_W).astype(jnp.float32)
    col = jnp.tile(jnp.arange(GRID_W), rows).astype(jnp.float32)
    n_freq = HEAD_DIM // 4
    freqs = ROPE_BASE ** (-jnp.arange(n_freq, dtype=jnp.float32) / n_freq)
    ang = jnp.concatenate([row[:, None] * freqs, col[:, None] * freqs], axis=-1)
    return jnp.cos(ang), jnp.sin(ang)

def apply_rope(x, cos, sin):
    half = HEAD_DIM // 2
    T = x.shape[1]
    shp = (1, T) + (1,) * (x.ndim - 3) + (half,)
    c, s = cos.reshape(shp), sin.reshape(shp)
    xf = x.astype(jnp.float32)
    x1, x2 = xf[..., :half], xf[..., half:]
    return jnp.concatenate([x1 * c - x2 * s, x2 * c + x1 * s], axis=-1).astype(x.dtype)

def attend(q, k, v, mask=None, sink=None):
    s = jnp.einsum('bqhgd,bkhd->bhgqk', q, k).astype(jnp.float32) * (HEAD_DIM ** -0.5)
    if mask is not None:
        s = jnp.where(mask, s, NEG)
    m = jnp.max(s, axis=-1, keepdims=True)
    if sink is not None:
        sk = sink.astype(jnp.float32)[None, :, :, None, None]
        m = jnp.maximum(m, sk)
    e = jnp.exp(s - m)
    den = jnp.sum(e, axis=-1, keepdims=True)
    if sink is not None:
        den = den + jnp.exp(sk - m)
    p = (e / den).astype(v.dtype)
    return jnp.einsum('bhgqk,bkhd->bqhgd', p, v)

def windowed_latent_attention(q, k, v, kc, vc, sink):
    B, T = q.shape[:2]
    nb = T // BLK
    pad = ((0, 0), (BLK, BLK), (0, 0), (0, 0))
    kp, vp = jnp.pad(k, pad), jnp.pad(v, pad)
    qi = jnp.arange(BLK)[:, None]
    ki = jnp.arange(3 * BLK)[None, :]
    ctx_ok = jnp.ones((BLK, kc.shape[1]), dtype=bool)

    def block(n):
        start = n * BLK
        qb = lax.dynamic_slice_in_dim(q, start, BLK, axis=1)
        kb = jnp.concatenate([lax.dynamic_slice_in_dim(kp, start, 3 * BLK, axis=1), kc], axis=1)
        vb = jnp.concatenate([lax.dynamic_slice_in_dim(vp, start, 3 * BLK, axis=1), vc], axis=1)
        qpos = start + qi
        kpos = start - BLK + ki
        band = (jnp.abs(qpos - kpos) <= WINDOW) & (kpos >= 0) & (kpos < T)
        mask = jnp.concatenate([band, ctx_ok], axis=1)
        return attend(qb, kb, vb, mask, sink)

    out = lax.map(block, jnp.arange(nb))
    return jnp.moveaxis(out, 0, 1).reshape(B, T, -1)

def global_latent_attention(q, k_all, v_all):
    B, T = q.shape[:2]
    nb = T // BLK

    def block(n):
        qb = lax.dynamic_slice_in_dim(q, n * BLK, BLK, axis=1)
        return attend(qb, k_all, v_all)

    out = lax.map(block, jnp.arange(nb))
    return jnp.moveaxis(out, 0, 1).reshape(B, T, -1)

def pool_mix(u, w, scale):
    B, T = u.shape[:2]
    uf = u.astype(jnp.float32)
    cs = jnp.concatenate([jnp.zeros_like(uf[:, :1]), jnp.cumsum(uf, axis=1)], axis=1)
    t = jnp.arange(T)
    means = []
    for g, win in enumerate(POOL_WINDOWS):
        lo = jnp.clip(t - win // 2, 0, T)
        hi = jnp.clip(t + win // 2, 0, T)
        cnt = (hi - lo).astype(jnp.float32)[None, :, None]
        means.append((cs[:, hi, g] - cs[:, lo, g]) / cnt)
    pooled = jnp.stack(means, axis=2)
    d = (pooled - uf).astype(u.dtype)
    y = jnp.einsum('btgc,gce->btge', d, w).reshape(B, T, POOL_CH)
    return y * scale

def split_ab(p):
    B, T = p.shape[:2]
    o = POOL_CH
    u = p[..., :o].reshape(B, T, POOL_GROUPS, POOL_GC)
    q = p[..., o:o + B_HEADS * HEAD_DIM].reshape(B, T, B_KV, B_HEADS // B_KV, HEAD_DIM)
    o += B_HEADS * HEAD_DIM
    k = p[..., o:o + B_KV * HEAD_DIM].reshape(B, T, B_KV, HEAD_DIM)
    o += B_KV * HEAD_DIM
    v = p[..., o:o + B_KV * HEAD_DIM].reshape(B, T, B_KV, HEAD_DIM)
    return u, q, k, v

def mixer_ab(h, hc, w_in, w_out, pool_w, pool_scale, sink, cos, sin, need_ctx):
    u, q, k, v = split_ab(h @ w_in)
    uc, qc, kc, vc = split_ab(hc @ w_in)
    q, k = apply_rope(q, cos, sin), apply_rope(k, cos, sin)
    a = windowed_latent_attention(q, k, v, kc, vc, sink)
    y = jnp.concatenate([pool_mix(u, pool_w, pool_scale), a], axis=-1) @ w_out
    yc = None
    if need_ctx:
        B, L = hc.shape[:2]
        ac = attend(qc, kc, vc, None, sink).reshape(B, L, -1)
        yc = jnp.concatenate([pool_mix(uc, pool_w, pool_scale), ac], axis=-1) @ w_out
    return y, yc

def split_c(p, q_g, k_g):
    B, T = p.shape[:2]
    o = C_HEADS * HEAD_DIM
    q = p[..., :o].reshape(B, T, C_KV, C_HEADS // C_KV, HEAD_DIM)
    k = p[..., o:o + C_KV * HEAD_DIM].reshape(B, T, C_KV, HEAD_DIM)
    o += C_KV * HEAD_DIM
    v = p[..., o:o + C_KV * HEAD_DIM].reshape(B, T, C_KV, HEAD_DIM)
    return rms_norm(q, q_g), rms_norm(k, k_g), v

def mixer_c(h, hc, w_qkv, w_out, q_g, k_g, cos, sin, need_ctx):
    q, k, v = split_c(h @ w_qkv, q_g, k_g)
    qc, kc, vc = split_c(hc @ w_qkv, q_g, k_g)
    q, k = apply_rope(q, cos, sin), apply_rope(k, cos, sin)
    k_all = jnp.concatenate([k, kc], axis=1)
    v_all = jnp.concatenate([v, vc], axis=1)
    y = global_latent_attention(q, k_all, v_all) @ w_out
    yc = None
    if need_ctx:
        B, L = hc.shape[:2]
        yc = attend(qc, kc, vc).reshape(B, L, -1) @ w_out
    return y, yc

def conv_ffn(h, w_up, conv_w, conv_b, w_down):
    u = h @ w_up
    up = jnp.pad(u, ((0, 0), (1, 1), (0, 0)))
    u = up[:, :-2] * conv_w[0] + up[:, 1:-1] * conv_w[1] + up[:, 2:] * conv_w[2] + conv_b
    a, b = jnp.split(u, 2, axis=-1)
    return (jax.nn.gelu(a) * b) @ w_down

def ada_params(cvec, w, b):
    return jnp.split(jax.nn.silu(cvec) @ w + b, 6, axis=-1)

def pre_mod(x, g, shift, scale):
    return rms_norm(x, g) * (1 + scale) + shift

def post_add(x, y, g, gate):
    return x + gate * rms_norm(y, g)

def setup_inputs(seed: int = 0) -> dict:
    key = jax.random.key(seed)
    ks = jax.random.split(key, 24)
    f32 = jnp.float32
    D = D_MODEL

    def nrm(k, shape, s):
        return jax.random.normal(k, shape, f32) * s

    return {
        "x": nrm(ks[0], (BATCH, SEQ, D), 1.0),
        "c": nrm(ks[1], (BATCH, D), 1.0),
        "ctx": nrm(ks[2], (BATCH, CTX_LEN, D), 1.0),
        "c_ctx": nrm(ks[3], (D,), 1.0),
        "ada_w": nrm(ks[4], (DEPTH, D, 6 * D), 0.5 * D ** -0.5),
        "ada_b": nrm(ks[5], (DEPTH, 6 * D), 0.02),
        "mix_pre_g": 1.0 + nrm(ks[6], (DEPTH, D), 0.02),
        "mix_post_g": 1.0 + nrm(ks[7], (DEPTH, D), 0.02),
        "ffn_pre_g": 1.0 + nrm(ks[8], (DEPTH, D), 0.02),
        "ffn_post_g": 1.0 + nrm(ks[9], (DEPTH, D), 0.02),
        "ab_w_in": nrm(ks[10], (N_EVEN, D, AB_IN), D ** -0.5),
        "ab_w_out": nrm(ks[11], (N_EVEN, POOL_CH + B_HEADS * HEAD_DIM, D), D ** -0.5),
        "pool_w": nrm(ks[12], (N_EVEN, POOL_GROUPS, POOL_GC, POOL_GC), POOL_GC ** -0.5),
        "pool_scale": 1.0 + nrm(ks[13], (N_EVEN, POOL_CH), 0.1),
        "sink_logit": nrm(ks[14], (N_EVEN, B_KV, B_HEADS // B_KV), 0.5),
        "c_w_qkv": nrm(ks[15], (N_ODD, D, C_IN), D ** -0.5),
        "c_w_out": nrm(ks[16], (N_ODD, C_HEADS * HEAD_DIM, D), D ** -0.5),
        "c_q_g": 1.0 + nrm(ks[17], (N_ODD, HEAD_DIM), 0.02),
        "c_k_g": 1.0 + nrm(ks[18], (N_ODD, HEAD_DIM), 0.02),
        "ffn_w_up": nrm(ks[19], (DEPTH, D, 2 * D_FF), D ** -0.5),
        "ffn_conv_w": nrm(ks[20], (DEPTH, 3, 2 * D_FF), 3 ** -0.5),
        "ffn_conv_b": nrm(ks[21], (DEPTH, 2 * D_FF), 0.02),
        "ffn_w_down": nrm(ks[22], (DEPTH, D_FF, D), D_FF ** -0.5),
    }

def reference(x, c, ctx, c_ctx, ada_w, ada_b, mix_pre_g, mix_post_g, ffn_pre_g, ffn_post_g,
              ab_w_in, ab_w_out, pool_w, pool_scale, sink_logit,
              c_w_qkv, c_w_out, c_q_g, c_k_g,
              ffn_w_up, ffn_conv_w, ffn_conv_b, ffn_w_down):
    T = x.shape[1]
    cos, sin = rope_tables(T)
    xc = ctx
    for l in range(DEPTH):
        need_ctx = l < DEPTH - 1
        sh1, sc1, g1, sh2, sc2, g2 = [m[:, None, :] for m in ada_params(c, ada_w[l], ada_b[l])]
        csh1, csc1, cg1, csh2, csc2, cg2 = ada_params(c_ctx, ada_w[l], ada_b[l])
        h = pre_mod(x, mix_pre_g[l], sh1, sc1)
        hc = pre_mod(xc, mix_pre_g[l], csh1, csc1)
        i = l // 2
        if l % 2 == 0:
            y, yc = mixer_ab(h, hc, ab_w_in[i], ab_w_out[i], pool_w[i], pool_scale[i], sink_logit[i],
                             cos, sin, need_ctx)
        else:
            y, yc = mixer_c(h, hc, c_w_qkv[i], c_w_out[i], c_q_g[i], c_k_g[i], cos, sin, need_ctx)
        x = post_add(x, y, mix_post_g[l], g1)
        f = conv_ffn(pre_mod(x, ffn_pre_g[l], sh2, sc2), ffn_w_up[l], ffn_conv_w[l], ffn_conv_b[l], ffn_w_down[l])
        x = post_add(x, f, ffn_post_g[l], g2)
        if need_ctx:
            xc = post_add(xc, yc, mix_post_g[l], cg1)
            fc = conv_ffn(pre_mod(xc, ffn_pre_g[l], csh2, csc2), ffn_w_up[l], ffn_conv_w[l], ffn_conv_b[l], ffn_w_down[l])
            xc = post_add(xc, fc, ffn_post_g[l], cg2)
    return x


_drawn_inputs = setup_inputs


def setup_inputs(seed=0):
    import zlib

    import numpy as np

    out = dict(_drawn_inputs(seed))
    spreads = {}
    factors = {'mix_pre_g': 7.853,
     'mix_post_g': 6.608,
     'ffn_pre_g': 5.258,
     'ffn_post_g': 7.096,
     'sink_logit': 8.0,
     'c_q_g': 8.0,
     'c_k_g': 8.0,
     'ffn_conv_b': 5.403}
    for name, (base, spread) in spreads.items():
        noise = np.random.default_rng([zlib.crc32(name.encode()), seed]).standard_normal(out[name].shape)
        drawn = base * np.exp(spread * noise) if base else spread * noise
        out[name] = __import__('jax').numpy.asarray(drawn.astype(out[name].dtype))
    for name, factor in factors.items():
        out[name] = (out[name] * factor).astype(out[name].dtype)
    return out
```

```python
from contextlib import ExitStack

import concourse.bass as bass
from concourse import mybir

F32 = mybir.dt.float32
F32R = mybir.dt.float32r
BF16 = mybir.dt.bfloat16
ALU = mybir.AluOpType
ACT = mybir.ActivationFunctionType
AX_X = mybir.AxisListType.X

P = 128
BANK = 512
D = 1024
KC = D // P
SEQ, CTX = 512, 256
LAT_T, CTX_T = SEQ // P, CTX // P
ALL_T = LAT_T + CTX_T
TOK = SEQ + CTX
HD = 64
GROUP = 4
POOL_CH = D // 2
POOL_WINDOWS = (2, 4, 8, 16)
PAD = max(POOL_WINDOWS) // 2
UBUF = SEQ + CTX + 4 * PAD
B_HEADS, B_KV = 8, 2
C_HEADS, C_KV = 16, 4
DFF = (8 * D // 3) // 128 * 128
FT = DFF // P
EPS = 1e-6
SCALE = HD ** -0.5
STREAMS = ((0, SEQ), (SEQ, CTX))
PADDED = ((PAD, SEQ), (SEQ + 3 * PAD, CTX))

RAW = 3
UNITS = {"proj0": 12, "out0": 8, "up0": 2 * FT, "down0": 2 * FT,
         "proj1": 12, "out1": 8, "up1": 2 * FT, "down1": 2 * FT}
RINGS = {"proj": 4, "out": 4, "up": 3, "down": 3}
FIRST_UNIT = {}
_n = 0
for _k, _v in UNITS.items():
    FIRST_UNIT[_k] = _n
    _n += _v

VEC_ROWS = 52
CONV_ROWS = 3 * 2 * FT
BIAS_ROWS = 2 * 2 * FT

PROJ = {
    0: (("pool", 0, 512, ALL_T, 0), ("kv", 1024, 256, ALL_T, 0), ("q", 512, 512, ALL_T, 0)),
    1: (("kv", 1024, 512, ALL_T, 0), ("q", 0, 512, LAT_T, 0), ("q", 512, 512, LAT_T, 8)),
}


def attention_groups(l):
    ctx = [LAT_T, LAT_T + 1]
    if l == 1:
        return [(j, n, list(range(ALL_T)), {}) for j in range(C_KV) for n in range(LAT_T)]
    out = []
    for j in range(B_KV):
        for n in range(LAT_T):
            near = [m for m in (n - 1, n, n + 1) if 0 <= m < LAT_T]
            out.append((j, n, ctx + near, {m: int(m > n) for m in near if m != n}))
        out += [(j, n, ctx, {}) for n in ctx]
    return out


INTERLEAVE = ("S0", "S1", "C", "E0", "C", "E1", "D0", "S2", "C", "D1", "E2", "C", "S3", "D2", "C", "E3", "C", "D3")


def attention_steps(groups):
    steps, before, ended = [], None, None
    slots = INTERLEAVE.count("C")
    for g in range(len(groups) + 1):
        n = len(groups[g - 1][2]) if g else 0
        at = {c * slots // n: c for c in range(n)}
        slot = 0
        for token in INTERLEAVE:
            if token == "C":
                if slot in at:
                    steps.append(("T", g - 1, at[slot]))
                    if before is not None:
                        steps.append(("V", *before))
                    if ended is not None:
                        steps.append(("O", ended, 0))
                        ended = None
                    if before is not None and before[1] == len(groups[before[0]][2]) - 1:
                        ended = before[0]
                    before = (g - 1, at[slot])
                slot += 1
            elif g < len(groups):
                steps.append((token[0], g, int(token[1])))
    return steps + [("V", *before), ("O", before[0], 0)]


def key_pieces(keys):
    out = []
    for i, t in enumerate(keys):
        if out and out[-1][1] + out[-1][2] == t * P and (i * P) % BANK:
            out[-1][2] += P
        else:
            out.append([i * P, t * P, P])
    return out


def hybrid_backbone_kernel(nc, x_in, c, ctx_in, c_ctx, ada_w, ada_b, mix_pre_g, mix_post_g, ffn_pre_g,
                           ffn_post_g, ab_w_in, ab_w_out, pool_w, pool_scale, sink_logit, c_w_qkv, c_w_out,
                           c_q_g, c_k_g, ffn_w_up, ffn_conv_w, ffn_conv_b, ffn_w_down,
                           ident_in, rope_in, mask_in, edge_in, out):
    es = ExitStack()
    with es:
        cursor = [(nc.sbuf_base + 63) // 64 * 64]

        def sb(name, shape, dt=F32, at=None):
            size = 2 if dt == BF16 else 4
            for s in shape[1:]:
                size *= s
            size = (size + 63) // 64 * 64
            if at is None:
                at = cursor[0]
                cursor[0] += size
            t = nc.alloc_sbuf_tensor_at(name, shape, dt, offset=at)
            return t, at + size

        def keep(name, shape, dt=F32):
            return sb(name, shape, dt)[0]

        x = keep("x", [P, ALL_T, D])
        hT_hi = keep("hT_hi", [P, KC, TOK], F32R)
        hT_lo = keep("hT_lo", [P, KC, TOK], F32R)
        raw = keep("raw", [P, RAW, 1024])
        split_at = cursor[0]
        w_hi = keep("w_hi", [P, 4, 1024], F32R)
        w_lo = keep("w_lo", [P, 4, 1024], F32R)
        ident = keep("ident", [P, P])
        ident_b = keep("ident_b", [P, P], BF16)
        mask_b = keep("mask_b", [P, 2, P], BF16)
        rope = keep("rope", [P, 2, ALL_T, HD])
        edge = keep("edge", [P, 4, 2, PAD])
        cols = keep("cols", [P, VEC_ROWS])
        convw = [keep(f"convw{l}", [P, 3, 2 * FT]) for l in range(2)]
        convb = keep("convb", [P, 2, 2 * FT])
        cstat = keep("cstat", [P, KC, 32])
        mul_col = keep("mul_col", [P, 2, 2, KC])
        add_col = keep("add_col", [P, 2, 2, KC])
        gate_rows = keep("gate_rows", [P, BANK])
        nsink = keep("nsink", [P, B_HEADS])
        minus_half = keep("minus_half", [P, 32])
        ssum = keep("ssum", [P, 2, 8])
        rms = keep("rms", [P, 8])
        gate_at = cursor[0]
        gate = keep("gate", [P, 2, D])
        region = cursor[0]

        pw_hi, a = sb("pw_hi", [P, 4, P], F32R, gate_at)
        pw_lo, a = sb("pw_lo", [P, 4, P], F32R, a)
        pw, a = sb("pw", [P, 4, P], F32, a)
        vecs, a = sb("vecs", [P, 4, P], F32, region)
        silu, a = sb("silu", [P, 2, 16], F32, a)
        mask_f, a = sb("mask_f", [P, 2, P], F32, a)
        ada_ring, a = sb("ada_ring", [P, 8, 2048], F32, a)
        ada_rows, a = sb("ada_rows", [P, 3, BANK], F32, a)
        bias_rows, a = sb("bias_rows", [P, 3, BANK], F32, a)
        post_rows, a = sb("post_rows", [P, BANK], F32, a)
        tops = [a]
        xn, a = sb("xn", [P, ALL_T, D], F32, region)
        junk, a = sb("junk", [P, 2, D], F32, a)
        h32, a = sb("h32", [P, 2, TOK], F32, a)
        qT, a = sb("qT", [P, C_HEADS * SEQ], F32R, region)
        kT, a = sb("kT", [P, 2, C_KV, TOK], F32R, a)
        v_hi, a = sb("v_hi", [P, ALL_T, C_KV * HD], F32R, a)
        v_lo, a = sb("v_lo", [P, ALL_T, C_KV * HD], F32R, a)
        qkn, a = sb("qkn", [P, BANK], F32, a)
        qka, a = sb("qka", [P, BANK], F32, a)
        qkb, a = sb("qkb", [P, BANK], F32, a)
        qks, a = sb("qks", [P, 1024], F32R, a)
        sq, a = sb("sq", [P, BANK], F32, a)
        qk_ss, a = sb("qk_ss", [P, 8], F32, a)
        qk_ms, a = sb("qk_ms", [P, 8], F32, a)
        qk_r, a = sb("qk_r", [P, 8], F32, a)
        tops.append(a)
        qk_tab, b = sb("qk_tab", [P, 4, ALL_T, HD], F32, gate_at)
        qk_gain, b = sb("qk_gain", [P, 2, HD], F32, b)
        assert b <= region
        q0T, a = sb("q0T", [P, B_HEADS, TOK], F32R, region)
        k0T, a = sb("k0T", [P, 2, B_KV, TOK], F32R, a)
        v0_hi, a = sb("v0_hi", [P, ALL_T, B_KV * HD], F32R, a)
        v0_lo, a = sb("v0_lo", [P, ALL_T, B_KV * HD], F32R, a)
        d_hi, a = sb("d_hi", [P, UBUF], F32R, a)
        d_lo, a = sb("d_lo", [P, UBUF], F32R, a)
        sums, a = sb("sums", [P, 2, UBUF], F32, a)
        ubuf, a = sb("ubuf", [P, 4, UBUF], F32, a)
        assert a <= region + 4 * (C_HEADS * SEQ + 2 * C_KV * TOK + 2 * ALL_T * C_KV * HD)
        prob, a = sb("prob", [P, 2, GROUP, TOK], F32, split_at)
        pT_hi, a = sb("pT_hi", [P, 2, BANK], F32R, a)
        pT_lo, a = sb("pT_lo", [P, 2, BANK], F32R, a)
        assert a <= split_at + 2 * 4 * 4096
        o_tmp, a = sb("o_tmp", [P, 2, 2, P], F32, tops[1])
        small, a = sb("small", [P, 5, 64], F32, a)
        y0, a = sb("y0", [P, ALL_T, BANK], F32, region)
        sqj, a = sb("sqj", [P, 2, BANK], F32, a)
        t0, a = sb("t0", [P, BANK], F32, a)
        t1, a = sb("t1", [P, BANK], F32, a)
        act_g, a = sb("act_g", [P, FT, TOK], F32, region)
        conv_a, a = sb("conv_a", [P, TOK], F32, a)
        conv_b, a = sb("conv_b", [P, TOK], F32, a)
        gelu, a = sb("gelu", [P, TOK], F32, a)
        tops.append(a)
        hT_at = split_at - RAW * 4096 - 2 * KC * TOK * 4
        y0d, b = sb("y0d", [P, ALL_T, BANK], F32, hT_at)
        sqjd, b = sb("sqjd", [P, 2, BANK], F32, b)
        t0d, b = sb("t0d", [P, BANK], F32, b)
        t1d, b = sb("t1d", [P, BANK], F32, b)
        g_hi, b = sb("g_hi", [P, 3, TOK], F32R, b)
        g_lo, b = sb("g_lo", [P, 3, TOK], F32R, b)
        assert b <= hT_at + 2 * KC * TOK * 4
        assert max(tops) <= nc.sbuf_usable_end, (tops, nc.sbuf_usable_end)

        ps = es.enter_context(nc.psum_tensor("ps", [P, 8, BANK], F32))
        psf = ps[:, :, :].rearrange("p b n -> p (b n)")

        def bank(n, width=BANK):
            return psf[:, n * BANK:n * BANK + width]

        def sem(name):
            return es.enter_context(nc.semaphore(name))

        x_landed = sem("x_landed")
        rows_landed = sem("rows_landed")
        late_landed = sem("late_landed")
        store_done = sem("store_done")
        landed = [sem(f"w_landed{i}") for i in range(RAW)]
        hi_split = sem("w_hi_split")
        lo_split = sem("w_lo_split")
        used = {k: sem(f"{k}_w_used") for k in UNITS}
        closed = {k: sem(f"{k}_closed") for k in ("pe", "act", "dve", "pool")}
        sems = {}

        def s(name):
            if name not in sems:
                sems[name] = sem(name)
            return sems[name]

        def close(eng, name):
            eng.drain().then_inc(closed[name], 1)

        def after_phase(eng, n):
            for k in ("pe", "act", "dve", "pool"):
                eng.wait_ge(closed[k], n)

        def unit_slot(phase, u):
            return u % RINGS[phase[:-1]]

        def load_unit(sp, phase, m, src, width, turn=0, per_turn=0):
            n = FIRST_UNIT[phase] + m
            if n >= RAW:
                sp.wait_ge(lo_split, turn * per_turn + (n - RAW + 1))
            sp.dma_start(raw_view(n % RAW, src, width), src).then_inc(landed[n % RAW], 16)

        def raw_view(slot, src, width):
            v = raw[:, slot, 0:width]
            return v if len(src.shape) == 2 else v.rearrange("p (k n) -> p k n", k=src.shape[1])

        def split_hi(act, phase, m, width, turn=0, per_turn=0, free=True):
            n = FIRST_UNIT[phase] + m
            act.wait_ge(landed[n % RAW], turn * (16 * per_turn // RAW) + 16 * (n // RAW + 1))
            if free:
                ring = RINGS[phase[:-1]]
                act.wait_ge(used[phase], turn * per_turn + (m - ring + 1))
            nc.scalar.activation(w_hi[:, unit_slot(phase, m), 0:width], raw[:, n % RAW, 0:width],
                                 ACT.Copy).then_inc(hi_split, 1)

        def split_lo(pool, phase, m, width, turn=0, per_turn=0):
            n = FIRST_UNIT[phase] + m
            pool.wait_ge(hi_split, turn * per_turn + (n + 1))
            slot = unit_slot(phase, m)
            nc.gpsimd.tensor_tensor(w_lo[:, slot, 0:width], raw[:, n % RAW, 0:width],
                                    w_hi[:, slot, 0:width].bitcast(F32), ALU.subtract).then_inc(lo_split, 1)

        def wait_split(pe, phase, m, turn=0, per_turn=0):
            pe.wait_ge(lo_split, turn * per_turn + (FIRST_UNIT[phase] + m + 1))

        def mm3(outp, s_hi, s_lo, m_hi, m_lo, first, last):
            nc.tensor.matmul(outp, s_hi, m_hi, start=first, stop=False, skip_group_check=True)
            nc.tensor.matmul(outp, s_hi, m_lo, start=False, stop=False, skip_group_check=True)
            return nc.tensor.matmul(outp, s_lo, m_hi, start=False, stop=last, skip_group_check=True)

        def setup_sync(sp):
            def ld(dst, src):
                sp.dma_start(dst, src).then_inc(rows_landed, 16)

            def rows(a):
                return a.rearrange("a (k n) -> (a k) n", n=P)

            ld(ident[:, :], ident_in)
            ld(vecs[0:16, 0, :], rows(mix_pre_g))
            ld(vecs[16:32, 0, :], rows(ffn_pre_g))
            ld(vecs[32:40, 0, :], rows(c))
            ld(vecs[40:48, 0, :], c_ctx.rearrange("(k n) -> k n", n=P))
            ld(vecs[48:52, 0, :], rows(pool_scale))
            ld(vecs[0:CONV_ROWS, 1, :], ffn_conv_w[0].rearrange("t (f n) -> (t f) n", n=P))
            ld(vecs[0:CONV_ROWS, 2, :], ffn_conv_w[1].rearrange("t (f n) -> (t f) n", n=P))
            ld(vecs[0:BIAS_ROWS // 2, 3, :], ffn_conv_b[0:1].rearrange("a (f n) -> (a f) n", n=P))
            ld(vecs[BIAS_ROWS // 2:BIAS_ROWS, 3, :], ffn_conv_b[1:2].rearrange("a (f n) -> (a f) n", n=P))

        def late_sync(sp):
            def ld(dst, src):
                sp.dma_start(dst, src).then_inc(late_landed, 16)

            ld(mask_f[:, :, :], mask_in.rearrange("a p n -> p a n"))
            ld(rope[:, :, :, :], rope_in.rearrange("a (t p) n -> p a t n", p=P))
            ld(edge[:, :, :, :], edge_in.partition_broadcast(P))
            ld(nsink[:, :], sink_logit.rearrange("a j g -> a (j g)").partition_broadcast(P).rearrange("p a n -> p (a n)"))
            ld(pw[:, :, :], pool_w[0].rearrange("g p n -> p g n"))
            sp.dma_start(x[:, 0:LAT_T, :], x_in[0].rearrange("(t p) n -> p t n", p=P)).then_inc(x_landed, 16)
            sp.dma_start(x[:, LAT_T:ALL_T, :], ctx_in[0].rearrange("(t p) n -> p t n", p=P)).then_inc(x_landed, 16)

        def setup_tensor(pe):
            pe.wait_ge(rows_landed, 16 * 10)
            for n, (t, r) in enumerate(((0, VEC_ROWS), (1, CONV_ROWS), (2, CONV_ROWS), (3, BIAS_ROWS))):
                nc.tensor.transpose(bank(n, r), vecs[0:r, t, :], ident[0:r, 0:r]).then_inc(s("rows_turned"), 1)
            close(pe, "pe")

        def setup_vector(dve):
            nc.vector.memset(cstat[:, :, :], 0.0).then_inc(s("setup_dve"), 1)
            nc.vector.memset(minus_half[:, :], -0.5).then_inc(s("setup_dve"), 1)
            dve.wait_ge(s("rows_turned"), 1)
            nc.vector.tensor_copy(cols[:, :], bank(0, VEC_ROWS)).then_inc(s("setup_dve"), 1)
            dve.wait_ge(s("exp_c"), 1)
            nc.vector.tensor_scalar(silu[:, 1, :], silu[:, 0, :], 1.0, None, ALU.add).then_inc(s("setup_dve"), 1)
            dve.wait_ge(s("setup_dve"), 4)
            nc.vector.reciprocal(silu[:, 0, :], silu[:, 1, :]).then_inc(s("setup_dve"), 1)
            dve.wait_ge(s("setup_dve"), 5)
            nc.vector.tensor_tensor(cstat[:, :, 0:2].rearrange("p k v -> p v k"),
                                    cols[:, 32:48].rearrange("p (v k) -> p v k", v=2),
                                    silu[:, 0, :].rearrange("p (v k) -> p v k", v=2), ALU.mult).then_inc(s("setup_dve"), 1)
            for n in range(2):
                dve.wait_ge(s("rows_turned"), 2 + n)
                nc.vector.tensor_copy(convw[n][:, :, :].rearrange("p t f -> p (t f)"),
                                      bank(1 + n, CONV_ROWS)).then_inc(s("setup_dve"), 1)
            dve.wait_ge(s("rows_turned"), 4)
            nc.vector.tensor_copy(convb[:, :, :].rearrange("p l f -> p (l f)"), bank(3, BIAS_ROWS)).then_inc(s("setup_dve"), 1)
            close(dve, "dve")

        def setup_scalar(act):
            act.wait_ge(s("setup_dve"), 3)
            nc.scalar.activation(silu[:, 0, :], cols[:, 32:48], ACT.Exp, scale=-1.0).then_inc(s("exp_c"), 1)
            close(act, "act")

        ADA_BASE = {0: 0, 1: 24}

        def ada_sync(sp, l):
            if l:
                after_phase(sp, 9)
                for i, g in enumerate((c_q_g, c_k_g)):
                    sp.dma_start(qk_gain[:, i, :], g[0].partition_broadcast(P)).then_inc(s("gain_landed"), 16)
            for j in range(4):
                sp.dma_start(bias_rows[32 * j:32 * j + 32, :, :],
                             ada_b[l].rearrange("(r j n) -> j r n", r=3, j=4)[j].partition_broadcast(32)
                             ).then_inc(s(f"bias_landed{l}"), 16)
                g = (mix_post_g, ffn_post_g)[j // 2]
                sp.dma_start(post_rows[32 * j:32 * j + 32, :],
                             g[l, (j % 2) * BANK:(j % 2 + 1) * BANK].partition_broadcast(32)
                             ).then_inc(s(f"bias_landed{l}"), 16)
            with sp.Fori(0, 3) as r:
                for k in range(KC):
                    sp.wait_ge(s(f"ada{l}_used"), r * KC + (k + 1))
                    sp.dma_start(ada_ring[:, k, :], ada_w[l, k * P:(k + 1) * P, bass.ds(r * 2048, 2048)]
                                 ).then_inc(s(f"ada_landed{k}"), 16)

        def ada_tensor(pe, l):
            pe.wait_ge(s("setup_dve"), 6)
            pe.sem_inc(s(f"ada{l}_used"), KC)
            with pe.Fori(0, 3) as r:
                pe.wait_ge(s(f"ada{l}_rows"), r + 1)
                for k in range(KC):
                    pe.wait_ge(s(f"ada_landed{k}"), r * 16 + (16 + 48 * l))
                    for j in range(4):
                        mm = nc.tensor.matmul(ps[32 * j:32 * j + 32, 4, :], cstat[:, k, :],
                                              ada_ring[:, k, j * BANK:(j + 1) * BANK],
                                              start=k == 0, stop=k == KC - 1, skip_group_check=True)
                    mm.then_inc(s(f"ada{l}_used"), 1)
            pe.wait_ge(s(f"ada{l}_rows"), 4)
            for r in range(3):
                for sub in range(4):
                    mm = nc.tensor.transpose(bank(r)[:, sub * P:(sub + 1) * P],
                                             ada_rows[:, r, sub * P:(sub + 1) * P], ident[:, :])
            mm.then_inc(s(f"ada{l}_cols"), 1)
            close(pe, "pe")

        def ada_vector(dve, l):
            dve.sem_inc(s(f"ada{l}_rows"), 1)
            dve.wait_ge(s(f"bias_landed{l}"), 8 * 16)
            with dve.Fori(0, 3) as r:
                dve.wait_ge(s(f"ada{l}_used"), r * KC + 2 * KC)
                nc.vector.tensor_tensor(ada_rows[:, bass.ds(r, 1), :].rearrange("p a n -> p (a n)"), bank(4),
                                        bias_rows[:, bass.ds(r, 1), :].rearrange("p a n -> p (a n)"),
                                        ALU.add).then_inc(s(f"ada{l}_rows"), 1)
            dve.wait_ge(s(f"ada{l}_rows"), 4)
            for i, r in enumerate((1, 2)):
                q = slice(64 * i, 64 * i + 64)
                nc.vector.tensor_tensor(gate_rows[q, :], ada_rows[q, r, :], post_rows[q, :],
                                        ALU.mult).then_inc(s(f"ada{l}_fin"), 1)
            dve.wait_ge(s(f"ada{l}_cols"), 1)

            def turned(r, j, v):
                return bank(r).rearrange("p (s j v) -> p j s v", s=4, j=4)[:, j:j + 2, :, v]

            for sub, (sh, sc, gcol) in enumerate((((0, 0), (0, 2), 8 * l), ((1, 2), (2, 0), 16 + 8 * l))):
                for v in range(2):
                    a = add_col[:, sub, v, :].rearrange("p (j s) -> p j s", j=2)
                    m = mul_col[:, sub, v, :].rearrange("p (j s) -> p j s", j=2)
                    g = cols[:, gcol:gcol + 8].rearrange("p (j s) -> p j s", j=2)
                    nc.vector.tensor_copy(a, turned(*sh, v)).then_inc(s(f"ada{l}_fin"), 1)
                    nc.vector.scalar_tensor_tensor(out=m, in0=turned(*sc, v), scalar=1.0, in1=g,
                                                   op0=ALU.add, op1=ALU.mult).then_inc(s(f"ada{l}_fin"), 1)
            if l == 0:
                dve.wait_ge(late_landed, 5 * 16)
                nc.vector.tensor_copy(ident_b[:, :], ident[:, :]).then_inc(s("late_dve"), 1)
                nc.vector.tensor_copy(mask_b[:, :, :], mask_f[:, :, :]).then_inc(s("late_dve"), 1)
                nc.vector.tensor_copy(pw_hi[:, :, :], pw[:, :, :]).then_inc(s("late_dve"), 1)
                dve.wait_ge(s("late_dve"), 3)
                nc.vector.tensor_tensor(pw_lo[:, :, :], pw[:, :, :], pw_hi[:, :, :].bitcast(F32),
                                        ALU.subtract).then_inc(s("late_dve"), 1)
                nc.vector.tensor_scalar(nsink[:, :], nsink[:, :], -1.0, None, ALU.mult).then_inc(s("late_dve"), 1)
            close(dve, "dve")

        def norm_scalar(act, tag, before, sub, nt, prefetch):
            after_phase(act, before)
            if tag == "mix0":
                act.wait_ge(x_landed, 2 * 16)
            for t in range(nt):
                if t >= 2:
                    act.wait_ge(s(f"{tag}_sq"), t - 1)
                nc.scalar.activation(junk[:, t % 2, :], x[:, t, :], ACT.Square,
                                     accum_out=ssum[:, 0, t:t + 1]).then_inc(s(f"{tag}_sq"), 1)
            prefetch(act)
            ns = 2 if nt == ALL_T else 1
            for k in range(KC):
                act.wait_ge(s(f"{tag}_turned"), k + 1)
                if k >= 2:
                    act.wait_ge(s(f"{tag}_split"), 2 * (k - 1))
                for v in range(ns):
                    c0, n = STREAMS[v]
                    nc.scalar.activation(h32[:, k % 2, c0:c0 + n], bank(2 * (k % 2), 1024)[:, c0:c0 + n],
                                         ACT.Identity, bias=add_col[:, sub, v, k:k + 1],
                                         scale=mul_col[:, sub, v, k:k + 1]).then_inc(s(f"{tag}_h32"), 1)
            close(act, "act")

        def norm_pool(pool, tag, before, nt, prefetch):
            after_phase(pool, before)
            prefetch(pool)
            pool.wait_ge(s(f"{tag}_sq"), nt)
            nc.gpsimd.tensor_scalar(ssum[:, 1, 0:nt], ssum[:, 0, 0:nt], 1.0 / D, EPS, ALU.mult,
                                    ALU.add).then_inc(s(f"{tag}_rms"), 1)
            pool.wait_ge(s(f"{tag}_rms"), 1)
            nc.gpsimd.tensor_tensor(rms[:, 0:nt], ssum[:, 1, 0:nt], minus_half[:, 0:nt],
                                    ALU.pow).then_inc(s(f"{tag}_rms"), 1)
            close(pool, "pool")

        def norm_vector(dve, tag, before, nt):
            after_phase(dve, before)
            dve.wait_ge(s(f"{tag}_rms"), 2)
            for t in range(nt):
                nc.vector.tensor_scalar(xn[:, t, :], x[:, t, :], rms[:, t:t + 1], None,
                                        ALU.mult).then_inc(s(f"{tag}_xn"), 1)
            ns = 2 if nt == ALL_T else 1
            T = nt * P
            for k in range(KC):
                dve.wait_ge(s(f"{tag}_h32"), ns * (k + 1))
                nc.vector.tensor_copy(hT_hi[:, k, 0:T], h32[:, k % 2, 0:T]).then_inc(s(f"{tag}_split"), 1)
                dve.wait_ge(s(f"{tag}_split"), 2 * k + 1)
                nc.vector.tensor_tensor(hT_lo[:, k, 0:T], h32[:, k % 2, 0:T], hT_hi[:, k, 0:T].bitcast(F32),
                                        ALU.subtract).then_inc(s(f"{tag}_split"), 1)
            close(dve, "dve")

        def norm_tensor(pe, tag, before, nt):
            after_phase(pe, before)
            ns = 2 if nt == ALL_T else 1
            for k in range(KC):
                if k >= 2:
                    pe.wait_ge(s(f"{tag}_h32"), ns * (k - 1))
                for t in range(nt):
                    if k == 0:
                        pe.wait_ge(s(f"{tag}_xn"), t + 1)
                    mm = nc.tensor.transpose(bank(2 * (k % 2), 1024)[:, t * P:(t + 1) * P],
                                             xn[:, t, k * P:(k + 1) * P], ident[:, :])
                mm.then_inc(s(f"{tag}_turned"), 1)
            close(pe, "pe")

        def token_tiles(l):
            out = []
            for gi, (kind, _, w, nt, h0) in enumerate(PROJ[l]):
                if kind != "pool":
                    heads = w // HD if kind == "q" else w // HD // 2
                    out += [(gi, kind, t, heads, h0) for t in range(nt)]
            return out

        def rope_plan(l):
            base, n, tb, m = [], 0, [], 0
            for _, kind, _, heads, _ in token_tiles(l):
                base.append(n)
                tb.append(m)
                n += 6 + (2 if l else 0) + (kind == "kv")
                m += 2 if (l or kind == "q") else 1
            return base + [n], tb + [m]

        def proj_sync(sp, l):
            w = (ab_w_in, c_w_qkv)[l][0]
            m = 0
            for _, c0, width, _, _ in PROJ[l]:
                for u in range(4):
                    src = w[2 * u * P:(2 * u + 2) * P, c0:c0 + width].rearrange("(k p) n -> p k n", p=P)
                    load_unit(sp, f"proj{l}", m, src, 2 * width)
                    m += 1

        def unit_width(l, m):
            return 2 * PROJ[l][m // 4][2]

        def acc_free_steps(l, kind):
            return (2 if l else 2) + (kind == "kv")

        def proj_tensor(pe, l, before, tag):
            phase = f"proj{l}"
            base, tb = rope_plan(l)
            tiles = token_tiles(l)
            q_t = (q0T[:, :, :], qT[:, :].rearrange("p (h n) -> p h n", h=C_HEADS))[l]

            def turn(n):
                _, kind, _, heads, _ = tiles[n]
                blocks = heads if kind == "q" else 2 * heads
                pe.wait_ge(s(f"qk_steps{l}"), base[n + 1])
                if kind == "kv":
                    pe.wait_ge(s(f"k_dup{l}"), n + 1)
                for b in range(tb[n + 1] - tb[n]):
                    nb = tb[n] + b
                    if nb >= 2:
                        pe.wait_ge(s(f"turned_read{l}"), nb - 1)
                    for i in range(4):
                        mm = nc.tensor.transpose(bank(2 + nb % 2)[:, i * P:(i + 1) * P],
                                                 qks[:, (4 * b + i) * P:(4 * b + i + 1) * P].bitcast(F32), ident[:, :])
                    mm.then_inc(s(f"qk_turned{l}"), 1)

            after_phase(pe, before - 1)
            for k in range(KC):
                pe.wait_ge(s(f"{tag}_split"), 2 * (k + 1))
            pe.wait_ge(closed["act"], before)
            m = n = 0
            for gi, (kind, _, width, nt, _) in enumerate(PROJ[l]):
                def wv(part, k, c0, w):
                    slot = unit_slot(phase, m + k // 2)
                    return part[:, slot, (k % 2) * width + c0:(k % 2) * width + c0 + w]

                if kind == "pool":
                    for f in range(4):
                        if f >= 2:
                            pe.wait_ge(s("u_read"), 2 * (f - 1))
                        for k in range(KC):
                            if f == 0 and k % 2 == 0:
                                wait_split(pe, phase, m + k // 2)
                            for c0, w in STREAMS:
                                mm = mm3(bank(4 + 2 * (f % 2), 1024)[:, c0:c0 + w], wv(w_hi, k, f * P, P), wv(w_lo, k, f * P, P),
                                         hT_hi[:, k, c0:c0 + w], hT_lo[:, k, c0:c0 + w], k == 0, k == KC - 1)
                            if f == 3 and k in (1, 3, 5):
                                mm.then_inc(used[phase], 1)
                        mm.then_inc(s("u_done"), 1)
                    pe.drain().then_inc(used[phase], 1)
                else:
                    for t in range(nt):
                        if n >= 2:
                            pe.wait_ge(s(f"qk_steps{l}"), base[n - 2] + acc_free_steps(l, tiles[n - 2][1]))
                        for k in range(KC):
                            if t == 0 and k % 2 == 0:
                                wait_split(pe, phase, m + k // 2)
                            tt = slice(t * P, (t + 1) * P)
                            mm = mm3(bank(n % 2, width), hT_hi[:, k, tt], hT_lo[:, k, tt],
                                     wv(w_hi, k, 0, width), wv(w_lo, k, 0, width), k == 0, k == KC - 1)
                            if t == nt - 1 and k in (1, 3, 5):
                                mm.then_inc(used[phase], 1)
                        mm.then_inc(s(f"acc_done{l}"), 1)
                        if n >= 1:
                            turn(n - 1)
                        n += 1
                    pe.drain().then_inc(used[phase], 1)
                m += 4
            turn(n - 1)
            if l == 0:
                for f in range(4):
                    pe.wait_ge(s("pool_d"), 2 * f + 2)
                    if f >= 2:
                        pe.wait_ge(s("pool_out"), 4 * (f - 1))
                    for v, (c0, w) in enumerate(STREAMS):
                        p0 = PADDED[v][0]
                        mm = mm3(bank(4 + 2 * (f % 2), 1024)[:, c0:c0 + w], pw_hi[:, f, :], pw_lo[:, f, :],
                                 d_hi[:, p0:p0 + w], d_lo[:, p0:p0 + w], True, True)
                    mm.then_inc(s("pool_mm"), 1)
            close(pe, "pe")

        def proj_prefetch(l):
            def act_part(act):
                for m in range(4):
                    split_hi(act, f"proj{l}", m, unit_width(l, m), free=False)

            def pool_part(pool):
                for m in range(4):
                    split_lo(pool, f"proj{l}", m, unit_width(l, m))
            return act_part, pool_part

        def proj_scalar(act, l, before):
            phase = f"proj{l}"
            base, tb = rope_plan(l)
            tiles = token_tiles(l)
            q_t = (q0T[:, :, :], qT[:, :].rearrange("p (h n) -> p h n", h=C_HEADS))[l]
            k_t = (k0T, kT)[l]
            vh = (v0_hi, v_hi)[l]
            kvh = (B_KV, C_KV)[l]

            def read_turned(n):
                _, kind, t, heads, h0 = tiles[n]
                for b in range(tb[n + 1] - tb[n]):
                    nb = tb[n] + b
                    act.wait_ge(s(f"qk_turned{l}"), nb + 1)
                    src = bank(2 + nb % 2).rearrange("p (i n) -> p i n", i=4)
                    tt = slice(t * P, (t + 1) * P)
                    if kind == "q":
                        dst = q_t[:, h0 + 4 * b:h0 + 4 * b + 4, tt]
                    else:
                        src = bank(2 + nb % 2).rearrange("p (j a n) -> p j a n", j=2, a=2)
                        dst = k_t[:, :, 2 * b:2 * b + 2, tt].rearrange("p a j n -> p j a n")
                    nc.scalar.activation(dst, src, ACT.Copy).then_inc(s(f"turned_read{l}"), 1)

            after_phase(act, before)
            m, n = 4, 0
            for gi, (kind, _, width, nt, _) in enumerate(PROJ[l]):
                if kind == "pool":
                    for f in range(4):
                        act.wait_ge(s("u_done"), f + 1)
                        act.wait_ge(s("u_zeroed"), 1)
                        for v, (c0, w) in enumerate(STREAMS):
                            p0 = PADDED[v][0]
                            nc.scalar.activation(ubuf[:, f, p0:p0 + w], bank(4 + 2 * (f % 2), 1024)[:, c0:c0 + w],
                                                 ACT.Copy).then_inc(s("u_read"), 1)
                else:
                    for t in range(nt):
                        act.wait_ge(s(f"acc_done{l}"), n + 1)
                        heads = tiles[n][3]
                        if l:
                            if n:
                                act.wait_ge(s(f"qk_steps{l}"), base[n - 1] + 1 + (tiles[n - 1][1] == "kv"))
                            nc.scalar.activation(sq[:, 0:heads * HD], bank(n % 2, heads * HD),
                                                 ACT.Square).then_inc(s("qk_sq"), 1)
                        if kind == "kv":
                            nc.scalar.activation(vh[:, t, 0:kvh * HD], bank(n % 2)[:, heads * HD:2 * heads * HD],
                                                 ACT.Copy).then_inc(s(f"v_hi{l}"), 1)
                        if n:
                            read_turned(n - 1)
                        if kind == "kv":
                            act.wait_ge(s(f"qk_steps{l}"), base[n + 1])
                            kk = qks[:, 0:heads * 4 * HD].rearrange("p (i d n) -> p i d n", d=2, n=HD)
                            nc.scalar.activation(kk[:, :, 1, :], kk[:, :, 0, :].bitcast(F32),
                                                 ACT.Copy).then_inc(s(f"k_dup{l}"), 1)
                        n += 1
                if gi < 2:
                    for i in range(4):
                        split_hi(act, phase, m, unit_width(l, m))
                        m += 1
            read_turned(n - 1)
            if l == 0:
                for f in range(4):
                    act.wait_ge(s("pool_mm"), f + 1)
                    for v, (c0, w) in enumerate(STREAMS):
                        nc.scalar.activation(hT_hi[:, f, c0:c0 + w], bank(4 + 2 * (f % 2), 1024)[:, c0:c0 + w],
                                             ACT.Copy, scale=cols[:, 48 + f:49 + f]).then_inc(s("pool_hi"), 1)
            close(act, "act")

        DIFFERENCE_AFTER = (0, 2, 7, 9)

        def window_sums(pool, windows):
            for f in windows:
                pool.wait_ge(s("u_read"), 2 * f + 2)
                src, reach = ubuf[:, f, :], 1
                for step in range(f + 1):
                    h = max(1, 2 ** step // 2)
                    dst = sums[:, step % 2, :]
                    lo, hi = reach, UBUF - reach
                    if step == 0:
                        a, b = src[:, lo - 1:hi - 1], src[:, lo:hi]
                    else:
                        a, b = src[:, lo - h:hi - h], src[:, lo + h:hi + h]
                    if step:
                        pool.wait_ge(s("win_sum"), f * (f + 1) // 2 + step)
                    elif f:
                        pool.wait_ge(s("pool_d32"), 3 * f)
                    nc.gpsimd.tensor_tensor(dst[:, lo:hi], a, b, ALU.add).then_inc(s("win_sum"), 1)
                    src = dst
                    reach += max(1, 2 ** step)

        def proj_pool(pool, l, before):
            phase = f"proj{l}"
            after_phase(pool, before)
            m, n = 4, 0
            tiles = token_tiles(l)
            base, _ = rope_plan(l)
            for gi, (kind, _, width, nt, _) in enumerate(PROJ[l]):
                if kind == "pool":
                    nc.gpsimd.memset(ubuf[:, :, :], 0.0).then_inc(s("u_zeroed"), 1)
                    for i in range(4):
                        split_lo(pool, phase, m, unit_width(l, m))
                        m += 1
                    window_sums(pool, (0, 1))
                elif l:
                    for t in range(nt):
                        pool.wait_ge(s(f"qk_steps{l}"), base[n] + 1 + (kind == "kv"))
                        heads = tiles[n][3]
                        nc.gpsimd.tensor_scalar(qk_ms[:, 0:heads], qk_ss[:, 0:heads], 1.0 / HD, EPS, ALU.mult,
                                                ALU.add).then_inc(s("qk_rms"), 1)
                        pool.wait_ge(s("qk_rms"), 2 * n + 1)
                        nc.gpsimd.tensor_tensor(qk_r[:, 0:heads], qk_ms[:, 0:heads], minus_half[:, 0:heads],
                                                ALU.pow).then_inc(s("qk_rms"), 1)
                        n += 1
                if kind != "pool" and gi < 2:
                    for i in range(4):
                        split_lo(pool, phase, m, unit_width(l, m))
                        m += 1
            if l == 0:
                window_sums(pool, (2, 3))
            close(pool, "pool")

        def proj_vector(dve, l, before):
            base, _ = rope_plan(l)
            tiles = token_tiles(l)
            vh, vl = ((v0_hi, v0_lo), (v_hi, v_lo))[l]
            steps = s(f"qk_steps{l}")
            after_phase(dve, before)
            if l:
                dve.wait_ge(s("gain_landed"), 2 * 16)
                nc.vector.tensor_scalar(qk_gain[:, 0, :], qk_gain[:, 0, :], SCALE, None, ALU.mult).then_inc(s("qk_tab"), 1)
                dve.wait_ge(s("qk_tab"), 1)
                for i in range(4):
                    nc.vector.tensor_tensor(qk_tab[:, i, :, :], rope[:, i % 2, :, :],
                                            qk_gain[:, i // 2, :].unsqueeze(1).broadcast_to([P, ALL_T, HD]),
                                            ALU.mult).then_inc(s("qk_tab"), 1)
                dve.wait_ge(s("qk_tab"), 5)
            for n, (gi, kind, t, heads, h0) in enumerate(tiles):
                W = heads * HD
                src = bank(n % 2, W).rearrange("p (h d) -> p h d", d=HD)
                at = base[n]
                if n:
                    dve.wait_ge(steps, at)
                if kind == "kv":
                    dve.wait_ge(s(f"v_hi{l}"), n + 1)
                    nc.vector.tensor_tensor(vl[:, t, 0:W], bank(n % 2)[:, W:2 * W],
                                            vh[:, t, 0:W].bitcast(F32), ALU.subtract).then_inc(steps, 1)
                    at += 1
                else:
                    dve.wait_ge(s(f"acc_done{l}"), n + 1)
                if l:
                    dve.wait_ge(s("qk_sq"), n + 1)
                    nc.vector.reduce_sum(qk_ss[:, 0:heads], sq[:, 0:W].rearrange("p (h d) -> p h d", d=HD),
                                         AX_X).then_inc(steps, 1)
                    dve.wait_ge(s("qk_rms"), 2 * n + 2)
                    nrm = qkn[:, 0:W].rearrange("p (h d) -> p h d", d=HD)
                    nc.vector.tensor_tensor(nrm, src, qk_r[:, 0:heads].unsqueeze(2).broadcast_to([P, heads, HD]),
                                            ALU.mult).then_inc(steps, 1)
                    at += 2
                    dve.wait_ge(steps, at)
                    src = nrm
                    tab = [qk_tab[:, 2 * (kind == "kv") + i, t, :] for i in range(2)]
                else:
                    tab = [rope[:, i, t, :] for i in range(2)]
                a = qka[:, 0:W].rearrange("p (h d) -> p h d", d=HD)
                b = qkb[:, 0:W].rearrange("p (h d) -> p h d", d=HD)
                for dst, tb_ in zip((a, b), tab):
                    nc.vector.tensor_tensor(dst, src, tb_.unsqueeze(1).broadcast_to([P, heads, HD]),
                                            ALU.mult).then_inc(steps, 1)
                at += 2
                dve.wait_ge(steps, at)
                half = HD // 2
                nc.vector.tensor_tensor(a[:, :, 0:half], a[:, :, 0:half], b[:, :, half:HD],
                                        ALU.subtract).then_inc(steps, 1)
                nc.vector.tensor_tensor(a[:, :, half:HD], a[:, :, half:HD], b[:, :, 0:half],
                                        ALU.add).then_inc(steps, 1)
                at += 2
                dve.wait_ge(steps, at)
                if n:
                    dve.wait_ge(s(f"qk_turned{l}"), rope_plan(l)[1][n])
                if kind == "q":
                    v = qks[:, 0:2 * W].rearrange("p (h a d) -> p h a d", a=2, d=HD)
                    hi, lo = v[:, :, 0, :], v[:, :, 1, :]
                else:
                    v = qks[:, 0:4 * W].rearrange("p (h a c d) -> p h a c d", a=2, c=2, d=HD)
                    hi, lo = v[:, :, 0, 0, :], v[:, :, 1, 0, :]
                nc.vector.tensor_copy(hi, a).then_inc(steps, 1)
                dve.wait_ge(steps, at + 1)
                nc.vector.tensor_tensor(lo, a, hi.bitcast(F32), ALU.subtract).then_inc(steps, 1)
                assert at + 2 == base[n + 1]
                if l == 0 and n in DIFFERENCE_AFTER:
                    pool_difference(dve, DIFFERENCE_AFTER.index(n))
            if l == 0:
                for f in range(4):
                    if f:
                        dve.wait_ge(s("pool_mm"), f)
                    dve.wait_ge(s("pool_d32"), 3 * f + 3)
                    nc.vector.tensor_copy(d_hi[:, 0:UBUF], ubuf[:, f, :]).then_inc(s("pool_d"), 1)
                    dve.wait_ge(s("pool_d"), 2 * f + 1)
                    nc.vector.tensor_tensor(d_lo[:, 0:UBUF], ubuf[:, f, :], d_hi[:, 0:UBUF].bitcast(F32),
                                            ALU.subtract).then_inc(s("pool_d"), 1)
                    if f:
                        pool_lo(dve, f - 1)
                pool_lo(dve, 3)
            close(dve, "dve")

        def pool_difference(dve, f):
            acc = sums[:, f % 2, :]
            dve.wait_ge(s("win_sum"), (f + 1) * (f + 2) // 2)
            for v, (p0, w) in enumerate(PADDED):
                e = acc[:, p0:p0 + w]
                ends = e.rearrange("p (a n) -> p a n", n=PAD)[:, 0:w // PAD:w // PAD - 1, :]
                nc.vector.tensor_tensor(ends, ends, edge[:, f, :, :], ALU.mult).then_inc(s("pool_d32"), 1)
            dve.wait_ge(s("pool_d32"), 3 * f + 2)
            lo = PADDED[0][0]
            nc.vector.scalar_tensor_tensor(out=ubuf[:, f, lo:UBUF - PAD], in0=acc[:, lo:UBUF - PAD],
                                           scalar=1.0 / POOL_WINDOWS[f], in1=ubuf[:, f, lo:UBUF - PAD],
                                           op0=ALU.mult, op1=ALU.subtract).then_inc(s("pool_d32"), 1)

        def pool_lo(dve, f):
            dve.wait_ge(s("pool_hi"), 2 * f + 2)
            for c0, w in STREAMS:
                nc.vector.scalar_tensor_tensor(out=hT_lo[:, f, c0:c0 + w], in0=bank(4 + 2 * (f % 2), 1024)[:, c0:c0 + w],
                                               scalar=cols[:, 48 + f:49 + f], in1=hT_hi[:, f, c0:c0 + w].bitcast(F32),
                                               op0=ALU.mult, op1=ALU.subtract).then_inc(s("pool_out"), 2)

        def attn_setup(l):
            groups = attention_groups(l)
            first = [0]
            for g in groups:
                first.append(first[-1] + len(g[2]))
            return groups, attention_steps(groups), first

        mx, negm, den, rden, esink = (small[:, i, :] for i in range(5))

        def attn_tensor(pe, l, before):
            groups, steps, first = attn_setup(l)
            q_t = (q0T[:, :, :], qT[:, :].rearrange("p (h n) -> p h n", h=C_HEADS))[l]
            k_t = (k0T, kT)[l]
            vh, vl = ((v0_hi, v0_lo), (v_hi, v_lo))[l]
            per = 2 if l == 0 else 1
            after_phase(pe, before)
            for kind, g, i in steps:
                j, n, keys, masks = groups[g]
                if kind == "S":
                    h = 4 * g + i
                    if h >= 2:
                        pe.wait_ge(s(f"exp_done{l}"), per * (h - 2) + 1)
                    sc = bank(2 * (h % 2), 1024)
                    lhs = q_t[:, GROUP * j + i, n * P:(n + 1) * P]
                    pieces = key_pieces(keys)
                    for part in range(2):
                        for p0, k0, w in pieces:
                            mm = nc.tensor.matmul(sc[:, p0:p0 + w], lhs, k_t[:, part, j, k0:k0 + w],
                                                  start=part == 0 and p0 % BANK == 0, stop=part == 1,
                                                  skip_group_check=True)
                    for c, t in enumerate(keys):
                        if t in masks:
                            mm = nc.tensor.matmul(sc[:, c * P:(c + 1) * P], ident_b[:, :], mask_b[:, masks[t], :],
                                                  start=False, stop=True, skip_group_check=True)
                    mm.then_inc(s(f"scores{l}"), 1)
                elif kind == "T":
                    cg = first[g] + i
                    pe.wait_ge(s(f"prob_norm{l}"), 4 * g + 4)
                    if cg >= 2:
                        pe.wait_ge(s(f"pT_lo{l}"), cg - 1)
                    for h in range(GROUP):
                        mm = nc.tensor.transpose(bank(4 + cg % 2)[:, h * P:(h + 1) * P],
                                                 prob[:, g % 2, h, i * P:(i + 1) * P], ident[:, :])
                    mm.then_inc(s(f"prob_turned{l}"), 1)
                elif kind == "V":
                    cg = first[g] + i
                    pe.wait_ge(s(f"pT_lo{l}"), cg + 1)
                    if i == 0 and g >= 2:
                        pe.wait_ge(s(f"o_read{l}"), 2 * (g - 1))
                    vt = (slice(None), keys[i], slice(j * HD, (j + 1) * HD))
                    mm = mm3(ps[0:HD, 6 + g % 2, :], vh[vt], vl[vt], pT_hi[:, cg % 2, :], pT_lo[:, cg % 2, :],
                             i == 0, i == len(keys) - 1)
                    mm.then_inc(s(f"pv{l}"), 1)
            close(pe, "pe")

        def attn_scalar(act, l, before):
            groups, steps, first = attn_setup(l)
            after_phase(act, before)
            per = 3 if l == 0 else 2
            for kind, g, i in steps:
                j, n, keys, masks = groups[g]
                h = 4 * g + i
                if kind == "E":
                    act.wait_ge(s(f"smax{l}"), h + 1)
                    W = len(keys) * P
                    nc.scalar.activation(prob[:, g % 2, i, 0:W], bank(2 * (h % 2), 1024)[:, 0:W], ACT.Exp,
                                         bias=negm[:, h:h + 1], scale=SCALE if l == 0 else 1.0,
                                         accum_out=den[:, h:h + 1]).then_inc(s(f"exp_done{l}"), 1)
                    if l == 0:
                        nc.scalar.activation(esink[:, h:h + 1], nsink[:, GROUP * j + i:GROUP * j + i + 1], ACT.Exp,
                                             bias=negm[:, h:h + 1], scale=-1.0).then_inc(s(f"exp_done{l}"), 1)
                elif kind == "T":
                    cg = first[g] + i
                    act.wait_ge(s(f"prob_turned{l}"), cg + 1)
                    if cg >= 2:
                        act.wait_ge(s(f"pv{l}"), cg - 1)
                    nc.scalar.activation(pT_hi[:, cg % 2, :], bank(4 + cg % 2), ACT.Copy).then_inc(s(f"pT_hi{l}"), 1)
                elif kind == "O":
                    act.wait_ge(s(f"pv{l}"), first[g + 1])
                    if g >= 2:
                        act.wait_ge(s(f"o_split{l}"), 2 * (g - 1))
                    src = ps[0:HD, 6 + g % 2, :].rearrange("p (a b n) -> p a b n", a=2, b=2)
                    for odd in range(2):
                        nc.scalar.activation(o_tmp[64 * odd:64 * odd + 64, g % 2, :, :], src[:, :, odd, :],
                                             ACT.Copy).then_inc(s(f"o_read{l}"), 1)
            close(act, "act")

        def attn_vector(dve, l, before):
            groups, steps, first = attn_setup(l)
            c_first = 4 if l == 0 else 0
            after_phase(dve, before)
            nden = 2 if l == 0 else 1

            def denominator(h):
                dve.wait_ge(s(f"exp_done{l}"), nden * h + nden)
                d = den
                if l == 0:
                    nc.vector.tensor_tensor(rden[:, h:h + 1], den[:, h:h + 1], esink[:, h:h + 1],
                                            ALU.add).then_inc(s(f"rden{l}"), 1)
                    dve.wait_ge(s(f"rden{l}"), 2 * h + 1)
                    d = rden
                nc.vector.reciprocal(rden[:, h:h + 1], d[:, h:h + 1]).then_inc(s(f"rden{l}"), 1)

            for kind, g, i in steps:
                j, n, keys, masks = groups[g]
                h = 4 * g + i
                if kind == "S":
                    dve.wait_ge(s(f"scores{l}"), h + 1)
                    sc = bank(2 * (h % 2), 1024)[:, 0:len(keys) * P]
                    if l == 0:
                        nc.vector.reduce_max(mx[:, h:h + 1], sc, AX_X).then_inc(s("smax_raw"), 1)
                        dve.wait_ge(s("smax_raw"), h + 1)
                        nc.vector.scalar_tensor_tensor(out=negm[:, h:h + 1], in0=mx[:, h:h + 1], scalar=-SCALE,
                                                       in1=nsink[:, GROUP * j + i:GROUP * j + i + 1],
                                                       op0=ALU.mult, op1=ALU.min).then_inc(s("smax0"), 1)
                    else:
                        nc.vector.tensor_reduce(negm[:, h:h + 1], sc, AX_X, ALU.max, negate=True).then_inc(s("smax1"), 1)
                elif kind == "D":
                    denominator(h)
                elif kind == "T":
                    cg = first[g] + i
                    dve.wait_ge(s(f"pT_hi{l}"), cg + 1)
                    nc.vector.tensor_tensor(pT_lo[:, cg % 2, :], bank(4 + cg % 2), pT_hi[:, cg % 2, :].bitcast(F32),
                                            ALU.subtract).then_inc(s(f"pT_lo{l}"), 1)
                elif kind == "O":
                    dve.wait_ge(s(f"o_read{l}"), 2 * g + 2)
                    cc = slice(c_first + 2 * j, c_first + 2 * j + 2)
                    tt = slice(n * P, (n + 1) * P)
                    nc.vector.tensor_copy(hT_hi[:, cc, tt], o_tmp[:, g % 2, :, :]).then_inc(s(f"o_split{l}"), 1)
                    dve.wait_ge(s(f"o_split{l}"), 2 * g + 1)
                    nc.vector.tensor_tensor(hT_lo[:, cc, tt], o_tmp[:, g % 2, :, :], hT_hi[:, cc, tt].bitcast(F32),
                                            ALU.subtract).then_inc(s(f"o_split{l}"), 1)
            close(dve, "dve")

        def attn_pool(pool, l, before):
            groups, steps, first = attn_setup(l)
            after_phase(pool, before)
            per = 2 if l == 0 else 1
            for g, (j, n, keys, masks) in enumerate(groups):
                for i in range(GROUP):
                    h = 4 * g + i
                    pool.wait_ge(s(f"rden{l}"), per * (h + 1))
                    pr = prob[:, g % 2, i, 0:len(keys) * P]
                    nc.gpsimd.tensor_scalar(pr, pr, rden[:, h:h + 1], 1.0, ALU.mult,
                                            ALU.mult).then_inc(s(f"prob_norm{l}"), 1)
            close(pool, "pool")

        def gate_tensor(pe, tag, sub, nv):
            for i in range(2 * nv):
                v, half = divmod(i, 2)
                row = 64 * sub + 32 * half + v
                if i >= 2:
                    pe.wait_ge(s(f"{tag}_gate"), i - 1)
                nc.tensor.matmul(bank(6 + i % 2), ident[:, row:row + 1].broadcast_to([P, P]), gate_rows[:, :],
                                 start=True, stop=True, skip_group_check=True).then_inc(s(f"{tag}_gate_mm"), 1)

        def gate_scalar(act, tag, nv):
            for i in range(2 * nv):
                v, half = divmod(i, 2)
                act.wait_ge(s(f"{tag}_gate_mm"), i + 1)
                nc.scalar.activation(gate[:, v, half * BANK:(half + 1) * BANK], bank(6 + i % 2),
                                     ACT.Copy).then_inc(s(f"{tag}_gate"), 1)

        def first_half_scalar(act, tag, t, acc, y0_, sqj_):
            nc.scalar.activation(y0_[:, t, :], acc, ACT.Copy).then_inc(s(f"{tag}_y0"), 1)

        def square_scalar(act, tag, half, t, nt, src, sqj_):
            i = half * nt + t
            if i >= 2:
                act.wait_ge(s(f"{tag}_ysq"), i - 1)
            nc.scalar.activation(sqj_[:, i % 2, :], src, ACT.Square,
                                 accum_out=ssum[:, half, t:t + 1]).then_inc(s(f"{tag}_ysq"), 1)

        def post_pool(pool, tag, nt):
            for t in range(nt):
                pool.wait_ge(s(f"{tag}_ysq"), nt + t + 1)
                nc.gpsimd.tensor_tensor(ssum[:, 0, t:t + 1], ssum[:, 0, t:t + 1], ssum[:, 1, t:t + 1],
                                        ALU.add).then_inc(s(f"{tag}_yr"), 1)
                pool.wait_ge(s(f"{tag}_yr"), 3 * t + 1)
                nc.gpsimd.tensor_scalar(ssum[:, 0, t:t + 1], ssum[:, 0, t:t + 1], 1.0 / D, EPS, ALU.mult,
                                        ALU.add).then_inc(s(f"{tag}_yr"), 1)
                pool.wait_ge(s(f"{tag}_yr"), 3 * t + 2)
                nc.gpsimd.tensor_tensor(rms[:, t:t + 1], ssum[:, 0, t:t + 1], minus_half[:, 0:1],
                                        ALU.pow).then_inc(s(f"{tag}_yr"), 1)

        def post_vector(dve, tag, nt, acc_of, y0_, t0_, t1_):
            dve.wait_ge(s(f"{tag}_gate"), 2 * (2 if nt == ALL_T else 1))
            for t in range(nt):
                v = int(t >= LAT_T)
                dve.wait_ge(s(f"{tag}_yr"), 3 * t + 3)
                if t:
                    dve.wait_ge(s(f"{tag}_post"), 4 * t)
                nc.vector.scalar_tensor_tensor(out=t1_[:, :], in0=acc_of(t), scalar=rms[:, t:t + 1],
                                               in1=gate[:, v, BANK:D], op0=ALU.mult, op1=ALU.mult).then_inc(s(f"{tag}_post"), 1)
                nc.vector.scalar_tensor_tensor(out=t0_[:, :], in0=y0_[:, t, :], scalar=rms[:, t:t + 1],
                                               in1=gate[:, v, 0:BANK], op0=ALU.mult, op1=ALU.mult).then_inc(s(f"{tag}_post"), 1)
                for half, tt in ((1, t1_), (0, t0_)):
                    dve.wait_ge(s(f"{tag}_post"), 4 * t + 2 - half)
                    xv = x[:, t, half * BANK:(half + 1) * BANK]
                    nc.vector.tensor_tensor(xv, xv, tt[:, :], ALU.add).then_inc(s(f"{tag}_post"), 1)

        def out_prefetch_scalar(act, l):
            for m in range(4):
                split_hi(act, f"out{l}", m, 1024, free=False)

        def out_sync(sp, l):
            w = (ab_w_out, c_w_out)[l][0]
            for m in range(8):
                half, u = divmod(m, 4)
                load_unit(sp, f"out{l}", m, w[2 * u * P:(2 * u + 2) * P, half * BANK:(half + 1) * BANK]
                          .rearrange("(k p) n -> p k n", p=P), 1024)

        def out_tensor(pe, l, before, nt):
            phase, tag = f"out{l}", f"mixpost{l}"
            after_phase(pe, before)
            gate_tensor(pe, tag, 0, 2 if nt == ALL_T else 1)
            for half in range(2):
                for t in range(nt):
                    n = half * nt + t
                    if n >= 4:
                        if n - 4 < nt:
                            pe.wait_ge(s(f"{tag}_y0"), n - 3)
                        else:
                            pe.wait_ge(s(f"{tag}_post"), 4 * (n - 4 - nt) + 1)
                    for k in range(KC):
                        m = 4 * half + k // 2
                        if t == 0 and k % 2 == 0:
                            wait_split(pe, phase, m)
                        slot, c0 = unit_slot(phase, m), (k % 2) * BANK
                        tt = slice(t * P, (t + 1) * P)
                        mm = mm3(bank(n % 4), hT_hi[:, k, tt], hT_lo[:, k, tt], w_hi[:, slot, c0:c0 + BANK],
                                 w_lo[:, slot, c0:c0 + BANK], k == 0, k == KC - 1)
                        if t == nt - 1 and k in (1, 3, 5):
                            mm.then_inc(used[phase], 1)
                    mm.then_inc(s(f"{tag}_acc"), 1)
                pe.drain().then_inc(used[phase], 1)
            close(pe, "pe")

        def out_scalar(act, l, before, nt):
            phase, tag = f"out{l}", f"mixpost{l}"
            after_phase(act, before)
            out_prefetch_scalar(act, l)
            gate_scalar(act, tag, 2 if nt == ALL_T else 1)
            for t in range(nt):
                act.wait_ge(s(f"{tag}_acc"), t + 1)
                first_half_scalar(act, tag, t, bank(t % 4), y0, sqj)
                act.wait_ge(s(f"{tag}_y0"), t + 1)
                square_scalar(act, tag, 0, t, nt, y0[:, t, :], sqj)
            for m in range(4, 8):
                split_hi(act, phase, m, 1024)
            for t in range(nt):
                act.wait_ge(s(f"{tag}_acc"), nt + t + 1)
                square_scalar(act, tag, 1, t, nt, bank((nt + t) % 4), sqj)
            close(act, "act")

        def out_pool(pool, l, before, nt):
            after_phase(pool, before)
            for m in range(8):
                split_lo(pool, f"out{l}", m, 1024)
            post_pool(pool, f"mixpost{l}", nt)
            close(pool, "pool")

        def out_vector(dve, l, before, nt):
            after_phase(dve, before)
            post_vector(dve, f"mixpost{l}", nt, lambda t: bank((nt + t) % 4), y0, t0, t1)
            close(dve, "dve")

        TURN = 6
        TURNS = 2 * FT // TURN

        def up_sync(sp, l):
            with sp.Fori(0, TURNS) as i:
                for m in range(TURN):
                    c0 = (m // 2) * P + (m % 2) * DFF
                    src = ffn_w_up[l][:, bass.ds(i * (3 * P) + c0, P)].rearrange("(k p) n -> p k n", p=P)
                    load_unit(sp, f"up{l}", m, src, 1024, i, TURN)

        def up_prefetch(l):
            def act_part(act):
                for m in range(3):
                    split_hi(act, f"up{l}", m, 1024, free=False)

            def pool_part(pool):
                for m in range(3):
                    split_lo(pool, f"up{l}", m, 1024)
            return act_part, pool_part

        def up_tensor(pe, l, before, nt, tag):
            phase = f"up{l}"
            streams = STREAMS[:1 if nt == LAT_T else 2]
            pe.wait_ge(closed["act"], before)
            pe.wait_ge(s(f"{tag}_split"), 2 * KC)
            with pe.Fori(0, TURNS) as i:
                for m in range(TURN):
                    wait_split(pe, phase, m, i, TURN)
                    pe.wait_ge(s(f"taps{l}"), i * TURN + (m + 1))
                    slot = unit_slot(phase, m)
                    acc = bank(2 * (m % 3), 1024)
                    for k in range(KC):
                        kk = slice(k * P, (k + 1) * P)
                        for c0, w in streams:
                            mm = mm3(acc[:, c0:c0 + w], w_hi[:, slot, kk], w_lo[:, slot, kk],
                                     hT_hi[:, k, c0:c0 + w], hT_lo[:, k, c0:c0 + w], k == 0, k == KC - 1)
                    mm.then_inc(used[phase], 1)
            close(pe, "pe")

        def up_scalar(act, l, before, nt):
            phase = f"up{l}"
            T = nt * P
            after_phase(act, before)
            act.sem_inc(s(f"gated{l}"), 1)
            act.sem_inc(s(f"gelu{l}"), 1)

            def turn(i, last):
                for m in range(TURN):
                    b = m % 2
                    col = i * 3 + (m // 2 + b * FT)
                    act.wait_ge(used[phase], i * TURN + (m + 1))
                    act.wait_ge(s(f"gated{l}") if b else s(f"gelu{l}"), i * 3 + (m // 2 + 1))
                    nc.scalar.activation((conv_a, conv_b)[b][:, 0:T], bank(2 * (m % 3), 1024)[:, 0:T], ACT.Identity,
                                         bias=convb[:, l, bass.ds(col, 1)],
                                         scale=convw[l][:, 1, bass.ds(col, 1)]).then_inc(s(f"center{l}"), 1)
                    if not (last and m >= TURN - 3):
                        split_hi(act, phase, m + 3, 1024, i, TURN)
                    if not b:
                        act.wait_ge(s(f"taps{l}"), i * TURN + (m + 4))
                        act.wait_ge(s(f"gated{l}"), i * 3 + (m // 2 + 1))
                        nc.scalar.activation(gelu[:, 0:T], conv_a[:, 0:T], ACT.Gelu_apprx_tanh).then_inc(s(f"gelu{l}"), 1)

            with act.Fori(0, TURNS - 1) as i:
                turn(i, False)
            turn(TURNS - 1, True)
            close(act, "act")

        def up_pool(pool, l, before):
            after_phase(pool, before)
            with pool.Fori(0, TURNS - 1) as i:
                for m in range(3, 3 + TURN):
                    split_lo(pool, f"up{l}", m, 1024, i, TURN)
            for m in range(3, TURN):
                split_lo(pool, f"up{l}", m + TURN * (TURNS - 1), 1024)
            close(pool, "pool")

        def up_vector(dve, l, before, nt):
            streams = STREAMS[:1 if nt == LAT_T else 2]
            T = nt * P
            ns = len(streams)
            after_phase(dve, before)
            dve.sem_inc(s(f"taps{l}"), 3)
            with dve.Fori(0, TURNS) as i:
                for m in range(TURN):
                    b = m % 2
                    col = i * 3 + (m // 2 + b * FT)
                    dve.wait_ge(s(f"center{l}"), i * TURN + (m + 1))
                    cv = (conv_a, conv_b)[b]
                    acc = bank(2 * (m % 3), 1024)
                    for c0, w in streams:
                        nc.vector.scalar_tensor_tensor(out=cv[:, c0 + 1:c0 + w], in0=acc[:, c0:c0 + w - 1],
                                                       scalar=convw[l][:, 0, bass.ds(col, 1)], in1=cv[:, c0 + 1:c0 + w],
                                                       op0=ALU.mult, op1=ALU.add).then_inc(s(f"tap0_{l}"), 1)
                    for v, (c0, w) in enumerate(streams):
                        dve.wait_ge(s(f"tap0_{l}"), i * (TURN * ns) + (m * ns + v + 1))
                        op = nc.vector.scalar_tensor_tensor(out=cv[:, c0:c0 + w - 1], in0=acc[:, c0 + 1:c0 + w],
                                                            scalar=convw[l][:, 2, bass.ds(col, 1)], in1=cv[:, c0:c0 + w - 1],
                                                            op0=ALU.mult, op1=ALU.add)
                        if v == ns - 1:
                            op.then_inc(s(f"taps{l}"), 1)
                    if b:
                        dve.wait_ge(s(f"taps{l}"), i * TURN + (m + 4))
                        dve.wait_ge(s(f"gelu{l}"), i * 3 + (m // 2 + 2))
                        nc.vector.tensor_tensor(act_g[:, bass.ds(i * 3 + m // 2, 1), 0:T].rearrange("p a n -> p (a n)"),
                                                gelu[:, 0:T], conv_b[:, 0:T], ALU.mult).then_inc(s(f"gated{l}"), 1)
            close(dve, "dve")

        DTURNS = FT // 3

        def down_sync(sp, l):
            for half in range(2):
                with sp.Fori(0, DTURNS) as i:
                    for m in range(3):
                        src = ffn_w_down[l][bass.ds(i * (3 * P) + m * P, P), half * BANK:(half + 1) * BANK]
                        load_unit(sp, f"down{l}", half * FT + m, src, BANK, i, 3)

        def down_tensor(pe, l, before, nt):
            phase, tag = f"down{l}", f"ffnpost{l}"
            after_phase(pe, before)
            gate_tensor(pe, tag, 1, 2 if nt == ALL_T else 1)

            def unit(i, m, half, first, last, tiles):
                slot = unit_slot(phase, m)
                for t in tiles:
                    if half and first:
                        pe.wait_ge(s(f"{tag}_y0"), t + 1)
                    tt = slice(t * P, (t + 1) * P)
                    mm = mm3(bank(t), g_hi[:, slot, tt], g_lo[:, slot, tt], w_hi[:, slot, 0:BANK],
                             w_lo[:, slot, 0:BANK], first, last)
                return mm

            def ready(i, m, half):
                wait_split(pe, phase, half * FT + m, i, 3)
                pe.wait_ge(s(f"g_lo{l}"), i * 3 + (half * FT + m + 1))

            for half in range(2):
                for m in range(3):
                    ready(0, m, half)
                    unit(0, m, half, m == 0, False, range(nt)).then_inc(used[phase], 1)
                with pe.Fori(1, DTURNS - 1) as i:
                    for m in range(3):
                        ready(i, m, half)
                        unit(i, m, half, False, False, range(nt)).then_inc(used[phase], 1)
                for m in range(3):
                    ready(DTURNS - 1, m, half)
                for t in range(nt):
                    for m in range(3):
                        mm = unit(DTURNS - 1, m, half, False, m == 2, (t,))
                    mm.then_inc(s(f"{tag}_acc"), 1)
                pe.drain().then_inc(used[phase], 3)
            close(pe, "pe")

        def down_split(act, l, nt, half, m, i=0, first=False):
            phase = f"down{l}"
            T = nt * P
            split_hi(act, phase, half * FT + m, BANK, i, 3, free=not (first and half == 0))
            nc.scalar.activation(g_hi[:, m, 0:T], act_g[:, bass.ds(i * 3 + m, 1), 0:T].rearrange("p a n -> p (a n)"),
                                 ACT.Copy).then_inc(s(f"g_hi{l}"), 1)

        def down_scalar(act, l, before, nt):
            tag = f"ffnpost{l}"
            after_phase(act, before)
            for half in range(2):
                if half == 0:
                    for m in range(3):
                        down_split(act, l, nt, 0, m, 0, True)
                    gate_scalar(act, tag, 2 if nt == ALL_T else 1)
                with act.Fori(1, DTURNS) as i:
                    for m in range(3):
                        down_split(act, l, nt, half, m, i)
                for t in range(nt):
                    act.wait_ge(s(f"{tag}_acc"), half * nt + t + 1)
                    if half == 0:
                        first_half_scalar(act, tag, t, bank(t), y0d, sqjd)
                    else:
                        square_scalar(act, tag, 1, t, nt, bank(t), sqjd)
                if half == 0:
                    for m in range(3):
                        down_split(act, l, nt, 1, m, 0)
                    for t in range(nt):
                        act.wait_ge(s(f"{tag}_y0"), t + 1)
                        square_scalar(act, tag, 0, t, nt, y0d[:, t, :], sqjd)
            close(act, "act")

        def down_pool(pool, l, before, nt):
            after_phase(pool, before)
            for half in range(2):
                with pool.Fori(0, DTURNS) as i:
                    for m in range(3):
                        split_lo(pool, f"down{l}", half * FT + m, BANK, i, 3)
            post_pool(pool, f"ffnpost{l}", nt)
            close(pool, "pool")

        def down_vector(dve, l, before, nt):
            T = nt * P
            after_phase(dve, before)
            for half in range(2):
                with dve.Fori(0, DTURNS) as i:
                    for m in range(3):
                        dve.wait_ge(s(f"g_hi{l}"), i * 3 + (half * FT + m + 1))
                        nc.vector.tensor_tensor(g_lo[:, m, 0:T],
                                                act_g[:, bass.ds(i * 3 + m, 1), 0:T].rearrange("p a n -> p (a n)"),
                                                g_hi[:, m, 0:T].bitcast(F32), ALU.subtract).then_inc(s(f"g_lo{l}"), 1)
            post_vector(dve, f"ffnpost{l}", nt, bank, y0d, t0d, t1d)
            close(dve, "dve")

        block = es.enter_context(nc.Block())
        NT = {0: ALL_T, 1: LAT_T}

        @block.sync
        def _(sp):
            setup_sync(sp)
            ada_sync(sp, 0)
            late_sync(sp)
            for l in range(2):
                if l:
                    ada_sync(sp, 1)
                proj_sync(sp, l)
                out_sync(sp, l)
                up_sync(sp, l)
                down_sync(sp, l)
            for t in range(LAT_T):
                sp.wait_ge(s("ffnpost1_post"), 4 * t + 4)
                sp.dma_start(out[0, t * P:(t + 1) * P, :], x[:, t, :]).then_inc(store_done, 16)
            sp.wait_ge(store_done, 16 * LAT_T)

        @block.tensor
        def _(pe):
            setup_tensor(pe)
            for l in range(2):
                b = 8 * l
                after_phase(pe, b + 1)
                ada_tensor(pe, l)
                norm_tensor(pe, f"mix{l}", b + 2, ALL_T)
                proj_tensor(pe, l, b + 3, f"mix{l}")
                attn_tensor(pe, l, b + 4)
                out_tensor(pe, l, b + 5, NT[l])
                norm_tensor(pe, f"ffn{l}", b + 6, NT[l])
                up_tensor(pe, l, b + 7, NT[l], f"ffn{l}")
                down_tensor(pe, l, b + 8, NT[l])

        @block.scalar
        def _(act):
            setup_scalar(act)
            for l in range(2):
                b = 8 * l
                close(act, "act")
                norm_scalar(act, f"mix{l}", b + 2, 0, ALL_T, proj_prefetch(l)[0])
                proj_scalar(act, l, b + 3)
                attn_scalar(act, l, b + 4)
                out_scalar(act, l, b + 5, NT[l])
                norm_scalar(act, f"ffn{l}", b + 6, 1, NT[l], up_prefetch(l)[0])
                up_scalar(act, l, b + 7, NT[l])
                down_scalar(act, l, b + 8, NT[l])

        @block.gpsimd
        def _(pool):
            close(pool, "pool")
            for l in range(2):
                b = 8 * l
                close(pool, "pool")
                norm_pool(pool, f"mix{l}", b + 2, ALL_T, proj_prefetch(l)[1])
                proj_pool(pool, l, b + 3)
                attn_pool(pool, l, b + 4)
                out_pool(pool, l, b + 5, NT[l])
                norm_pool(pool, f"ffn{l}", b + 6, NT[l], up_prefetch(l)[1])
                up_pool(pool, l, b + 7)
                down_pool(pool, l, b + 8, NT[l])

        @block.vector
        def _(dve):
            setup_vector(dve)
            for l in range(2):
                b = 8 * l
                after_phase(dve, b + 1)
                ada_vector(dve, l)
                norm_vector(dve, f"mix{l}", b + 2, ALL_T)
                proj_vector(dve, l, b + 3)
                attn_vector(dve, l, b + 4)
                out_vector(dve, l, b + 5, NT[l])
                norm_vector(dve, f"ffn{l}", b + 6, NT[l])
                up_vector(dve, l, b + 7, NT[l])
                down_vector(dve, l, b + 8, NT[l])


def shape_constants():
    import numpy as np

    ident = np.eye(P, dtype=np.float32)
    grid_w, n_freq = 64, HD // 4
    pos = np.arange(SEQ)
    freqs = np.float32(10000.0) ** (-np.arange(n_freq, dtype=np.float32) / np.float32(n_freq))
    ang = np.concatenate([(pos // grid_w).astype(np.float32)[:, None] * freqs,
                          (pos % grid_w).astype(np.float32)[:, None] * freqs], axis=-1)
    rope = np.zeros((2, TOK, HD), np.float32)
    rope[0] = 1.0
    rope[0, :SEQ] = np.tile(np.cos(ang), 2)
    rope[1, :SEQ] = np.tile(np.sin(ang), 2)
    q, k = np.arange(P)[:, None], np.arange(P)[None, :]
    mask = np.zeros((2, P, P), np.float32)
    mask[0][k < q] = -1e30
    mask[1][k > q] = -1e30
    edge = np.ones((4, 2, PAD), np.float32)
    for g, w in enumerate(POOL_WINDOWS):
        for i in range(PAD):
            edge[g, 0, i] = w / (min(i, w // 2) + w // 2)
            edge[g, 1, PAD - 1 - i] = w / (w // 2 + min(i + 1, w // 2))
    return {"ident": ident, "rope": rope, "mask": mask, "edge": edge}


_INS = ["x", "c", "ctx", "c_ctx", "ada_w", "ada_b", "mix_pre_g", "mix_post_g", "ffn_pre_g", "ffn_post_g",
        "ab_w_in", "ab_w_out", "pool_w", "pool_scale", "sink_logit", "c_w_qkv", "c_w_out", "c_q_g", "c_k_g",
        "ffn_w_up", "ffn_conv_w", "ffn_conv_b", "ffn_w_down"]


def kernel(**inputs):
    import numpy as np
    import concourse.bacc as bacc
    from concourse.bass_utils import run_bass_kernel_spmd as run

    nc = bacc.Bacc("TRN2", target_bir_lowering=False, num_devices=1, dynamic_dma_scratch_size=1024)
    arrays = {f"in_{n}_dram": np.ascontiguousarray(inputs[n]) for n in _INS}
    arrays.update({f"const_{n}_dram": a for n, a in shape_constants().items()})
    args = [nc.dram_tensor(n, a.shape, mybir.dt.from_np(a.dtype), kind="ExternalInput").ap()
            for n, a in arrays.items()]
    args.append(nc.dram_tensor("out_dram", (1, SEQ, D), F32, kind="ExternalOutput").ap())
    hybrid_backbone_kernel(nc, *args)
    r = run(nc, [arrays], core_ids=[0])
    return r.results[0]["out_dram"]
```

```python
from contextlib import ExitStack

import concourse.bass as bass
from concourse import mybir

F32 = mybir.dt.float32
F32R = mybir.dt.float32r
BF16 = mybir.dt.bfloat16
ALU = mybir.AluOpType
ACT = mybir.ActivationFunctionType
AX_X = mybir.AxisListType.X

P = 128
BANK = 512
D = 1024
KC = D // P
SEQ, CTX = 512, 256
LAT_T, CTX_T = SEQ // P, CTX // P
ALL_T = LAT_T + CTX_T
TOK = SEQ + CTX
HD = 64
GROUP = 4
POOL_CH = D // 2
POOL_WINDOWS = (2, 4, 8, 16)
PAD = max(POOL_WINDOWS) // 2
UBUF = SEQ + CTX + 4 * PAD
B_HEADS, B_KV = 8, 2
C_HEADS, C_KV = 16, 4
DFF = (8 * D // 3) // 128 * 128
FT = DFF // P
EPS = 1e-6
SCALE = HD ** -0.5
STREAMS = ((0, SEQ), (SEQ, CTX))
PADDED = ((PAD, SEQ), (SEQ + 3 * PAD, CTX))

RAW = 3
UNITS = {"proj0": 12, "out0": 8, "up0": 2 * FT, "down0": 2 * FT,
         "proj1": 12, "out1": 8, "up1": 2 * FT, "down1": 2 * FT}
RINGS = {"proj": 4, "out": 4, "up": 3, "down": 3}
FIRST_UNIT = {}
_n = 0
for _k, _v in UNITS.items():
    FIRST_UNIT[_k] = _n
    _n += _v

VEC_ROWS = 52
CONV_ROWS = 3 * 2 * FT
BIAS_ROWS = 2 * 2 * FT

PROJ = {
    0: (("pool", 0, 512, ALL_T, 0), ("kv", 1024, 256, ALL_T, 0), ("q", 512, 512, ALL_T, 0)),
    1: (("kv", 1024, 512, ALL_T, 0), ("q", 0, 512, LAT_T, 0), ("q", 512, 512, LAT_T, 8)),
}


def attention_groups(l):
    ctx = [LAT_T, LAT_T + 1]
    if l == 1:
        return [(j, n, list(range(ALL_T)), {}) for j in range(C_KV) for n in range(LAT_T)]
    out = []
    for j in range(B_KV):
        for n in range(LAT_T):
            near = [m for m in (n - 1, n, n + 1) if 0 <= m < LAT_T]
            out.append((j, n, ctx + near, {m: int(m > n) for m in near if m != n}))
        out += [(j, n, ctx, {}) for n in ctx]
    return out


INTERLEAVE = ("S0", "S1", "C", "E0", "C", "E1", "D0", "S2", "C", "D1", "E2", "C", "S3", "D2", "C", "E3", "C", "D3")


def attention_steps(groups):
    steps, before, ended = [], None, None
    slots = INTERLEAVE.count("C")
    for g in range(len(groups) + 1):
        n = len(groups[g - 1][2]) if g else 0
        at = {c * slots // n: c for c in range(n)}
        slot = 0
        for token in INTERLEAVE:
            if token == "C":
                if slot in at:
                    steps.append(("T", g - 1, at[slot]))
                    if before is not None:
                        steps.append(("V", *before))
                    if ended is not None:
                        steps.append(("O", ended, 0))
                        ended = None
                    if before is not None and before[1] == len(groups[before[0]][2]) - 1:
                        ended = before[0]
                    before = (g - 1, at[slot])
                slot += 1
            elif g < len(groups):
                steps.append((token[0], g, int(token[1])))
    return steps + [("V", *before), ("O", before[0], 0)]


def key_pieces(keys):
    out = []
    for i, t in enumerate(keys):
        if out and out[-1][1] + out[-1][2] == t * P and (i * P) % BANK:
            out[-1][2] += P
        else:
            out.append([i * P, t * P, P])
    return out


def hybrid_backbone_kernel(nc, x_in, c, ctx_in, c_ctx, ada_w, ada_b, mix_pre_g, mix_post_g, ffn_pre_g,
                           ffn_post_g, ab_w_in, ab_w_out, pool_w, pool_scale, sink_logit, c_w_qkv, c_w_out,
                           c_q_g, c_k_g, ffn_w_up, ffn_conv_w, ffn_conv_b, ffn_w_down,
                           ident_in, rope_in, mask_in, edge_in, out):
    es = ExitStack()
    with es:
        cursor = [(nc.sbuf_base + 63) // 64 * 64]

        def sb(name, shape, dt=F32, at=None):
            size = 2 if dt == BF16 else 4
            for s in shape[1:]:
                size *= s
            size = (size + 63) // 64 * 64
            if at is None:
                at = cursor[0]
                cursor[0] += size
            t = nc.alloc_sbuf_tensor_at(name, shape, dt, offset=at)
            return t, at + size

        def keep(name, shape, dt=F32):
            return sb(name, shape, dt)[0]

        x = keep("x", [P, ALL_T, D])
        hT_hi = keep("hT_hi", [P, KC, TOK], F32R)
        hT_lo = keep("hT_lo", [P, KC, TOK], F32R)
        raw = keep("raw", [P, RAW, 1024])
        split_at = cursor[0]
        w_hi = keep("w_hi", [P, 4, 1024], F32R)
        w_lo = keep("w_lo", [P, 4, 1024], F32R)
        ident = keep("ident", [P, P])
        ident_b = keep("ident_b", [P, P], BF16)
        mask_b = keep("mask_b", [P, 2, P], BF16)
        rope = keep("rope", [P, 2, ALL_T, HD])
        edge = keep("edge", [P, 4, 2, PAD])
        cols = keep("cols", [P, VEC_ROWS])
        convw = [keep(f"convw{l}", [P, 3, 2 * FT]) for l in range(2)]
        convb = keep("convb", [P, 2, 2 * FT])
        cstat = keep("cstat", [P, KC, 32])
        mul_col = keep("mul_col", [P, 2, 2, KC])
        add_col = keep("add_col", [P, 2, 2, KC])
        gate_rows = keep("gate_rows", [P, D])
        nsink = keep("nsink", [P, B_HEADS])
        minus_half = keep("minus_half", [P, 32])
        ssum = keep("ssum", [P, 2, 8])
        rms = keep("rms", [P, 8])
        xsum = keep("xsum", [P, 8])
        xrms = keep("xrms", [P, 8])
        select = keep("select", [P, 64])
        select_v = keep("select_v", [P, 2, 32])
        gate_at = cursor[0]
        gate = keep("gate", [P, 2, D])
        region = cursor[0]

        pw_hi, a = sb("pw_hi", [P, 4, P], F32R, gate_at)
        pw_lo, a = sb("pw_lo", [P, 4, P], F32R, a)
        pw, a = sb("pw", [P, 4, P], F32, a)
        vecs, a = sb("vecs", [P, 4, P], F32, region)
        silu, a = sb("silu", [P, 2, 16], F32, a)
        mask_f, a = sb("mask_f", [P, 2, P], F32, a)
        xn_at = region + 24 * 1024
        xn, a = sb("xn", [P, ALL_T, D], F32, xn_at)
        h32, tail = sb("h32", [P, 2, TOK], F32, a)
        def ada_memory(tag, acc_at, slots_at, bias_at, post_at):
            acc = sb(f"ada_acc_{tag}", [P, 2, D], F32, acc_at)[0]
            slots = [sb(f"ada_w_{tag}{i}", [P, D], F32, o)[0] for i, o in enumerate(slots_at)]
            bias = sb(f"ada_bias_{tag}", [P, D], F32, bias_at)[0]
            post = sb(f"ada_post_{tag}", [P, D], F32, post_at)[0]
            return acc, slots, bias, post

        KB4 = 4096
        beside_out = ada_memory("out", tail, [region + 20 * 1024] + [tail + i * KB4 for i in (2, 3, 4)],
                                tail + 5 * KB4, tail + 6 * KB4)
        beside_proj = ada_memory("proj", region, [region + i * KB4 for i in (2, 3, 4, 5)],
                                 region + 4 * (B_HEADS * TOK + 2 * B_KV * TOK + 2 * ALL_T * B_KV * HD), tail + 7 * KB4)
        conv_at = region + 4 * FT * TOK
        beside_up = ada_memory("up", conv_at + 3 * 4 * TOK, [gate_at, gate_at + KB4, split_at + 3 * KB4, split_at + 7 * KB4],
                               conv_at, conv_at + KB4)
        tops = [tail + 8 * KB4, conv_at + 3 * 4 * TOK + 2 * KB4]
        qT, a = sb("qT", [P, C_HEADS * SEQ], F32R, region)
        kT, a = sb("kT", [P, 2, C_KV, TOK], F32R, a)
        v_hi, a = sb("v_hi", [P, ALL_T, C_KV * HD], F32R, a)
        v_lo, a = sb("v_lo", [P, ALL_T, C_KV * HD], F32R, a)
        qkn_at = a
        qkn, a = sb("qkn", [P, BANK], F32, a)
        qka, a = sb("qka", [P, BANK], F32, a)
        qkb, a = sb("qkb", [P, BANK], F32, a)
        qks, a = sb("qks", [P, 1024], F32R, a)
        sq, a = sb("sq", [P, BANK], F32, a)
        qk_ss, a = sb("qk_ss", [P, 8], F32, a)
        qk_ms, a = sb("qk_ms", [P, 8], F32, a)
        qk_r, a = sb("qk_r", [P, 8], F32, a)
        tops.append(a)
        qk_gain, a = sb("qk_gain", [P, 2, HD], F32, max(tops[1:]))
        tops.append(a)
        qk_tab, b = sb("qk_tab", [P, 4, ALL_T, HD], F32, gate_at)
        assert b <= region
        q0T, a = sb("q0T", [P, B_HEADS, TOK], F32R, region)
        k0T, a = sb("k0T", [P, 2, B_KV, TOK], F32R, a)
        v0_hi, a = sb("v0_hi", [P, ALL_T, B_KV * HD], F32R, a)
        v0_lo, a = sb("v0_lo", [P, ALL_T, B_KV * HD], F32R, a)
        d_hi, a = sb("d_hi", [P, UBUF], F32R, a)
        d_lo, a = sb("d_lo", [P, UBUF], F32R, a)
        sums, a = sb("sums", [P, 2, UBUF], F32, a)
        ubuf, a = sb("ubuf", [P, 4, UBUF], F32, a)
        assert a <= region + 4 * (C_HEADS * SEQ + 2 * C_KV * TOK + 2 * ALL_T * C_KV * HD)
        prob, a = sb("prob", [P, 2, GROUP, TOK], F32, split_at)
        pT_hi, a = sb("pT_hi", [P, 2, BANK], F32R, a)
        pT_lo, a = sb("pT_lo", [P, 2, BANK], F32R, a)
        assert a <= split_at + 2 * 4 * 4096
        o_tmp, a = sb("o_tmp", [P, 2, 2, P], F32, qkn_at)
        small, a = sb("small", [P, 5, 64], F32, a)
        y0, a = sb("y0", [P, ALL_T, BANK], F32, region)
        sqj, a = sb("sqj", [P, 2, BANK], F32, a)
        t0, a = sb("t0", [P, BANK], F32, a)
        t1, a = sb("t1", [P, BANK], F32, a)
        assert a <= region + 20 * 1024
        act_g, a = sb("act_g", [P, FT, TOK], F32, region)
        conv_a, a = sb("conv_a", [P, TOK], F32, a)
        conv_b, a = sb("conv_b", [P, TOK], F32, a)
        gelu, a = sb("gelu", [P, TOK], F32, a)
        tops.append(a)
        hT_at = split_at - RAW * 4096 - 2 * KC * TOK * 4
        y0d, b = sb("y0d", [P, ALL_T, BANK], F32, hT_at)
        sqjd, b = sb("sqjd", [P, 2, BANK], F32, b)
        t0d, b = sb("t0d", [P, BANK], F32, b)
        t1d, b = sb("t1d", [P, BANK], F32, b)
        g_hi, b = sb("g_hi", [P, 3, TOK], F32R, b)
        g_lo, b = sb("g_lo", [P, 3, TOK], F32R, b)
        assert b <= hT_at + 2 * KC * TOK * 4
        assert hT_at + 2 * KC * TOK * 4 + RAW * 4096 == split_at
        assert max(tops) <= nc.sbuf_usable_end, (tops, nc.sbuf_usable_end)

        ps = es.enter_context(nc.psum_tensor("ps", [P, 8, BANK], F32))
        psf = ps[:, :, :].rearrange("p b n -> p (b n)")

        def bank(n, width=BANK):
            return psf[:, n * BANK:n * BANK + width]

        def sem(name):
            return es.enter_context(nc.semaphore(name))

        x_landed = sem("x_landed")
        ctx_landed = sem("ctx_landed")
        rows_landed = sem("rows_landed")
        late_landed = sem("late_landed")
        store_done = sem("store_done")
        landed = [sem(f"w_landed{i}") for i in range(RAW)]
        hi_split = sem("w_hi_split")
        lo_split = sem("w_lo_split")
        used = {k: sem(f"{k}_w_used") for k in UNITS}
        closed = {k: sem(f"{k}_closed") for k in ("pe", "act", "dve", "pool")}
        sems = {}

        def s(name):
            if name not in sems:
                sems[name] = sem(name)
            return sems[name]

        def close(eng, name):
            eng.drain().then_inc(closed[name], 1)

        def after_phase(eng, n):
            for k in ("pe", "act", "dve", "pool"):
                eng.wait_ge(closed[k], n)

        def unit_slot(phase, u):
            return u % RINGS[phase[:-1]]

        def load_unit(sp, phase, m, src, width, turn=0, per_turn=0):
            n = FIRST_UNIT[phase] + m
            if n >= RAW:
                sp.wait_ge(lo_split, turn * per_turn + (n - RAW + 1))
            sp.dma_start(raw_view(n % RAW, src, width), src).then_inc(landed[n % RAW], 16)

        def raw_view(slot, src, width):
            v = raw[:, slot, 0:width]
            return v if len(src.shape) == 2 else v.rearrange("p (k n) -> p k n", k=src.shape[1])

        def split_hi(act, phase, m, width, turn=0, per_turn=0, free=True):
            n = FIRST_UNIT[phase] + m
            act.wait_ge(landed[n % RAW], turn * (16 * per_turn // RAW) + 16 * (n // RAW + 1))
            if free:
                ring = RINGS[phase[:-1]]
                act.wait_ge(used[phase], turn * per_turn + (m - ring + 1))
            nc.scalar.activation(w_hi[:, unit_slot(phase, m), 0:width], raw[:, n % RAW, 0:width],
                                 ACT.Copy).then_inc(hi_split, 1)

        def split_lo(pool, phase, m, width, turn=0, per_turn=0):
            n = FIRST_UNIT[phase] + m
            pool.wait_ge(hi_split, turn * per_turn + (n + 1))
            slot = unit_slot(phase, m)
            nc.gpsimd.tensor_tensor(w_lo[:, slot, 0:width], raw[:, n % RAW, 0:width],
                                    w_hi[:, slot, 0:width].bitcast(F32), ALU.subtract).then_inc(lo_split, 1)

        def wait_split(pe, phase, m, turn=0, per_turn=0):
            pe.wait_ge(lo_split, turn * per_turn + (FIRST_UNIT[phase] + m + 1))

        def mm3(outp, s_hi, s_lo, m_hi, m_lo, first, last):
            nc.tensor.matmul(outp, s_hi, m_hi, start=first, stop=False, skip_group_check=True)
            nc.tensor.matmul(outp, s_hi, m_lo, start=False, stop=False, skip_group_check=True)
            return nc.tensor.matmul(outp, s_lo, m_hi, start=False, stop=last, skip_group_check=True)

        def setup_sync(sp):
            def ld(dst, src):
                sp.dma_start(dst, src).then_inc(rows_landed, 16)

            def rows(a):
                return a.rearrange("a (k n) -> (a k) n", n=P)

            ld(ident[:, :], ident_in)
            ld(vecs[0:16, 0, :], rows(mix_pre_g))
            ld(vecs[16:32, 0, :], rows(ffn_pre_g))
            ld(vecs[32:40, 0, :], rows(c))
            ld(vecs[40:48, 0, :], c_ctx.rearrange("(k n) -> k n", n=P))
            ld(vecs[48:52, 0, :], rows(pool_scale))
            ld(vecs[0:CONV_ROWS, 1, :], ffn_conv_w[0].rearrange("t (f n) -> (t f) n", n=P))
            ld(vecs[0:CONV_ROWS, 2, :], ffn_conv_w[1].rearrange("t (f n) -> (t f) n", n=P))
            ld(vecs[0:BIAS_ROWS // 2, 3, :], ffn_conv_b[0:1].rearrange("a (f n) -> (a f) n", n=P))
            ld(vecs[BIAS_ROWS // 2:BIAS_ROWS, 3, :], ffn_conv_b[1:2].rearrange("a (f n) -> (a f) n", n=P))

        def late_sync(sp):
            def ld(dst, src):
                sp.dma_start(dst, src).then_inc(late_landed, 16)

            ld(mask_f[:, :, :], mask_in.rearrange("a p n -> p a n"))
            ld(rope[:, :, :, :], rope_in.rearrange("a (t p) n -> p a t n", p=P))
            ld(edge[:, :, :, :], edge_in.partition_broadcast(P))
            ld(nsink[:, :], sink_logit.rearrange("a j g -> a (j g)").partition_broadcast(P).rearrange("p a n -> p (a n)"))
            ld(pw[:, :, :], pool_w[0].rearrange("g p n -> p g n"))

        def x_sync(sp):
            sp.dma_start(x[:, 0:LAT_T, :], x_in[0].rearrange("(t p) n -> p t n", p=P)).then_inc(x_landed, 16)
            sp.dma_start(x[:, LAT_T:ALL_T, :], ctx_in[0].rearrange("(t p) n -> p t n", p=P)).then_inc(ctx_landed, 16)

        def setup_tensor(pe):
            pe.wait_ge(rows_landed, 16 * 10)
            for n, (t, r) in enumerate(((0, VEC_ROWS), (1, CONV_ROWS), (2, CONV_ROWS), (3, BIAS_ROWS))):
                nc.tensor.transpose(bank(n, r), vecs[0:r, t, :], ident[0:r, 0:r]).then_inc(s("rows_turned"), 1)
            close(pe, "pe")

        SETUP_DVE = 5

        def setup_vector(dve):
            nc.vector.memset(cstat[:, :, :], 0.0).then_inc(s("setup_dve"), 1)
            nc.vector.memset(minus_half[:, :], -0.5).then_inc(s("setup_dve"), 1)
            nc.vector.memset(select[:, :], 0.0).then_inc(s("setup_dve"), 1)
            nc.vector.memset(gate_rows[:, :], 0.0).then_inc(s("setup_dve"), 1)
            dve.wait_ge(s("setup_dve"), 3)
            nc.vector.memset(select[:, 32:33], 1.0).then_inc(s("setup_dve"), 1)
            dve.wait_ge(s("rows_turned"), 1)
            nc.vector.tensor_copy(cols[:, :], bank(0, VEC_ROWS)).then_inc(s("setup_dve"), 1)
            dve.wait_ge(s("exp_c"), 1)
            nc.vector.tensor_scalar(silu[:, 1, :], silu[:, 0, :], 1.0, None, ALU.add).then_inc(s("setup_dve"), 1)
            dve.wait_ge(s("setup_dve"), 7)
            nc.vector.reciprocal(silu[:, 0, :], silu[:, 1, :]).then_inc(s("setup_dve"), 1)
            dve.wait_ge(s("setup_dve"), 8)
            nc.vector.tensor_tensor(cstat[:, :, 0:2].rearrange("p k v -> p v k"),
                                    cols[:, 32:48].rearrange("p (v k) -> p v k", v=2),
                                    silu[:, 0, :].rearrange("p (v k) -> p v k", v=2), ALU.mult).then_inc(s("setup_dve"), 1)
            for n in range(2):
                dve.wait_ge(s("rows_turned"), 2 + n)
                nc.vector.tensor_copy(convw[n][:, :, :].rearrange("p t f -> p (t f)"),
                                      bank(1 + n, CONV_ROWS)).then_inc(s("setup_dve"), 1)
            dve.wait_ge(s("rows_turned"), 4)
            nc.vector.tensor_copy(convb[:, :, :].rearrange("p l f -> p (l f)"), bank(3, BIAS_ROWS)).then_inc(s("setup_dve"), 1)
            close(dve, "dve")

        def setup_scalar(act):
            act.wait_ge(s("setup_dve"), 6)
            nc.scalar.activation(silu[:, 0, :], cols[:, 32:48], ACT.Exp, scale=-1.0).then_inc(s("exp_c"), 1)
            close(act, "act")

        ADA_RING = 4

        def ada_row(l, i, v):
            return 96 + 2 * (5 - i) + v if l else 32 * (i // 2) + 2 * (i % 2) + v

        def ada_load(sp, n, mem, l, rows, cols_, turn=0):
            if n >= ADA_RING:
                sp.wait_ge(s("ada_mac"), turn * (2 * KC) + 2 * (n - ADA_RING + 1))
            sp.dma_start(mem[1][n % ADA_RING][:, :], ada_w[l, rows, cols_]).then_inc(s(f"ada_landed{n % ADA_RING}"), 16)

        def ada_loads(sp, mem, first, last):
            for n in range(first, last):
                i, k = divmod(n, KC)
                ada_load(sp, n, mem, 0, slice(k * P, (k + 1) * P), slice(i * D, (i + 1) * D))

        def ada_small_loads(sp, mem, l, blocks):
            for i in blocks:
                r = ada_row(l, i, 0)
                sp.dma_start(mem[2][r:r + 2, :], ada_b[l, i * D:(i + 1) * D].partition_broadcast(2)
                             ).then_inc(s("ada_rows_landed"), 16)
            for i, g in ((2, mix_post_g), (5, ffn_post_g)):
                if i in blocks:
                    r0, r1 = ({2: (32, 34), 5: (64, 68)}, {2: (102, 108), 5: (96, 102)})[l][i]
                    sp.dma_start(mem[3][r0:r1, :], g[l, :].partition_broadcast(r1 - r0)
                                 ).then_inc(s("ada_rows_landed"), 16)

        def ada_mac(dve, mem, n, k, turn=0):
            acc, slots = mem[0], mem[1]
            if k == 0:
                if n:
                    dve.wait_ge(s("ada_sum"), turn + n // KC)
            else:
                dve.wait_ge(s("ada_mac"), turn * (2 * KC) + 2 * n)
            dve.wait_ge(s(f"ada_landed{n % ADA_RING}"), turn * (16 * KC // ADA_RING) + 16 * (n // ADA_RING + 1))
            for v in range(2):
                w, f = slots[n % ADA_RING][:, :], cstat[:, k, v:v + 1]
                if k == 0:
                    op = nc.vector.tensor_scalar(acc[:, v, :], w, f, None, ALU.mult)
                else:
                    op = nc.vector.scalar_tensor_tensor(out=acc[:, v, :], in0=w, scalar=f, in1=acc[:, v, :],
                                                        op0=ALU.mult, op1=ALU.add)
                op.then_inc(s("ada_mac"), 1)

        def ada_macs(dve, mem, blocks):
            for i in blocks:
                for k in range(KC):
                    ada_mac(dve, mem, i * KC + k, k)

        def ada_sum(pe, mem, i):
            pe.wait_ge(s("ada_mac"), 2 * KC * (i + 1))
            r0 = ada_row(0, i, 0) // 32 * 32
            for v in range(2):
                m = ada_row(0, i, v) - r0
                for half in range(2):
                    mm = nc.tensor.matmul(ps[r0:r0 + 32, 4 + half, :], select[:, 32 - m:64 - m],
                                          mem[0][:, v, half * BANK:(half + 1) * BANK],
                                          start=m == 0, stop=m == 3, skip_group_check=True)
            mm.then_inc(s("ada_sum"), 1)

        def ada_turn(pe, n, b):
            pe.wait_ge(s("ada_biased"), n)
            for k in range(KC):
                mm = nc.tensor.transpose(bank(b, 2 * BANK)[:, k * P:(k + 1) * P], gate_rows[:, k * P:(k + 1) * P],
                                         ident[:, :])
            mm.then_inc(s("ada_turned"), 1)

        def ada_bias(dve, mem, n, rows_landed_, r0, nr, src):
            dve.wait_ge(s("ada_rows_landed"), 16 * rows_landed_)
            nc.vector.tensor_tensor(gate_rows[r0:r0 + nr, :], src, mem[2][r0:r0 + nr, :],
                                    ALU.add).then_inc(s("ada_biased"), 1)

        def ada_columns(dve, n, l, blocks, b):
            dve.wait_ge(s("ada_turned"), n)
            turned = bank(b, 2 * BANK).rearrange("p (k r) -> p r k", r=P)
            for i in blocks:
                sub, what = divmod(i, 3)
                for v in range(2):
                    src = turned[:, ada_row(l, i, v), :]
                    if what == 0:
                        nc.vector.tensor_copy(add_col[:, sub, v, :], src).then_inc(s("ada_columns"), 1)
                    elif what == 1:
                        g = 16 * sub + 8 * l
                        nc.vector.scalar_tensor_tensor(out=mul_col[:, sub, v, :], in0=src, scalar=1.0,
                                                       in1=cols[:, g:g + 8], op0=ALU.add, op1=ALU.mult
                                                       ).then_inc(s("ada_columns"), 1)

        def ada_gates(dve, mem, n, r0, nr):
            dve.wait_ge(s("ada_turned"), n)
            nc.vector.tensor_tensor(gate_rows[r0:r0 + nr, :], gate_rows[r0:r0 + nr, :], mem[3][r0:r0 + nr, :],
                                    ALU.mult).then_inc(s("ada_gates"), 1)

        def start_vector(dve):
            ada_macs(dve, beside_out, (0, 1))
            dve.wait_ge(s("ada_sum"), 2)
            ada_bias(dve, beside_out, 1, 2, 0, 4, psf[0:4, 4 * BANK:6 * BANK])
            dve.wait_ge(late_landed, 5 * 16)
            nc.vector.tensor_copy(ident_b[:, :], ident[:, :]).then_inc(s("late_dve"), 1)
            nc.vector.tensor_copy(mask_b[:, :, :], mask_f[:, :, :]).then_inc(s("late_dve"), 1)
            nc.vector.tensor_scalar(nsink[:, :], nsink[:, :], -1.0, None, ALU.mult).then_inc(s("late_dve"), 1)
            ada_columns(dve, 1, 0, (0, 1), 4)
            nc.vector.tensor_copy(pw_hi[:, :, :], pw[:, :, :]).then_inc(s("late_dve"), 1)
            dve.wait_ge(s("late_dve"), 4)
            nc.vector.tensor_tensor(pw_lo[:, :, :], pw[:, :, :], pw_hi[:, :, :].bitcast(F32),
                                    ALU.subtract).then_inc(s("late_dve"), 1)
            close(dve, "dve")

        def start_tensor(pe):
            pe.wait_ge(s("setup_dve"), SETUP_DVE)
            ada_sum(pe, beside_out, 0)
            ada_sum(pe, beside_out, 1)
            ada_turn(pe, 1, 4)
            close(pe, "pe")

        def start_scalar(act):
            for t in range(ALL_T):
                act.wait_ge(x_landed if t < LAT_T else ctx_landed, 16)
                if t:
                    act.wait_ge(s("mix0_xn"), t)
                nc.scalar.activation(xn[:, t, :], x[:, t, :], ACT.Square,
                                     accum_out=xsum[:, t:t + 1]).then_inc(s("mix0_sq"), 1)
                act.wait_ge(s("mix0_rms"), 2 * t + 2)
                nc.scalar.activation(xn[:, t, :], x[:, t, :], ACT.Copy,
                                     scale=xrms[:, t:t + 1]).then_inc(s("mix0_xn"), 1)
            close(act, "act")

        def start_pool(pool):
            pool.wait_ge(s("setup_dve"), SETUP_DVE)
            for t in range(ALL_T):
                x_rms(pool, "mix0", t)
            close(pool, "pool")

        def x_square(act, tag, after, t):
            act.wait_ge(s(f"{after}_post"), 4 * t + 4)
            nc.scalar.activation(xn[:, t, :], x[:, t, :], ACT.Square, accum_out=xsum[:, t:t + 1]).then_inc(s(f"{tag}_sq"), 1)

        def x_rms(pool, tag, t):
            pool.wait_ge(s(f"{tag}_sq"), t + 1)
            nc.gpsimd.tensor_scalar(xsum[:, t:t + 1], xsum[:, t:t + 1], 1.0 / D, EPS, ALU.mult,
                                    ALU.add).then_inc(s(f"{tag}_rms"), 1)
            pool.wait_ge(s(f"{tag}_rms"), 2 * t + 1)
            nc.gpsimd.tensor_tensor(xrms[:, t:t + 1], xsum[:, t:t + 1], minus_half[:, 0:1],
                                    ALU.pow).then_inc(s(f"{tag}_rms"), 1)

        def x_normed(dve, tag, t):
            dve.wait_ge(s(f"{tag}_rms"), 2 * t + 2)
            nc.vector.tensor_scalar(xn[:, t, :], x[:, t, :], xrms[:, t:t + 1], None, ALU.mult).then_inc(s(f"{tag}_xn"), 1)

        def norm_scalar(act, tag, before, sub, nt, prefetch):
            after_phase(act, before)
            ns = 2 if nt == ALL_T else 1
            prefetch(act, range(0, 1))
            for k in range(KC):
                act.wait_ge(s(f"{tag}_turned"), k + 1)
                if k >= 2:
                    act.wait_ge(s(f"{tag}_split"), 2 * (k - 1))
                for v in range(ns):
                    c0, n = STREAMS[v]
                    nc.scalar.activation(h32[:, k % 2, c0:c0 + n], bank(2 * (k % 2), 1024)[:, c0:c0 + n],
                                         ACT.Identity, bias=add_col[:, sub, v, k:k + 1],
                                         scale=mul_col[:, sub, v, k:k + 1]).then_inc(s(f"{tag}_h32"), 1)
                if k % 2:
                    prefetch(act, range(1 + k // 2, 2 + k // 2))
            close(act, "act")

        def norm_pool(pool, tag, before, nt, prefetch):
            after_phase(pool, before)
            prefetch(pool)
            close(pool, "pool")

        def norm_vector(dve, tag, before, nt):
            after_phase(dve, before)
            ns = 2 if nt == ALL_T else 1
            T = nt * P
            for k in range(KC):
                dve.wait_ge(s(f"{tag}_h32"), ns * (k + 1))
                nc.vector.tensor_copy(hT_hi[:, k, 0:T], h32[:, k % 2, 0:T]).then_inc(s(f"{tag}_split"), 1)
                dve.wait_ge(s(f"{tag}_split"), 2 * k + 1)
                nc.vector.tensor_tensor(hT_lo[:, k, 0:T], h32[:, k % 2, 0:T], hT_hi[:, k, 0:T].bitcast(F32),
                                        ALU.subtract).then_inc(s(f"{tag}_split"), 1)
            close(dve, "dve")

        def norm_tensor(pe, tag, before, nt):
            after_phase(pe, before)
            ns = 2 if nt == ALL_T else 1
            for k in range(KC):
                if k >= 2:
                    pe.wait_ge(s(f"{tag}_h32"), ns * (k - 1))
                for t in range(nt):
                    if k == 0:
                        pe.wait_ge(s(f"{tag}_xn"), t + 1)
                    mm = nc.tensor.transpose(bank(2 * (k % 2), 1024)[:, t * P:(t + 1) * P],
                                             xn[:, t, k * P:(k + 1) * P], ident[:, :])
                mm.then_inc(s(f"{tag}_turned"), 1)
            close(pe, "pe")

        def token_tiles(l):
            out = []
            for gi, (kind, _, w, nt, h0) in enumerate(PROJ[l]):
                if kind != "pool":
                    heads = w // HD if kind == "q" else w // HD // 2
                    out += [(gi, kind, t, heads, h0) for t in range(nt)]
            return out

        def rope_plan(l):
            base, n, tb, m = [], 0, [], 0
            for _, kind, _, heads, _ in token_tiles(l):
                base.append(n)
                tb.append(m)
                n += 6 + (2 if l else 0) + (kind == "kv")
                m += 2 if (l or kind == "q") else 1
            return base + [n], tb + [m]

        def proj_sync(sp, l):
            w = (ab_w_in, c_w_qkv)[l][0]
            m = 0
            for _, c0, width, _, _ in PROJ[l]:
                for u in range(4):
                    src = w[2 * u * P:(2 * u + 2) * P, c0:c0 + width].rearrange("(k p) n -> p k n", p=P)
                    load_unit(sp, f"proj{l}", m, src, 2 * width)
                    if l == 0 and m == 6:
                        after_phase(sp, 3)
                        ada_small_loads(sp, beside_proj, 0, (2, 3))
                        ada_loads(sp, beside_proj, 2 * KC, 4 * KC)
                    m += 1

        def unit_width(l, m):
            return 2 * PROJ[l][m // 4][2]

        def acc_free_steps(l, kind):
            return (2 if l else 2) + (kind == "kv")

        def proj_tensor(pe, l, before, tag):
            phase = f"proj{l}"
            base, tb = rope_plan(l)
            tiles = token_tiles(l)
            q_t = (q0T[:, :, :], qT[:, :].rearrange("p (h n) -> p h n", h=C_HEADS))[l]

            def turn(n):
                _, kind, _, heads, _ = tiles[n]
                blocks = heads if kind == "q" else 2 * heads
                pe.wait_ge(s(f"qk_steps{l}"), base[n + 1])
                if kind == "kv":
                    pe.wait_ge(s(f"k_dup{l}"), n + 1)
                for b in range(tb[n + 1] - tb[n]):
                    nb = tb[n] + b
                    if nb >= 2:
                        pe.wait_ge(s(f"turned_read{l}"), nb - 1)
                    for i in range(4):
                        mm = nc.tensor.transpose(bank(2 + nb % 2)[:, i * P:(i + 1) * P],
                                                 qks[:, (4 * b + i) * P:(4 * b + i + 1) * P].bitcast(F32), ident[:, :])
                    mm.then_inc(s(f"qk_turned{l}"), 1)

            after_phase(pe, before - 1)
            for k in range(KC):
                pe.wait_ge(s(f"{tag}_split"), 2 * (k + 1))
            pe.wait_ge(closed["act"], before)
            m = n = 0
            for gi, (kind, _, width, nt, _) in enumerate(PROJ[l]):
                def wv(part, k, c0, w):
                    slot = unit_slot(phase, m + k // 2)
                    return part[:, slot, (k % 2) * width + c0:(k % 2) * width + c0 + w]

                if kind == "pool":
                    for f in range(4):
                        if f >= 2:
                            pe.wait_ge(s("u_read"), 2 * (f - 1))
                        for k in range(KC):
                            if f == 0 and k % 2 == 0:
                                wait_split(pe, phase, m + k // 2)
                            for c0, w in STREAMS:
                                mm = mm3(bank(2 * (f % 2), 1024)[:, c0:c0 + w], wv(w_hi, k, f * P, P), wv(w_lo, k, f * P, P),
                                         hT_hi[:, k, c0:c0 + w], hT_lo[:, k, c0:c0 + w], k == 0, k == KC - 1)
                            if f == 3 and k in (1, 3, 5):
                                mm.then_inc(used[phase], 1)
                        mm.then_inc(s("u_done"), 1)
                        if f == 2:
                            ada_sum(pe, beside_proj, 2)
                    pe.drain().then_inc(used[phase], 1)
                    pe.wait_ge(s("u_read"), 6)
                else:
                    for t in range(nt):
                        if n >= 2:
                            pe.wait_ge(s(f"qk_steps{l}"), base[n - 2] + acc_free_steps(l, tiles[n - 2][1]))
                        for k in range(KC):
                            if t == 0 and k % 2 == 0:
                                wait_split(pe, phase, m + k // 2)
                            tt = slice(t * P, (t + 1) * P)
                            mm = mm3(bank(n % 2, width), hT_hi[:, k, tt], hT_lo[:, k, tt],
                                     wv(w_hi, k, 0, width), wv(w_lo, k, 0, width), k == 0, k == KC - 1)
                            if t == nt - 1 and k in (1, 3, 5):
                                mm.then_inc(used[phase], 1)
                        mm.then_inc(s(f"acc_done{l}"), 1)
                        if l == 0 and n == 1:
                            pe.wait_ge(s("u_read"), 8)
                        if n >= 1:
                            turn(n - 1)
                        if l == 0 and n == 0:
                            ada_sum(pe, beside_proj, 3)
                        if l == 0 and n == 2:
                            ada_turn(pe, 2, 4)
                        n += 1
                    pe.drain().then_inc(used[phase], 1)
                m += 4
            turn(n - 1)
            if l == 0:
                for f in range(4):
                    pe.wait_ge(s("pool_d"), 2 * f + 2)
                    if f >= 2:
                        pe.wait_ge(s("pool_out"), 4 * (f - 1))
                    for v, (c0, w) in enumerate(STREAMS):
                        p0 = PADDED[v][0]
                        mm = mm3(bank(4 + 2 * (f % 2), 1024)[:, c0:c0 + w], pw_hi[:, f, :], pw_lo[:, f, :],
                                 d_hi[:, p0:p0 + w], d_lo[:, p0:p0 + w], True, True)
                    mm.then_inc(s("pool_mm"), 1)
            close(pe, "pe")

        def proj_prefetch(l):
            def act_part(act, units):
                for m in units:
                    if m < 4:
                        split_hi(act, f"proj{l}", m, unit_width(l, m), free=False)

            def pool_part(pool):
                for m in range(4):
                    split_lo(pool, f"proj{l}", m, unit_width(l, m))
            return act_part, pool_part

        def proj_scalar(act, l, before):
            phase = f"proj{l}"
            base, tb = rope_plan(l)
            tiles = token_tiles(l)
            q_t = (q0T[:, :, :], qT[:, :].rearrange("p (h n) -> p h n", h=C_HEADS))[l]
            k_t = (k0T, kT)[l]
            vh = (v0_hi, v_hi)[l]
            kvh = (B_KV, C_KV)[l]

            def read_turned(n):
                _, kind, t, heads, h0 = tiles[n]
                for b in range(tb[n + 1] - tb[n]):
                    nb = tb[n] + b
                    act.wait_ge(s(f"qk_turned{l}"), nb + 1)
                    src = bank(2 + nb % 2).rearrange("p (i n) -> p i n", i=4)
                    tt = slice(t * P, (t + 1) * P)
                    if kind == "q":
                        dst = q_t[:, h0 + 4 * b:h0 + 4 * b + 4, tt]
                    else:
                        src = bank(2 + nb % 2).rearrange("p (j a n) -> p j a n", j=2, a=2)
                        dst = k_t[:, :, 2 * b:2 * b + 2, tt].rearrange("p a j n -> p j a n")
                    nc.scalar.activation(dst, src, ACT.Copy).then_inc(s(f"turned_read{l}"), 1)

            after_phase(act, before)
            m, n = 4, 0
            for gi, (kind, _, width, nt, _) in enumerate(PROJ[l]):
                if kind == "pool":
                    for f in range(4):
                        act.wait_ge(s("u_done"), f + 1)
                        act.wait_ge(s("u_zeroed"), 1)
                        for v, (c0, w) in enumerate(STREAMS):
                            p0 = PADDED[v][0]
                            nc.scalar.activation(ubuf[:, f, p0:p0 + w], bank(2 * (f % 2), 1024)[:, c0:c0 + w],
                                                 ACT.Copy).then_inc(s("u_read"), 1)
                else:
                    for t in range(nt):
                        act.wait_ge(s(f"acc_done{l}"), n + 1)
                        heads = tiles[n][3]
                        if l:
                            if n:
                                act.wait_ge(s(f"qk_steps{l}"), base[n - 1] + 1 + (tiles[n - 1][1] == "kv"))
                            nc.scalar.activation(sq[:, 0:heads * HD], bank(n % 2, heads * HD),
                                                 ACT.Square).then_inc(s("qk_sq"), 1)
                        if kind == "kv":
                            nc.scalar.activation(vh[:, t, 0:kvh * HD], bank(n % 2)[:, heads * HD:2 * heads * HD],
                                                 ACT.Copy).then_inc(s(f"v_hi{l}"), 1)
                        if n:
                            read_turned(n - 1)
                        if kind == "kv":
                            act.wait_ge(s(f"qk_steps{l}"), base[n + 1])
                            kk = qks[:, 0:heads * 4 * HD].rearrange("p (i d n) -> p i d n", d=2, n=HD)
                            nc.scalar.activation(kk[:, :, 1, :], kk[:, :, 0, :].bitcast(F32),
                                                 ACT.Copy).then_inc(s(f"k_dup{l}"), 1)
                        n += 1
                if gi < 2:
                    for i in range(4):
                        split_hi(act, phase, m, unit_width(l, m))
                        m += 1
            read_turned(n - 1)
            if l == 0:
                for f in range(4):
                    act.wait_ge(s("pool_mm"), f + 1)
                    for v, (c0, w) in enumerate(STREAMS):
                        nc.scalar.activation(hT_hi[:, f, c0:c0 + w], bank(4 + 2 * (f % 2), 1024)[:, c0:c0 + w],
                                             ACT.Copy, scale=cols[:, 48 + f:49 + f]).then_inc(s("pool_hi"), 1)
            close(act, "act")

        DIFFERENCE_AFTER = (0, 2, 7, 9)

        def window_sums(pool, windows):
            for f in windows:
                pool.wait_ge(s("u_read"), 2 * f + 2)
                src, reach = ubuf[:, f, :], 1
                for step in range(f + 1):
                    h = max(1, 2 ** step // 2)
                    dst = sums[:, step % 2, :]
                    lo, hi = reach, UBUF - reach
                    if step == 0:
                        a, b = src[:, lo - 1:hi - 1], src[:, lo:hi]
                    else:
                        a, b = src[:, lo - h:hi - h], src[:, lo + h:hi + h]
                    if step:
                        pool.wait_ge(s("win_sum"), f * (f + 1) // 2 + step)
                    elif f:
                        pool.wait_ge(s("pool_d32"), 3 * f)
                    nc.gpsimd.tensor_tensor(dst[:, lo:hi], a, b, ALU.add).then_inc(s("win_sum"), 1)
                    src = dst
                    reach += max(1, 2 ** step)

        def proj_pool(pool, l, before):
            phase = f"proj{l}"
            after_phase(pool, before)
            m, n = 4, 0
            tiles = token_tiles(l)
            base, _ = rope_plan(l)
            for gi, (kind, _, width, nt, _) in enumerate(PROJ[l]):
                if kind == "pool":
                    nc.gpsimd.memset(ubuf[:, :, :], 0.0).then_inc(s("u_zeroed"), 1)
                    for i in range(4):
                        split_lo(pool, phase, m, unit_width(l, m))
                        m += 1
                    window_sums(pool, (0, 1))
                elif l:
                    for t in range(nt):
                        pool.wait_ge(s(f"qk_steps{l}"), base[n] + 1 + (kind == "kv"))
                        heads = tiles[n][3]
                        nc.gpsimd.tensor_scalar(qk_ms[:, 0:heads], qk_ss[:, 0:heads], 1.0 / HD, EPS, ALU.mult,
                                                ALU.add).then_inc(s("qk_rms"), 1)
                        pool.wait_ge(s("qk_rms"), 2 * n + 1)
                        nc.gpsimd.tensor_tensor(qk_r[:, 0:heads], qk_ms[:, 0:heads], minus_half[:, 0:heads],
                                                ALU.pow).then_inc(s("qk_rms"), 1)
                        n += 1
                if kind != "pool" and gi < 2:
                    for i in range(4):
                        split_lo(pool, phase, m, unit_width(l, m))
                        m += 1
            if l == 0:
                window_sums(pool, (2, 3))
            close(pool, "pool")

        def proj_vector(dve, l, before):
            base, _ = rope_plan(l)
            tiles = token_tiles(l)
            vh, vl = ((v0_hi, v0_lo), (v_hi, v_lo))[l]
            steps = s(f"qk_steps{l}")
            after_phase(dve, before)
            if l:
                dve.wait_ge(s("gain_landed"), 2 * 16)
                nc.vector.tensor_scalar(qk_gain[:, 0, :], qk_gain[:, 0, :], SCALE, None, ALU.mult).then_inc(s("qk_tab"), 1)
                dve.wait_ge(s("qk_tab"), 1)
                for i in range(4):
                    nc.vector.tensor_tensor(qk_tab[:, i, :, :], rope[:, i % 2, :, :],
                                            qk_gain[:, i // 2, :].unsqueeze(1).broadcast_to([P, ALL_T, HD]),
                                            ALU.mult).then_inc(s("qk_tab"), 1)
                dve.wait_ge(s("qk_tab"), 5)
            else:
                ada_macs(dve, beside_proj, (2, 3))
            for n, (gi, kind, t, heads, h0) in enumerate(tiles):
                W = heads * HD
                src = bank(n % 2, W).rearrange("p (h d) -> p h d", d=HD)
                at = base[n]
                if n:
                    dve.wait_ge(steps, at)
                if kind == "kv":
                    dve.wait_ge(s(f"v_hi{l}"), n + 1)
                    nc.vector.tensor_tensor(vl[:, t, 0:W], bank(n % 2)[:, W:2 * W],
                                            vh[:, t, 0:W].bitcast(F32), ALU.subtract).then_inc(steps, 1)
                    at += 1
                else:
                    dve.wait_ge(s(f"acc_done{l}"), n + 1)
                if l:
                    dve.wait_ge(s("qk_sq"), n + 1)
                    nc.vector.reduce_sum(qk_ss[:, 0:heads], sq[:, 0:W].rearrange("p (h d) -> p h d", d=HD),
                                         AX_X).then_inc(steps, 1)
                    dve.wait_ge(s("qk_rms"), 2 * n + 2)
                    nrm = qkn[:, 0:W].rearrange("p (h d) -> p h d", d=HD)
                    nc.vector.tensor_tensor(nrm, src, qk_r[:, 0:heads].unsqueeze(2).broadcast_to([P, heads, HD]),
                                            ALU.mult).then_inc(steps, 1)
                    at += 2
                    dve.wait_ge(steps, at)
                    src = nrm
                    tab = [qk_tab[:, 2 * (kind == "kv") + i, t, :] for i in range(2)]
                else:
                    tab = [rope[:, i, t, :] for i in range(2)]
                a = qka[:, 0:W].rearrange("p (h d) -> p h d", d=HD)
                b = qkb[:, 0:W].rearrange("p (h d) -> p h d", d=HD)
                for dst, tb_ in zip((a, b), tab):
                    nc.vector.tensor_tensor(dst, src, tb_.unsqueeze(1).broadcast_to([P, heads, HD]),
                                            ALU.mult).then_inc(steps, 1)
                at += 2
                dve.wait_ge(steps, at)
                half = HD // 2
                nc.vector.tensor_tensor(a[:, :, 0:half], a[:, :, 0:half], b[:, :, half:HD],
                                        ALU.subtract).then_inc(steps, 1)
                nc.vector.tensor_tensor(a[:, :, half:HD], a[:, :, half:HD], b[:, :, 0:half],
                                        ALU.add).then_inc(steps, 1)
                at += 2
                dve.wait_ge(steps, at)
                if n:
                    dve.wait_ge(s(f"qk_turned{l}"), rope_plan(l)[1][n])
                if kind == "q":
                    v = qks[:, 0:2 * W].rearrange("p (h a d) -> p h a d", a=2, d=HD)
                    hi, lo = v[:, :, 0, :], v[:, :, 1, :]
                else:
                    v = qks[:, 0:4 * W].rearrange("p (h a c d) -> p h a c d", a=2, c=2, d=HD)
                    hi, lo = v[:, :, 0, 0, :], v[:, :, 1, 0, :]
                nc.vector.tensor_copy(hi, a).then_inc(steps, 1)
                dve.wait_ge(steps, at + 1)
                nc.vector.tensor_tensor(lo, a, hi.bitcast(F32), ALU.subtract).then_inc(steps, 1)
                assert at + 2 == base[n + 1]
                if l == 0 and n == 0:
                    dve.wait_ge(s("ada_sum"), 4)
                    ada_bias(dve, beside_proj, 2, 5, 32, 4, psf[32:36, 4 * BANK:6 * BANK])
                if l == 0 and n == 2:
                    ada_columns(dve, 2, 0, (2, 3), 4)
                    ada_gates(dve, beside_proj, 2, 32, 2)
                if l == 0 and n in DIFFERENCE_AFTER:
                    pool_difference(dve, DIFFERENCE_AFTER.index(n))
            if l == 0:
                for f in range(4):
                    if f:
                        dve.wait_ge(s("pool_mm"), f)
                    dve.wait_ge(s("pool_d32"), 3 * f + 3)
                    nc.vector.tensor_copy(d_hi[:, 0:UBUF], ubuf[:, f, :]).then_inc(s("pool_d"), 1)
                    dve.wait_ge(s("pool_d"), 2 * f + 1)
                    nc.vector.tensor_tensor(d_lo[:, 0:UBUF], ubuf[:, f, :], d_hi[:, 0:UBUF].bitcast(F32),
                                            ALU.subtract).then_inc(s("pool_d"), 1)
                    if f:
                        pool_lo(dve, f - 1)
                pool_lo(dve, 3)
            close(dve, "dve")

        def pool_difference(dve, f):
            acc = sums[:, f % 2, :]
            dve.wait_ge(s("win_sum"), (f + 1) * (f + 2) // 2)
            for v, (p0, w) in enumerate(PADDED):
                e = acc[:, p0:p0 + w]
                ends = e.rearrange("p (a n) -> p a n", n=PAD)[:, 0:w // PAD:w // PAD - 1, :]
                nc.vector.tensor_tensor(ends, ends, edge[:, f, :, :], ALU.mult).then_inc(s("pool_d32"), 1)
            dve.wait_ge(s("pool_d32"), 3 * f + 2)
            lo = PADDED[0][0]
            nc.vector.scalar_tensor_tensor(out=ubuf[:, f, lo:UBUF - PAD], in0=acc[:, lo:UBUF - PAD],
                                           scalar=1.0 / POOL_WINDOWS[f], in1=ubuf[:, f, lo:UBUF - PAD],
                                           op0=ALU.mult, op1=ALU.subtract).then_inc(s("pool_d32"), 1)

        def pool_lo(dve, f):
            dve.wait_ge(s("pool_hi"), 2 * f + 2)
            for c0, w in STREAMS:
                nc.vector.scalar_tensor_tensor(out=hT_lo[:, f, c0:c0 + w], in0=bank(4 + 2 * (f % 2), 1024)[:, c0:c0 + w],
                                               scalar=cols[:, 48 + f:49 + f], in1=hT_hi[:, f, c0:c0 + w].bitcast(F32),
                                               op0=ALU.mult, op1=ALU.subtract).then_inc(s("pool_out"), 2)

        def attn_setup(l):
            groups = attention_groups(l)
            first = [0]
            for g in groups:
                first.append(first[-1] + len(g[2]))
            return groups, attention_steps(groups), first

        mx, negm, den, rden, esink = (small[:, i, :] for i in range(5))

        def attn_tensor(pe, l, before):
            groups, steps, first = attn_setup(l)
            q_t = (q0T[:, :, :], qT[:, :].rearrange("p (h n) -> p h n", h=C_HEADS))[l]
            k_t = (k0T, kT)[l]
            vh, vl = ((v0_hi, v0_lo), (v_hi, v_lo))[l]
            per = 2 if l == 0 else 1
            after_phase(pe, before)
            for kind, g, i in steps:
                j, n, keys, masks = groups[g]
                if kind == "S":
                    h = 4 * g + i
                    if h >= 2:
                        pe.wait_ge(s(f"exp_done{l}"), per * (h - 2) + 1)
                    sc = bank(2 * (h % 2), 1024)
                    lhs = q_t[:, GROUP * j + i, n * P:(n + 1) * P]
                    pieces = key_pieces(keys)
                    for part in range(2):
                        for p0, k0, w in pieces:
                            mm = nc.tensor.matmul(sc[:, p0:p0 + w], lhs, k_t[:, part, j, k0:k0 + w],
                                                  start=part == 0 and p0 % BANK == 0, stop=part == 1,
                                                  skip_group_check=True)
                    for c, t in enumerate(keys):
                        if t in masks:
                            mm = nc.tensor.matmul(sc[:, c * P:(c + 1) * P], ident_b[:, :], mask_b[:, masks[t], :],
                                                  start=False, stop=True, skip_group_check=True)
                    mm.then_inc(s(f"scores{l}"), 1)
                elif kind == "T":
                    cg = first[g] + i
                    pe.wait_ge(s(f"prob_norm{l}"), 4 * g + 4)
                    if cg >= 2:
                        pe.wait_ge(s(f"pT_lo{l}"), cg - 1)
                    for h in range(GROUP):
                        mm = nc.tensor.transpose(bank(4 + cg % 2)[:, h * P:(h + 1) * P],
                                                 prob[:, g % 2, h, i * P:(i + 1) * P], ident[:, :])
                    mm.then_inc(s(f"prob_turned{l}"), 1)
                elif kind == "V":
                    cg = first[g] + i
                    pe.wait_ge(s(f"pT_lo{l}"), cg + 1)
                    if i == 0 and g >= 2:
                        pe.wait_ge(s(f"o_read{l}"), 2 * (g - 1))
                    vt = (slice(None), keys[i], slice(j * HD, (j + 1) * HD))
                    mm = mm3(ps[0:HD, 6 + g % 2, :], vh[vt], vl[vt], pT_hi[:, cg % 2, :], pT_lo[:, cg % 2, :],
                             i == 0, i == len(keys) - 1)
                    mm.then_inc(s(f"pv{l}"), 1)
            close(pe, "pe")

        def attn_scalar(act, l, before):
            groups, steps, first = attn_setup(l)
            after_phase(act, before)
            per = 3 if l == 0 else 2
            for kind, g, i in steps:
                j, n, keys, masks = groups[g]
                h = 4 * g + i
                if kind == "E":
                    act.wait_ge(s(f"smax{l}"), h + 1)
                    W = len(keys) * P
                    nc.scalar.activation(prob[:, g % 2, i, 0:W], bank(2 * (h % 2), 1024)[:, 0:W], ACT.Exp,
                                         bias=negm[:, h:h + 1], scale=SCALE if l == 0 else 1.0,
                                         accum_out=den[:, h:h + 1]).then_inc(s(f"exp_done{l}"), 1)
                    if l == 0:
                        nc.scalar.activation(esink[:, h:h + 1], nsink[:, GROUP * j + i:GROUP * j + i + 1], ACT.Exp,
                                             bias=negm[:, h:h + 1], scale=-1.0).then_inc(s(f"exp_done{l}"), 1)
                elif kind == "T":
                    cg = first[g] + i
                    act.wait_ge(s(f"prob_turned{l}"), cg + 1)
                    if cg >= 2:
                        act.wait_ge(s(f"pv{l}"), cg - 1)
                    nc.scalar.activation(pT_hi[:, cg % 2, :], bank(4 + cg % 2), ACT.Copy).then_inc(s(f"pT_hi{l}"), 1)
                elif kind == "O":
                    act.wait_ge(s(f"pv{l}"), first[g + 1])
                    if g >= 2:
                        act.wait_ge(s(f"o_split{l}"), 2 * (g - 1))
                    src = ps[0:HD, 6 + g % 2, :].rearrange("p (a b n) -> p a b n", a=2, b=2)
                    for odd in range(2):
                        nc.scalar.activation(o_tmp[64 * odd:64 * odd + 64, g % 2, :, :], src[:, :, odd, :],
                                             ACT.Copy).then_inc(s(f"o_read{l}"), 1)
            close(act, "act")

        def attn_vector(dve, l, before):
            groups, steps, first = attn_setup(l)
            c_first = 4 if l == 0 else 0
            after_phase(dve, before)
            nden = 2 if l == 0 else 1

            def denominator(h):
                dve.wait_ge(s(f"exp_done{l}"), nden * h + nden)
                d = den
                if l == 0:
                    nc.vector.tensor_tensor(rden[:, h:h + 1], den[:, h:h + 1], esink[:, h:h + 1],
                                            ALU.add).then_inc(s(f"rden{l}"), 1)
                    dve.wait_ge(s(f"rden{l}"), 2 * h + 1)
                    d = rden
                nc.vector.reciprocal(rden[:, h:h + 1], d[:, h:h + 1]).then_inc(s(f"rden{l}"), 1)

            for kind, g, i in steps:
                j, n, keys, masks = groups[g]
                h = 4 * g + i
                if kind == "S":
                    dve.wait_ge(s(f"scores{l}"), h + 1)
                    sc = bank(2 * (h % 2), 1024)[:, 0:len(keys) * P]
                    if l == 0:
                        nc.vector.reduce_max(mx[:, h:h + 1], sc, AX_X).then_inc(s("smax_raw"), 1)
                        dve.wait_ge(s("smax_raw"), h + 1)
                        nc.vector.scalar_tensor_tensor(out=negm[:, h:h + 1], in0=mx[:, h:h + 1], scalar=-SCALE,
                                                       in1=nsink[:, GROUP * j + i:GROUP * j + i + 1],
                                                       op0=ALU.mult, op1=ALU.min).then_inc(s("smax0"), 1)
                    else:
                        nc.vector.tensor_reduce(negm[:, h:h + 1], sc, AX_X, ALU.max, negate=True).then_inc(s("smax1"), 1)
                elif kind == "D":
                    denominator(h)
                elif kind == "T":
                    cg = first[g] + i
                    dve.wait_ge(s(f"pT_hi{l}"), cg + 1)
                    nc.vector.tensor_tensor(pT_lo[:, cg % 2, :], bank(4 + cg % 2), pT_hi[:, cg % 2, :].bitcast(F32),
                                            ALU.subtract).then_inc(s(f"pT_lo{l}"), 1)
                elif kind == "O":
                    dve.wait_ge(s(f"o_read{l}"), 2 * g + 2)
                    cc = slice(c_first + 2 * j, c_first + 2 * j + 2)
                    tt = slice(n * P, (n + 1) * P)
                    nc.vector.tensor_copy(hT_hi[:, cc, tt], o_tmp[:, g % 2, :, :]).then_inc(s(f"o_split{l}"), 1)
                    dve.wait_ge(s(f"o_split{l}"), 2 * g + 1)
                    nc.vector.tensor_tensor(hT_lo[:, cc, tt], o_tmp[:, g % 2, :, :], hT_hi[:, cc, tt].bitcast(F32),
                                            ALU.subtract).then_inc(s(f"o_split{l}"), 1)
            close(dve, "dve")

        def attn_pool(pool, l, before):
            groups, steps, first = attn_setup(l)
            after_phase(pool, before)
            per = 2 if l == 0 else 1
            for g, (j, n, keys, masks) in enumerate(groups):
                for i in range(GROUP):
                    h = 4 * g + i
                    pool.wait_ge(s(f"rden{l}"), per * (h + 1))
                    pr = prob[:, g % 2, i, 0:len(keys) * P]
                    nc.gpsimd.tensor_scalar(pr, pr, rden[:, h:h + 1], 1.0, ALU.mult,
                                            ALU.mult).then_inc(s(f"prob_norm{l}"), 1)
            close(pool, "pool")

        def gate_tensor(pe, l, tag, sub, nv):
            for i in range(2 * nv):
                v, half = divmod(i, 2)
                row = ada_row(l, (2, 5)[sub], v)
                if i >= 2:
                    pe.wait_ge(s(f"{tag}_gate"), i - 1)
                nc.tensor.matmul(bank(6 + i % 2), ident[:, row:row + 1].broadcast_to([P, P]),
                                 gate_rows[:, half * BANK:(half + 1) * BANK],
                                 start=True, stop=True, skip_group_check=True).then_inc(s(f"{tag}_gate_mm"), 1)

        def gate_scalar(act, tag, nv):
            for i in range(2 * nv):
                v, half = divmod(i, 2)
                act.wait_ge(s(f"{tag}_gate_mm"), i + 1)
                nc.scalar.activation(gate[:, v, half * BANK:(half + 1) * BANK], bank(6 + i % 2),
                                     ACT.Copy).then_inc(s(f"{tag}_gate"), 1)

        def first_half_scalar(act, tag, t, acc, y0_, sqj_):
            nc.scalar.activation(y0_[:, t, :], acc, ACT.Copy).then_inc(s(f"{tag}_y0"), 1)

        def square_scalar(act, tag, half, t, nt, src, sqj_):
            i = half * nt + t
            if i >= 2:
                act.wait_ge(s(f"{tag}_ysq"), i - 1)
            nc.scalar.activation(sqj_[:, i % 2, :], src, ACT.Square,
                                 accum_out=ssum[:, half, t:t + 1]).then_inc(s(f"{tag}_ysq"), 1)

        def post_pool(pool, tag, nt, then):
            for t in range(nt):
                pool.wait_ge(s(f"{tag}_ysq"), nt + t + 1)
                nc.gpsimd.tensor_tensor(ssum[:, 0, t:t + 1], ssum[:, 0, t:t + 1], ssum[:, 1, t:t + 1],
                                        ALU.add).then_inc(s(f"{tag}_yr"), 1)
                pool.wait_ge(s(f"{tag}_yr"), 3 * t + 1)
                nc.gpsimd.tensor_scalar(ssum[:, 0, t:t + 1], ssum[:, 0, t:t + 1], 1.0 / D, EPS, ALU.mult,
                                        ALU.add).then_inc(s(f"{tag}_yr"), 1)
                pool.wait_ge(s(f"{tag}_yr"), 3 * t + 2)
                nc.gpsimd.tensor_tensor(rms[:, t:t + 1], ssum[:, 0, t:t + 1], minus_half[:, 0:1],
                                        ALU.pow).then_inc(s(f"{tag}_yr"), 1)
                if then and t:
                    x_rms(pool, then, t - 1)
            if then:
                x_rms(pool, then, nt - 1)

        def post_vector(dve, tag, nt, acc_of, y0_, t0_, t1_, then):
            dve.wait_ge(s(f"{tag}_gate"), 2 * (2 if nt == ALL_T else 1))
            for t in range(nt):
                v = int(t >= LAT_T)
                dve.wait_ge(s(f"{tag}_yr"), 3 * t + 3)
                if t:
                    dve.wait_ge(s(f"{tag}_post"), 4 * t)
                nc.vector.scalar_tensor_tensor(out=t1_[:, :], in0=acc_of(t), scalar=rms[:, t:t + 1],
                                               in1=gate[:, v, BANK:D], op0=ALU.mult, op1=ALU.mult).then_inc(s(f"{tag}_post"), 1)
                nc.vector.scalar_tensor_tensor(out=t0_[:, :], in0=y0_[:, t, :], scalar=rms[:, t:t + 1],
                                               in1=gate[:, v, 0:BANK], op0=ALU.mult, op1=ALU.mult).then_inc(s(f"{tag}_post"), 1)
                for half, tt in ((1, t1_), (0, t0_)):
                    dve.wait_ge(s(f"{tag}_post"), 4 * t + 2 - half)
                    xv = x[:, t, half * BANK:(half + 1) * BANK]
                    nc.vector.tensor_tensor(xv, xv, tt[:, :], ALU.add).then_inc(s(f"{tag}_post"), 1)
                if then and t:
                    x_normed(dve, then, t - 1)
            if then:
                x_normed(dve, then, nt - 1)

        def out_prefetch_scalar(act, l):
            for m in range(4):
                split_hi(act, f"out{l}", m, 1024, free=False)

        def out_sync(sp, l):
            w = (ab_w_out, c_w_out)[l][0]
            n = 4 * KC
            for m in range(8):
                half, u = divmod(m, 4)
                load_unit(sp, f"out{l}", m, w[2 * u * P:(2 * u + 2) * P, half * BANK:(half + 1) * BANK]
                          .rearrange("(k p) n -> p k n", p=P), 1024)
                if l == 0 and 2 <= m < 7:
                    if m == 2:
                        after_phase(sp, 5)
                    more = 2 if m < 6 else 8
                    ada_loads(sp, beside_out, n, n + more)
                    n += more
                    if m == 2:
                        ada_small_loads(sp, beside_out, 0, (4, 5))

        def out_tensor(pe, l, before, nt):
            phase, tag = f"out{l}", f"mixpost{l}"
            after_phase(pe, before)
            gate_tensor(pe, l, tag, 0, 2 if nt == ALL_T else 1)
            for half in range(2):
                for t in range(nt):
                    n = half * nt + t
                    if n >= 4:
                        if n - 4 < nt:
                            pe.wait_ge(s(f"{tag}_y0"), n - 3)
                        else:
                            pe.wait_ge(s(f"{tag}_post"), 4 * (n - 4 - nt) + 1)
                    for k in range(KC):
                        m = 4 * half + k // 2
                        if t == 0 and k % 2 == 0:
                            wait_split(pe, phase, m)
                        slot, c0 = unit_slot(phase, m), (k % 2) * BANK
                        tt = slice(t * P, (t + 1) * P)
                        mm = mm3(bank(n % 4), hT_hi[:, k, tt], hT_lo[:, k, tt], w_hi[:, slot, c0:c0 + BANK],
                                 w_lo[:, slot, c0:c0 + BANK], k == 0, k == KC - 1)
                        if t == nt - 1 and k in (1, 3, 5):
                            mm.then_inc(used[phase], 1)
                    mm.then_inc(s(f"{tag}_acc"), 1)
                    if l == 0 and n == 2:
                        ada_sum(pe, beside_out, 4)
                    elif l == 0 and n == 4:
                        ada_sum(pe, beside_out, 5)
                    elif l == 0 and n == 6:
                        ada_turn(pe, 3, 4)
                pe.drain().then_inc(used[phase], 1)
            close(pe, "pe")

        def out_scalar(act, l, before, nt):
            phase, tag = f"out{l}", f"mixpost{l}"
            after_phase(act, before)
            out_prefetch_scalar(act, l)
            gate_scalar(act, tag, 2 if nt == ALL_T else 1)
            for t in range(nt):
                act.wait_ge(s(f"{tag}_acc"), t + 1)
                first_half_scalar(act, tag, t, bank(t % 4), y0, sqj)
                act.wait_ge(s(f"{tag}_y0"), t + 1)
                square_scalar(act, tag, 0, t, nt, y0[:, t, :], sqj)
            for m in range(4, 8):
                split_hi(act, phase, m, 1024)
            for t in range(nt):
                act.wait_ge(s(f"{tag}_acc"), nt + t + 1)
                square_scalar(act, tag, 1, t, nt, bank((nt + t) % 4), sqj)
                if t:
                    x_square(act, f"ffn{l}", tag, t - 1)
            x_square(act, f"ffn{l}", tag, nt - 1)
            close(act, "act")

        def out_pool(pool, l, before, nt):
            after_phase(pool, before)
            for m in range(8):
                split_lo(pool, f"out{l}", m, 1024)
            post_pool(pool, f"mixpost{l}", nt, f"ffn{l}")
            close(pool, "pool")

        def out_vector(dve, l, before, nt):
            after_phase(dve, before)
            if l == 0:
                ada_macs(dve, beside_out, (4, 5))
                dve.wait_ge(s("ada_sum"), 6)
                dve.wait_ge(s("mixpost0_gate_mm"), 4)
                ada_bias(dve, beside_out, 3, 8, 64, 4, psf[64:68, 4 * BANK:6 * BANK])
                ada_columns(dve, 3, 0, (4, 5), 4)
                ada_gates(dve, beside_out, 3, 64, 4)
            post_vector(dve, f"mixpost{l}", nt, lambda t: bank((nt + t) % 4), y0, t0, t1, f"ffn{l}")
            close(dve, "dve")

        TURN = 6
        TURNS = 2 * FT // TURN

        def up_sync(sp, l):
            def turn(i, with_ada):
                for m in range(TURN):
                    c0 = (m // 2) * P + (m % 2) * DFF
                    src = ffn_w_up[l][:, bass.ds(i * (3 * P) + c0, P)].rearrange("(k p) n -> p k n", p=P)
                    load_unit(sp, f"up{l}", m, src, 1024, i, TURN)
                    if with_ada and m >= 2:
                        if m == 2:
                            after_phase(sp, 6)
                        for k in (2 * m - 4, 2 * m - 3):
                            ada_load(sp, 6 * KC + k, beside_up, 1, slice(k * P, (k + 1) * P), bass.ds(i * D, D), i)

            with sp.Fori(0, TURNS - 1) as i:
                turn(i, l == 0)
            turn(TURNS - 1, False)

        def up_prefetch(l):
            def act_part(act, units):
                for m in units:
                    if m < 3:
                        split_hi(act, f"up{l}", m, 1024, free=False)

            def pool_part(pool):
                for m in range(3):
                    split_lo(pool, f"up{l}", m, 1024)
            return act_part, pool_part

        def up_tensor(pe, l, before, nt, tag):
            phase = f"up{l}"
            streams = STREAMS[:1 if nt == LAT_T else 2]
            pe.wait_ge(closed["act"], before)
            pe.wait_ge(s(f"{tag}_split"), 2 * KC)
            if l == 0:
                for half in range(2):
                    nc.tensor.matmul(ps[96:128, 6 + half, :], select[:, 0:32],
                                     rope[:, :, :, :].rearrange("p a t n -> p (a t n)")[:, 0:BANK],
                                     start=True, stop=True, skip_group_check=True)

            def turn(i, with_ada):
                for m in range(TURN):
                    wait_split(pe, phase, m, i, TURN)
                    pe.wait_ge(s(f"taps{l}"), i * TURN + (m + 1))
                    slot = unit_slot(phase, m)
                    acc = bank(2 * (m % 3), 1024)
                    for k in range(KC):
                        kk = slice(k * P, (k + 1) * P)
                        for c0, w in streams:
                            mm = mm3(acc[:, c0:c0 + w], w_hi[:, slot, kk], w_lo[:, slot, kk],
                                     hT_hi[:, k, c0:c0 + w], hT_lo[:, k, c0:c0 + w], k == 0, k == KC - 1)
                    mm.then_inc(used[phase], 1)
                if with_ada:
                    pe.wait_ge(s("ada_mac"), i * (2 * KC) + 14 * KC)
                    pe.wait_ge(s("ada_selector"), i * 2 + 2)
                    for v in range(2):
                        for half in range(2):
                            mm = nc.tensor.matmul(ps[96:128, 6 + half, :], select_v[:, v, :],
                                                  beside_up[0][:, v, half * BANK:(half + 1) * BANK],
                                                  start=False, stop=True, skip_group_check=True)
                    mm.then_inc(s("ada_sum"), 1)

            with pe.Fori(0, TURNS - 1) as i:
                turn(i, l == 0)
            turn(TURNS - 1, False)
            close(pe, "pe")

        def up_scalar(act, l, before, nt):
            phase = f"up{l}"
            T = nt * P
            after_phase(act, before)
            act.sem_inc(s(f"gated{l}"), 1)
            act.sem_inc(s(f"gelu{l}"), 1)

            def turn(i, last):
                for m in range(TURN):
                    b = m % 2
                    col = i * 3 + (m // 2 + b * FT)
                    act.wait_ge(used[phase], i * TURN + (m + 1))
                    act.wait_ge(s(f"gated{l}") if b else s(f"gelu{l}"), i * 3 + (m // 2 + 1))
                    nc.scalar.activation((conv_a, conv_b)[b][:, 0:T], bank(2 * (m % 3), 1024)[:, 0:T], ACT.Identity,
                                         bias=convb[:, l, bass.ds(col, 1)],
                                         scale=convw[l][:, 1, bass.ds(col, 1)]).then_inc(s(f"center{l}"), 1)
                    if not (last and m >= TURN - 3):
                        split_hi(act, phase, m + 3, 1024, i, TURN)
                    if not b:
                        act.wait_ge(s(f"taps{l}"), i * TURN + (m + 4))
                        act.wait_ge(s(f"gated{l}"), i * 3 + (m // 2 + 1))
                        nc.scalar.activation(gelu[:, 0:T], conv_a[:, 0:T], ACT.Gelu_apprx_tanh).then_inc(s(f"gelu{l}"), 1)

            with act.Fori(0, TURNS - 1) as i:
                turn(i, False)
            turn(TURNS - 1, True)
            close(act, "act")

        def up_pool(pool, l, before):
            after_phase(pool, before)
            with pool.Fori(0, TURNS - 1) as i:
                for m in range(3, 3 + TURN):
                    split_lo(pool, f"up{l}", m, 1024, i, TURN)
            for m in range(3, TURN):
                split_lo(pool, f"up{l}", m + TURN * (TURNS - 1), 1024)
            close(pool, "pool")

        def up_vector(dve, l, before, nt):
            streams = STREAMS[:1 if nt == LAT_T else 2]
            T = nt * P
            ns = len(streams)
            after_phase(dve, before)
            dve.sem_inc(s(f"taps{l}"), 3)

            def turn(i, with_ada):
                if with_ada:
                    dve.wait_ge(s("ada_sum"), i + 6)
                    for v in range(2):
                        nc.vector.tensor_copy(select_v[:, v, :], select[:, bass.ds(i * 2 + (22 - v), 32)]
                                              ).then_inc(s("ada_selector"), 1)
                for m in range(TURN):
                    b = m % 2
                    col = i * 3 + (m // 2 + b * FT)
                    dve.wait_ge(s(f"center{l}"), i * TURN + (m + 1))
                    cv = (conv_a, conv_b)[b]
                    acc = bank(2 * (m % 3), 1024)
                    for c0, w in streams:
                        nc.vector.scalar_tensor_tensor(out=cv[:, c0 + 1:c0 + w], in0=acc[:, c0:c0 + w - 1],
                                                       scalar=convw[l][:, 0, bass.ds(col, 1)], in1=cv[:, c0 + 1:c0 + w],
                                                       op0=ALU.mult, op1=ALU.add).then_inc(s(f"tap0_{l}"), 1)
                    for v, (c0, w) in enumerate(streams):
                        dve.wait_ge(s(f"tap0_{l}"), i * (TURN * ns) + (m * ns + v + 1))
                        op = nc.vector.scalar_tensor_tensor(out=cv[:, c0:c0 + w - 1], in0=acc[:, c0 + 1:c0 + w],
                                                            scalar=convw[l][:, 2, bass.ds(col, 1)], in1=cv[:, c0:c0 + w - 1],
                                                            op0=ALU.mult, op1=ALU.add)
                        if v == ns - 1:
                            op.then_inc(s(f"taps{l}"), 1)
                    if b:
                        dve.wait_ge(s(f"taps{l}"), i * TURN + (m + 4))
                        dve.wait_ge(s(f"gelu{l}"), i * 3 + (m // 2 + 2))
                        nc.vector.tensor_tensor(act_g[:, bass.ds(i * 3 + m // 2, 1), 0:T].rearrange("p a n -> p (a n)"),
                                                gelu[:, 0:T], conv_b[:, 0:T], ALU.mult).then_inc(s(f"gated{l}"), 1)
                    if with_ada and m < 4:
                        for k in (2 * m, 2 * m + 1):
                            ada_mac(dve, beside_up, 6 * KC + k, k, i)

            with dve.Fori(0, TURNS - 1) as i:
                turn(i, l == 0)
            turn(TURNS - 1, False)
            if l == 0:
                dve.wait_ge(s("ada_sum"), 12)
                nc.vector.tensor_copy(gate_rows[96:128, :], psf[96:128, 6 * BANK:8 * BANK]).then_inc(s("ada_raw"), 1)
            close(dve, "dve")

        DTURNS = FT // 3

        def down_sync(sp, l):
            for half in range(2):
                if l == 0 and half:
                    after_phase(sp, 8)
                    ada_small_loads(sp, beside_up, 1, range(6))
                with sp.Fori(0, DTURNS) as i:
                    for m in range(3):
                        src = ffn_w_down[l][bass.ds(i * (3 * P) + m * P, P), half * BANK:(half + 1) * BANK]
                        load_unit(sp, f"down{l}", half * FT + m, src, BANK, i, 3)

        def down_tensor(pe, l, before, nt):
            phase, tag = f"down{l}", f"ffnpost{l}"
            after_phase(pe, before)
            gate_tensor(pe, l, tag, 1, 2 if nt == ALL_T else 1)

            def unit(i, m, half, first, last, tiles):
                slot = unit_slot(phase, m)
                for t in tiles:
                    if half and first:
                        pe.wait_ge(s(f"{tag}_y0"), t + 1)
                    tt = slice(t * P, (t + 1) * P)
                    mm = mm3(bank(t), g_hi[:, slot, tt], g_lo[:, slot, tt], w_hi[:, slot, 0:BANK],
                             w_lo[:, slot, 0:BANK], first, last)
                return mm

            def ready(i, m, half):
                wait_split(pe, phase, half * FT + m, i, 3)
                pe.wait_ge(s(f"g_lo{l}"), i * 3 + (half * FT + m + 1))

            for half in range(2):
                for m in range(3):
                    ready(0, m, half)
                    unit(0, m, half, m == 0, False, range(nt)).then_inc(used[phase], 1)
                with pe.Fori(1, DTURNS - 1) as i:
                    for m in range(3):
                        ready(i, m, half)
                        unit(i, m, half, False, False, range(nt)).then_inc(used[phase], 1)
                for m in range(3):
                    ready(DTURNS - 1, m, half)
                for t in range(nt):
                    for m in range(3):
                        mm = unit(DTURNS - 1, m, half, False, m == 2, (t,))
                    mm.then_inc(s(f"{tag}_acc"), 1)
                pe.drain().then_inc(used[phase], 3)
                if l == 0 and half == 0:
                    pe.wait_ge(s(f"{tag}_gate"), 4)
                    ada_turn(pe, 4, 6)
            close(pe, "pe")

        def down_split(act, l, nt, half, m, i=0, first=False):
            phase = f"down{l}"
            T = nt * P
            split_hi(act, phase, half * FT + m, BANK, i, 3, free=not (first and half == 0))
            nc.scalar.activation(g_hi[:, m, 0:T], act_g[:, bass.ds(i * 3 + m, 1), 0:T].rearrange("p a n -> p (a n)"),
                                 ACT.Copy).then_inc(s(f"g_hi{l}"), 1)

        def down_scalar(act, l, before, nt):
            tag = f"ffnpost{l}"
            after_phase(act, before)
            for half in range(2):
                if half == 0:
                    for m in range(3):
                        down_split(act, l, nt, 0, m, 0, True)
                    gate_scalar(act, tag, 2 if nt == ALL_T else 1)
                with act.Fori(1, DTURNS) as i:
                    for m in range(3):
                        down_split(act, l, nt, half, m, i)
                for t in range(nt):
                    act.wait_ge(s(f"{tag}_acc"), half * nt + t + 1)
                    if half == 0:
                        first_half_scalar(act, tag, t, bank(t), y0d, sqjd)
                    else:
                        square_scalar(act, tag, 1, t, nt, bank(t), sqjd)
                        if l == 0 and t:
                            x_square(act, "mix1", tag, t - 1)
                if half == 0:
                    for m in range(3):
                        down_split(act, l, nt, 1, m, 0)
                    for t in range(nt):
                        act.wait_ge(s(f"{tag}_y0"), t + 1)
                        square_scalar(act, tag, 0, t, nt, y0d[:, t, :], sqjd)
            if l == 0:
                x_square(act, "mix1", tag, nt - 1)
            close(act, "act")

        def down_pool(pool, l, before, nt):
            after_phase(pool, before)
            for half in range(2):
                with pool.Fori(0, DTURNS) as i:
                    for m in range(3):
                        split_lo(pool, f"down{l}", half * FT + m, BANK, i, 3)
            post_pool(pool, f"ffnpost{l}", nt, None if l else "mix1")
            close(pool, "pool")

        def down_vector(dve, l, before, nt):
            T = nt * P
            after_phase(dve, before)
            for half in range(2):
                with dve.Fori(0, DTURNS) as i:
                    for m in range(3):
                        dve.wait_ge(s(f"g_hi{l}"), i * 3 + (half * FT + m + 1))
                        nc.vector.tensor_tensor(g_lo[:, m, 0:T],
                                                act_g[:, bass.ds(i * 3 + m, 1), 0:T].rearrange("p a n -> p (a n)"),
                                                g_hi[:, m, 0:T].bitcast(F32), ALU.subtract).then_inc(s(f"g_lo{l}"), 1)
                if l == 0 and half == 0:
                    dve.wait_ge(s("ffnpost0_gate_mm"), 4)
                    ada_bias(dve, beside_up, 4, 16, 96, 12, gate_rows[96:108, :])
            if l == 0:
                ada_columns(dve, 4, 1, range(6), 6)
                ada_gates(dve, beside_up, 4, 96, 12)
            post_vector(dve, f"ffnpost{l}", nt, bank, y0d, t0d, t1d, None if l else "mix1")
            close(dve, "dve")

        block = es.enter_context(nc.Block())
        NT = {0: ALL_T, 1: LAT_T}

        @block.sync
        def _(sp):
            setup_sync(sp)
            ada_loads(sp, beside_out, 0, KC)
            x_sync(sp)
            ada_small_loads(sp, beside_out, 0, (0, 1))
            ada_loads(sp, beside_out, KC, 2 * KC)
            late_sync(sp)
            for l in range(2):
                proj_sync(sp, l)
                out_sync(sp, l)
                up_sync(sp, l)
                down_sync(sp, l)
                if l == 0:
                    for i, g in enumerate((c_q_g, c_k_g)):
                        sp.dma_start(qk_gain[:, i, :], g[0].partition_broadcast(P)).then_inc(s("gain_landed"), 16)
            for t in range(LAT_T):
                sp.wait_ge(s("ffnpost1_post"), 4 * t + 4)
                sp.dma_start(out[0, t * P:(t + 1) * P, :], x[:, t, :]).then_inc(store_done, 16)
            sp.wait_ge(store_done, 16 * LAT_T)

        @block.tensor
        def _(pe):
            setup_tensor(pe)
            after_phase(pe, 1)
            start_tensor(pe)
            for l in range(2):
                b = 7 * l
                norm_tensor(pe, f"mix{l}", b + 2, ALL_T)
                proj_tensor(pe, l, b + 3, f"mix{l}")
                attn_tensor(pe, l, b + 4)
                out_tensor(pe, l, b + 5, NT[l])
                norm_tensor(pe, f"ffn{l}", b + 6, NT[l])
                up_tensor(pe, l, b + 7, NT[l], f"ffn{l}")
                down_tensor(pe, l, b + 8, NT[l])

        @block.scalar
        def _(act):
            setup_scalar(act)
            start_scalar(act)
            for l in range(2):
                b = 7 * l
                norm_scalar(act, f"mix{l}", b + 2, 0, ALL_T, proj_prefetch(l)[0])
                proj_scalar(act, l, b + 3)
                attn_scalar(act, l, b + 4)
                out_scalar(act, l, b + 5, NT[l])
                norm_scalar(act, f"ffn{l}", b + 6, 1, NT[l], up_prefetch(l)[0])
                up_scalar(act, l, b + 7, NT[l])
                down_scalar(act, l, b + 8, NT[l])

        @block.gpsimd
        def _(pool):
            close(pool, "pool")
            start_pool(pool)
            for l in range(2):
                b = 7 * l
                norm_pool(pool, f"mix{l}", b + 2, ALL_T, proj_prefetch(l)[1])
                proj_pool(pool, l, b + 3)
                attn_pool(pool, l, b + 4)
                out_pool(pool, l, b + 5, NT[l])
                norm_pool(pool, f"ffn{l}", b + 6, NT[l], up_prefetch(l)[1])
                up_pool(pool, l, b + 7)
                down_pool(pool, l, b + 8, NT[l])

        @block.vector
        def _(dve):
            setup_vector(dve)
            after_phase(dve, 1)
            start_vector(dve)
            for l in range(2):
                b = 7 * l
                norm_vector(dve, f"mix{l}", b + 2, ALL_T)
                proj_vector(dve, l, b + 3)
                attn_vector(dve, l, b + 4)
                out_vector(dve, l, b + 5, NT[l])
                norm_vector(dve, f"ffn{l}", b + 6, NT[l])
                up_vector(dve, l, b + 7, NT[l])
                down_vector(dve, l, b + 8, NT[l])


def shape_constants():
    import numpy as np

    ident = np.eye(P, dtype=np.float32)
    grid_w, n_freq = 64, HD // 4
    pos = np.arange(SEQ)
    freqs = np.float32(10000.0) ** (-np.arange(n_freq, dtype=np.float32) / np.float32(n_freq))
    ang = np.concatenate([(pos // grid_w).astype(np.float32)[:, None] * freqs,
                          (pos % grid_w).astype(np.float32)[:, None] * freqs], axis=-1)
    rope = np.zeros((2, TOK, HD), np.float32)
    rope[0] = 1.0
    rope[0, :SEQ] = np.tile(np.cos(ang), 2)
    rope[1, :SEQ] = np.tile(np.sin(ang), 2)
    q, k = np.arange(P)[:, None], np.arange(P)[None, :]
    mask = np.zeros((2, P, P), np.float32)
    mask[0][k < q] = -1e30
    mask[1][k > q] = -1e30
    edge = np.ones((4, 2, PAD), np.float32)
    for g, w in enumerate(POOL_WINDOWS):
        for i in range(PAD):
            edge[g, 0, i] = w / (min(i, w // 2) + w // 2)
            edge[g, 1, PAD - 1 - i] = w / (w // 2 + min(i + 1, w // 2))
    return {"ident": ident, "rope": rope, "mask": mask, "edge": edge}


_INS = ["x", "c", "ctx", "c_ctx", "ada_w", "ada_b", "mix_pre_g", "mix_post_g", "ffn_pre_g", "ffn_post_g",
        "ab_w_in", "ab_w_out", "pool_w", "pool_scale", "sink_logit", "c_w_qkv", "c_w_out", "c_q_g", "c_k_g",
        "ffn_w_up", "ffn_conv_w", "ffn_conv_b", "ffn_w_down"]


def kernel(**inputs):
    import numpy as np
    import concourse.bacc as bacc
    from concourse.bass_utils import run_bass_kernel_spmd as run

    nc = bacc.Bacc("TRN2", target_bir_lowering=False, num_devices=1, dynamic_dma_scratch_size=1024)
    arrays = {f"in_{n}_dram": np.ascontiguousarray(inputs[n]) for n in _INS}
    arrays.update({f"const_{n}_dram": a for n, a in shape_constants().items()})
    args = [nc.dram_tensor(n, a.shape, mybir.dt.from_np(a.dtype), kind="ExternalInput").ap()
            for n, a in arrays.items()]
    args.append(nc.dram_tensor("out_dram", (1, SEQ, D), F32, kind="ExternalOutput").ap())
    hybrid_backbone_kernel(nc, *args)
    r = run(nc, [arrays], core_ids=[0])
    return r.results[0]["out_dram"]
```

```python
from contextlib import ExitStack

import concourse.bass as bass
from concourse import mybir

F32 = mybir.dt.float32
F32R = mybir.dt.float32r
BF16 = mybir.dt.bfloat16
ALU = mybir.AluOpType
ACT = mybir.ActivationFunctionType
AX_X = mybir.AxisListType.X

P = 128
BANK = 512
D = 1024
KC = D // P
SEQ, CTX = 512, 256
LAT_T, CTX_T = SEQ // P, CTX // P
ALL_T = LAT_T + CTX_T
TOK = SEQ + CTX
HD = 64
GROUP = 4
POOL_CH = D // 2
POOL_WINDOWS = (2, 4, 8, 16)
PAD = max(POOL_WINDOWS) // 2
UBUF = SEQ + CTX + 4 * PAD
B_HEADS, B_KV = 8, 2
C_HEADS, C_KV = 16, 4
DFF = (8 * D // 3) // 128 * 128
FT = DFF // P
EPS = 1e-6
SCALE = HD ** -0.5
STREAMS = ((0, SEQ), (SEQ, CTX))
PADDED = ((PAD, SEQ), (SEQ + 3 * PAD, CTX))

RAW = 3
UNITS = {"proj0": 12, "out0": 8, "up0": 2 * FT, "down0": 2 * FT,
         "proj1": 12, "out1": 8, "up1": 2 * FT, "down1": 2 * FT}
RINGS = {"proj": 4, "out": 4, "up": 3, "down": 3}
FIRST_UNIT = {}
_n = 0
for _k, _v in UNITS.items():
    FIRST_UNIT[_k] = _n
    _n += _v

VEC_ROWS = 52
CONV_ROWS = 3 * 2 * FT
BIAS_ROWS = 2 * 2 * FT

PROJ = {
    0: (("pool", 0, 512, ALL_T, 0), ("kv", 1024, 256, ALL_T, 0), ("q", 512, 512, ALL_T, 0)),
    1: (("kv", 1024, 512, ALL_T, 0), ("q", 0, 512, LAT_T, 0), ("q", 512, 512, LAT_T, 8)),
}


def attention_groups(l):
    ctx = [LAT_T, LAT_T + 1]
    if l == 1:
        return [(j, n, list(range(ALL_T)), {}) for j in range(C_KV) for n in range(LAT_T)]
    out = []
    for j in range(B_KV):
        for n in range(LAT_T):
            near = [m for m in (n - 1, n, n + 1) if 0 <= m < LAT_T]
            out.append((j, n, ctx + near, {m: int(m > n) for m in near if m != n}))
        out += [(j, n, ctx, {}) for n in ctx]
    return out


INTERLEAVE = ("S0 S1 E0 D0 C S2 E1 C D1 C C E2 S3 D2 C E3 D3 C".split(),
              "S0 S1 E0 D0 C C S2 E1 D1 C C E2 S3 D2 C C E3 D3".split())


BEHIND = 2
PT = BEHIND + 1


def attention_steps(groups, order):
    steps, turned, ended = [], [], None
    slots = order.count("C")

    def product():
        nonlocal ended
        g, i = turned.pop(0)
        steps.append(("V", g, i))
        if ended is not None:
            steps.append(("O", ended, 0))
        ended = g if i == len(groups[g][2]) - 1 else None

    for g in range(len(groups) + 1):
        n = len(groups[g - 1][2]) if g else 0
        at = {c * slots // n: c for c in range(n)}
        slot = 0
        for token in order:
            if token == "C":
                if slot in at:
                    steps.append(("T", g - 1, at[slot]))
                    turned.append((g - 1, at[slot]))
                    if len(turned) > BEHIND:
                        product()
                slot += 1
            elif g < len(groups):
                steps.append((token[0], g, int(token[1])))
    while turned:
        product()
    return steps + [("O", ended, 0)]


def key_pieces(keys):
    out = []
    for i, t in enumerate(keys):
        if out and out[-1][1] + out[-1][2] == t * P and (i * P) % BANK:
            out[-1][2] += P
        else:
            out.append([i * P, t * P, P])
    return out


def hybrid_backbone_kernel(nc, x_in, c, ctx_in, c_ctx, ada_w, ada_b, mix_pre_g, mix_post_g, ffn_pre_g,
                           ffn_post_g, ab_w_in, ab_w_out, pool_w, pool_scale, sink_logit, c_w_qkv, c_w_out,
                           c_q_g, c_k_g, ffn_w_up, ffn_conv_w, ffn_conv_b, ffn_w_down,
                           ident_in, rope_in, mask_in, edge_in, out):
    es = ExitStack()
    with es:
        cursor = [(nc.sbuf_base + 63) // 64 * 64]

        def sb(name, shape, dt=F32, at=None):
            size = 2 if dt == BF16 else 4
            for s in shape[1:]:
                size *= s
            size = (size + 63) // 64 * 64
            if at is None:
                at = cursor[0]
                cursor[0] += size
            t = nc.alloc_sbuf_tensor_at(name, shape, dt, offset=at)
            return t, at + size

        def keep(name, shape, dt=F32):
            return sb(name, shape, dt)[0]

        x = keep("x", [P, ALL_T, D])
        hT_hi = keep("hT_hi", [P, KC, TOK], F32R)
        hT_lo = keep("hT_lo", [P, KC, TOK], F32R)
        raw = keep("raw", [P, RAW, 1024])
        split_at = cursor[0]
        w_hi = keep("w_hi", [P, 4, 1024], F32R)
        w_lo = keep("w_lo", [P, 4, 1024], F32R)
        ident = keep("ident", [P, P])
        ident_b = keep("ident_b", [P, P], BF16)
        mask_b = keep("mask_b", [P, 2, P], BF16)
        rope = keep("rope", [P, 2, ALL_T, HD])
        edge = keep("edge", [P, 4, 2, PAD])
        cols = keep("cols", [P, VEC_ROWS])
        convw = [keep(f"convw{l}", [P, 3, 2 * FT]) for l in range(2)]
        convb = keep("convb", [P, 2, 2 * FT])
        cstat = keep("cstat", [P, KC, 34])
        mul_col = keep("mul_col", [P, 2, 2, KC])
        add_col = keep("add_col", [P, 2, 2, KC])
        gate_rows = keep("gate_rows", [P, D])
        nsink = keep("nsink", [P, B_HEADS])
        minus_half = keep("minus_half", [P, 32])
        ssum = keep("ssum", [P, 2, 8])
        rms = keep("rms", [P, 8])
        xsum = keep("xsum", [P, 8])
        xrms = keep("xrms", [P, 8])
        select = keep("select", [P, 64])
        select_v = keep("select_v", [P, 2, 32])
        gate_at = cursor[0]
        gate = keep("gate", [P, 2, D])
        region = cursor[0]

        pw_hi, a = sb("pw_hi", [P, 4, P], F32R, gate_at)
        pw_lo, a = sb("pw_lo", [P, 4, P], F32R, a)
        pw, a = sb("pw", [P, 4, P], F32, a)
        vecs, a = sb("vecs", [P, 4, P], F32, region)
        silu, a = sb("silu", [P, 2, 16], F32, a)
        mask_f, a = sb("mask_f", [P, 2, P], F32, a)
        xn_at = region + 24 * 1024
        xn, a = sb("xn", [P, ALL_T, D], F32, xn_at)
        h32, tail = sb("h32", [P, 2, TOK], F32, a)
        def ada_memory(tag, acc_at, slots_at, bias_at, post_at):
            acc = sb(f"ada_acc_{tag}", [P, 2, D], F32, acc_at)[0]
            slots = [sb(f"ada_w_{tag}{i}", [P, D], F32, o)[0] for i, o in enumerate(slots_at)]
            bias = sb(f"ada_bias_{tag}", [P, D], F32, bias_at)[0]
            post = sb(f"ada_post_{tag}", [P, D], F32, post_at)[0]
            return acc, slots, bias, post

        KB4 = 4096
        beside_out = ada_memory("out", tail, [region + 20 * 1024] + [tail + i * KB4 for i in (2, 3, 4)],
                                tail + 5 * KB4, tail + 6 * KB4)
        beside_proj = ada_memory("proj", region, [region + i * KB4 for i in (2, 3, 4, 5)],
                                 region + 4 * (B_HEADS * TOK + 2 * B_KV * TOK + 2 * ALL_T * B_KV * HD), tail + 7 * KB4)
        start_w = [sb(f"start_w{i}", [P, 2, D], F32, o)[0]
                   for i, o in enumerate([region + 4 * 1024, region + 12 * 1024] + [xn_at + 6 * KB4 + i * 2 * KB4 for i in range(3)])]
        start_acc = [sb(f"start_acc{i}", [P, 2, D], F32, split_at + 2 * i * KB4)[0] for i in range(2)]
        start_bias = sb("start_bias", [P, D], F32, region + 20 * 1024)[0]
        conv_at = region + 4 * FT * TOK
        beside_up = ada_memory("up", conv_at + 3 * 4 * TOK, [gate_at, gate_at + KB4, split_at + 3 * KB4, split_at + 7 * KB4],
                               conv_at, conv_at + KB4)
        tops = [tail + 8 * KB4, xn_at + 12 * KB4, conv_at + 3 * 4 * TOK + 2 * KB4]
        qT, a = sb("qT", [P, C_HEADS * SEQ], F32R, region)
        kT, a = sb("kT", [P, 2, C_KV, TOK], F32R, a)
        v1, a = sb("v1", [P, ALL_T, C_KV, 2, HD], F32R, a)
        qkn_at = a
        qkn, a = sb("qkn", [P, BANK], F32, a)
        qka, a = sb("qka", [P, BANK], F32, a)
        qkb, a = sb("qkb", [P, BANK], F32, a)
        qks, a = sb("qks", [P, 1024], F32R, a)
        sq, a = sb("sq", [P, BANK], F32, a)
        qk_ss, a = sb("qk_ss", [P, 8], F32, a)
        qk_ms, a = sb("qk_ms", [P, 8], F32, a)
        qk_r, a = sb("qk_r", [P, 8], F32, a)
        tops.append(a)
        qk_gain, a = sb("qk_gain", [P, 2, HD], F32, max(tops[2:]))
        tops.append(a)
        qk_tab, b = sb("qk_tab", [P, 4, ALL_T, HD], F32, gate_at)
        assert b <= region
        q0T, a = sb("q0T", [P, B_HEADS, TOK], F32R, region)
        k0T, a = sb("k0T", [P, 2, B_KV, TOK], F32R, a)
        v0, a = sb("v0", [P, ALL_T, B_KV, 2, HD], F32R, a)
        d0, a = sb("d0", [P, 2, UBUF], F32R, a)
        d1, _ = sb("d1", [P, 2, UBUF], F32R, a)
        d_hi, d_lo = ([d[:, i, :] for d in (d0, d1)] for i in range(2))
        sums, a = sb("sums", [P, 2, UBUF], F32, a)
        ubuf, a = sb("ubuf", [P, 4, UBUF], F32, a)
        assert a <= region + 4 * (C_HEADS * SEQ + 2 * C_KV * TOK + 2 * ALL_T * C_KV * HD)
        prob, a = sb("prob", [P, 2, GROUP, TOK], F32, split_at)
        pT_hi, a = sb("pT_hi", [P, PT, BANK], F32R, a)
        assert a <= split_at + 2 * 4 * 4096
        o_tmp, a = sb("o_tmp", [P, 2, 2, P], F32, qkn_at)
        small, a = sb("small", [P, 5, 64], F32, a)
        pT_lo, a = sb("pT_lo", [P, PT, BANK], F32R, a)
        assert a <= max(tops[2:])
        y0, a = sb("y0", [P, ALL_T, BANK], F32, region)
        sqj, a = sb("sqj", [P, 2, BANK], F32, a)
        t0, a = sb("t0", [P, BANK], F32, a)
        t1, a = sb("t1", [P, BANK], F32, a)
        assert a <= region + 20 * 1024
        act_g, a = sb("act_g", [P, FT, TOK], F32, region)
        conv_a, a = sb("conv_a", [P, TOK], F32, a)
        conv_b, a = sb("conv_b", [P, TOK], F32, a)
        gelu, a = sb("gelu", [P, TOK], F32, a)
        tops.append(a)
        hT_at = split_at - RAW * 4096 - 2 * KC * TOK * 4
        y0d, b = sb("y0d", [P, ALL_T, BANK], F32, hT_at)
        sqjd, b = sb("sqjd", [P, 2, BANK], F32, b)
        t0d, b = sb("t0d", [P, BANK], F32, b)
        t1d, b = sb("t1d", [P, BANK], F32, b)
        g_hi, b = sb("g_hi", [P, 3, TOK], F32R, b)
        g_lo, b = sb("g_lo", [P, 3, TOK], F32R, b)
        assert b <= hT_at + 2 * KC * TOK * 4
        assert hT_at + 2 * KC * TOK * 4 + RAW * 4096 == split_at
        assert max(tops) <= nc.sbuf_usable_end, (tops, nc.sbuf_usable_end)

        ps = es.enter_context(nc.psum_tensor("ps", [P, 8, BANK], F32))
        psf = ps[:, :, :].rearrange("p b n -> p (b n)")

        def bank(n, width=BANK):
            return psf[:, n * BANK:n * BANK + width]

        def sem(name):
            return es.enter_context(nc.semaphore(name))

        x_landed = sem("x_landed")
        ctx_landed = sem("ctx_landed")
        rows_landed = sem("rows_landed")
        late_landed = sem("late_landed")
        store_done = sem("store_done")
        landed = [sem(f"w_landed{i}") for i in range(RAW)]
        hi_split = sem("w_hi_split")
        lo_split = sem("w_lo_split")
        used = {k: sem(f"{k}_w_used") for k in UNITS}
        closed = {k: sem(f"{k}_closed") for k in ("pe", "act", "dve", "pool")}
        sems = {}

        def s(name):
            if name not in sems:
                sems[name] = sem(name)
            return sems[name]

        def close(eng, name):
            eng.drain().then_inc(closed[name], 1)

        def after_phase(eng, n):
            for k in ("pe", "act", "dve", "pool"):
                eng.wait_ge(closed[k], n)

        def unit_slot(phase, u):
            return u % RINGS[phase[:-1]]

        def load_unit(sp, phase, m, src, width, turn=0, per_turn=0):
            n = FIRST_UNIT[phase] + m
            if n >= RAW:
                sp.wait_ge(lo_split, turn * per_turn + (n - RAW + 1))
            sp.dma_start(raw_view(n % RAW, src, width), src).then_inc(landed[n % RAW], 16)

        def raw_view(slot, src, width):
            v = raw[:, slot, 0:width]
            return v if len(src.shape) == 2 else v.rearrange("p (k n) -> p k n", k=src.shape[1])

        def split_hi(act, phase, m, width, turn=0, per_turn=0, free=True):
            n = FIRST_UNIT[phase] + m
            act.wait_ge(landed[n % RAW], turn * (16 * per_turn // RAW) + 16 * (n // RAW + 1))
            if free:
                ring = RINGS[phase[:-1]]
                act.wait_ge(used[phase], turn * per_turn + (m - ring + 1))
            nc.scalar.activation(w_hi[:, unit_slot(phase, m), 0:width], raw[:, n % RAW, 0:width],
                                 ACT.Copy).then_inc(hi_split, 1)

        def split_lo(pool, phase, m, width, turn=0, per_turn=0, by=nc.gpsimd):
            n = FIRST_UNIT[phase] + m
            pool.wait_ge(hi_split, turn * per_turn + (n + 1))
            slot = unit_slot(phase, m)
            by.tensor_tensor(w_lo[:, slot, 0:width], raw[:, n % RAW, 0:width],
                                    w_hi[:, slot, 0:width].bitcast(F32), ALU.subtract).then_inc(lo_split, 1)

        def wait_split(pe, phase, m, turn=0, per_turn=0):
            pe.wait_ge(lo_split, turn * per_turn + (FIRST_UNIT[phase] + m + 1))

        def mm3(outp, s_hi, s_lo, m_hi, m_lo, first, last):
            nc.tensor.matmul(outp, s_hi, m_hi, start=first, stop=False, skip_group_check=True)
            nc.tensor.matmul(outp, s_hi, m_lo, start=False, stop=False, skip_group_check=True)
            return nc.tensor.matmul(outp, s_lo, m_hi, start=False, stop=last, skip_group_check=True)

        def setup_sync(sp):
            def ld(dst, src):
                sp.dma_start(dst, src).then_inc(rows_landed, 16)

            def ld_conv(dst, src):
                sp.dma_start(dst, src).then_inc(s("conv_landed"), 16)

            def rows(a):
                return a.rearrange("a (k n) -> (a k) n", n=P)

            ld(ident[:, :], ident_in)
            ld(vecs[0:16, 0, :], rows(mix_pre_g))
            ld(vecs[16:32, 0, :], rows(ffn_pre_g))
            ld(vecs[32:40, 0, :], rows(c))
            ld(vecs[40:48, 0, :], c_ctx.rearrange("(k n) -> k n", n=P))
            ld(vecs[48:52, 0, :], rows(pool_scale))
            start_load(sp, 0)
            ld_conv(vecs[0:CONV_ROWS, 1, :], ffn_conv_w[0].rearrange("t (f n) -> (t f) n", n=P))
            ld_conv(vecs[0:CONV_ROWS, 2, :], ffn_conv_w[1].rearrange("t (f n) -> (t f) n", n=P))
            ld_conv(vecs[0:BIAS_ROWS // 2, 3, :], ffn_conv_b[0:1].rearrange("a (f n) -> (a f) n", n=P))
            ld_conv(vecs[BIAS_ROWS // 2:BIAS_ROWS, 3, :], ffn_conv_b[1:2].rearrange("a (f n) -> (a f) n", n=P))

        def late_sync(sp):
            def ld(dst, src):
                sp.dma_start(dst, src).then_inc(late_landed, 16)

            ld(mask_f[:, :, :], mask_in.rearrange("a p n -> p a n"))
            ld(rope[:, :, :, :], rope_in.rearrange("a (t p) n -> p a t n", p=P))
            ld(edge[:, :, :, :], edge_in.partition_broadcast(P))
            ld(nsink[:, :], sink_logit.rearrange("a j g -> a (j g)").partition_broadcast(P).rearrange("p a n -> p (a n)"))
            ld(pw[:, :, :], pool_w[0].rearrange("g p n -> p g n"))

        def x_sync(sp):
            sp.dma_start(x[:, 0:LAT_T, :], x_in[0].rearrange("(t p) n -> p t n", p=P)).then_inc(x_landed, 16)
            sp.dma_start(x[:, LAT_T:ALL_T, :], ctx_in[0].rearrange("(t p) n -> p t n", p=P)).then_inc(ctx_landed, 16)

        def setup_tensor(pe):
            pe.wait_ge(rows_landed, 16 * 6)
            for n, (t, r) in enumerate(((0, VEC_ROWS), (1, CONV_ROWS), (2, CONV_ROWS), (3, BIAS_ROWS))):
                if n == 1:
                    pe.wait_ge(s("conv_landed"), 16 * 4)
                nc.tensor.transpose(bank(n, r), vecs[0:r, t, :], ident[0:r, 0:r]).then_inc(s("rows_turned"), 1)
            close(pe, "pe")

        SETUP_DVE = 5

        def setup_vector(dve):
            nc.vector.memset(cstat[:, :, :], 0.0).then_inc(s("setup_dve"), 1)
            nc.vector.memset(minus_half[:, :], -0.5).then_inc(s("setup_dve"), 1)
            nc.vector.memset(select[:, :], 0.0).then_inc(s("setup_dve"), 1)
            nc.vector.memset(gate_rows[:, :], 0.0).then_inc(s("setup_dve"), 1)
            dve.wait_ge(s("setup_dve"), 3)
            nc.vector.memset(select[:, 32:33], 1.0).then_inc(s("setup_dve"), 1)
            dve.wait_ge(s("rows_turned"), 1)
            nc.vector.tensor_copy(cols[:, :], bank(0, VEC_ROWS)).then_inc(s("setup_dve"), 1)
            dve.wait_ge(s("exp_c"), 1)
            nc.vector.tensor_scalar(silu[:, 1, :], silu[:, 0, :], 1.0, None, ALU.add).then_inc(s("setup_dve"), 1)
            dve.wait_ge(s("setup_dve"), 7)
            nc.vector.reciprocal(silu[:, 0, :], silu[:, 1, :]).then_inc(s("setup_dve"), 1)
            dve.wait_ge(s("setup_dve"), 8)
            nc.vector.tensor_tensor(cstat[:, :, 2:4].rearrange("p k v -> p v k"),
                                    cols[:, 32:48].rearrange("p (v k) -> p v k", v=2),
                                    silu[:, 0, :].rearrange("p (v k) -> p v k", v=2), ALU.mult).then_inc(s("setup_dve"), 1)
            for n in range(2):
                dve.wait_ge(s("rows_turned"), 2 + n)
                nc.vector.tensor_copy(convw[n][:, :, :].rearrange("p t f -> p (t f)"),
                                      bank(1 + n, CONV_ROWS)).then_inc(s("setup_dve"), 1)
            dve.wait_ge(s("rows_turned"), 4)
            nc.vector.tensor_copy(convb[:, :, :].rearrange("p l f -> p (l f)"), bank(3, BIAS_ROWS)).then_inc(s("setup_dve"), 1)
            close(dve, "dve")

        def setup_scalar(act):
            act.wait_ge(s("setup_dve"), 6)
            nc.scalar.activation(silu[:, 0, :], cols[:, 32:48], ACT.Exp, scale=-1.0).then_inc(s("exp_c"), 1)
            close(act, "act")

        ADA_RING = 4
        START_MACS = 8
        START_RING = 4

        def ada_row(l, i, v):
            return 96 + 2 * (5 - i) + v if l else 32 * (i // 2) + 2 * (i % 2) + v

        def ada_load(sp, n, mem, l, rows, cols_, turn=0):
            if n >= ADA_RING:
                sp.wait_ge(s("ada_mac"), turn * (2 * KC) + (START_MACS + 2 * (n - ADA_RING + 1)))
            sp.dma_start(mem[1][n % ADA_RING][:, :], ada_w[l, rows, cols_]).then_inc(s(f"ada_landed{n % ADA_RING}"), 16)

        def ada_loads(sp, mem, first, last):
            for n in range(first, last):
                i, k = 2 + n // KC, n % KC
                ada_load(sp, n, mem, 0, slice(k * P, (k + 1) * P), slice(i * D, (i + 1) * D))

        def ada_small_loads(sp, mem, l, blocks):
            for i in blocks:
                r = ada_row(l, i, 0)
                sp.dma_start(mem[2][r:r + 2, :], ada_b[l, i * D:(i + 1) * D].partition_broadcast(2)
                             ).then_inc(s("ada_rows_landed"), 16)
            for i, g in ((2, mix_post_g), (5, ffn_post_g)):
                if i in blocks:
                    r0, r1 = ({2: (32, 34), 5: (64, 68)}, {2: (102, 108), 5: (96, 102)})[l][i]
                    sp.dma_start(mem[3][r0:r1, :], g[l, :].partition_broadcast(r1 - r0)
                                 ).then_inc(s("ada_rows_landed"), 16)

        def ada_mac(dve, mem, n, k, turn=0):
            acc, slots = mem[0], mem[1]
            if k == 0:
                dve.wait_ge(s("ada_sum"), turn + (2 + n // KC))
            else:
                dve.wait_ge(s("ada_mac"), turn * (2 * KC) + (START_MACS + 2 * n))
            dve.wait_ge(s(f"ada_landed{n % ADA_RING}"), turn * (16 * KC // ADA_RING) + 16 * (n // ADA_RING + 3))
            ada_products(acc, slots[n % ADA_RING][:, :], k)

        def ada_products(acc, w, k):
            for v in range(2):
                f = cstat[:, k, 2 + v:3 + v]
                if k == 0:
                    op = nc.vector.tensor_scalar(acc[:, v, :], w, f, None, ALU.mult)
                else:
                    op = nc.vector.scalar_tensor_tensor(out=acc[:, v, :], in0=w, scalar=f, in1=acc[:, v, :],
                                                        op0=ALU.mult, op1=ALU.add)
                op.then_inc(s("ada_mac"), 1)

        def ada_macs(dve, mem, blocks):
            for i in blocks:
                for k in range(KC):
                    ada_mac(dve, mem, (i - 2) * KC + k, k)

        def ada_sum(pe, mem, i):
            pe.wait_ge(s("ada_mac"), START_MACS + 2 * KC * (i - 1))
            r0 = ada_row(0, i, 0) // 32 * 32
            for v in range(2):
                m = ada_row(0, i, v) - r0
                for half in range(2):
                    mm = nc.tensor.matmul(ps[r0:r0 + 32, 4 + half, :], select[:, 32 - m:64 - m],
                                          mem[0][:, v, half * BANK:(half + 1) * BANK],
                                          start=m == 0, stop=m == 3, skip_group_check=True)
            mm.then_inc(s("ada_sum"), 1)

        def ada_turn(pe, n, b):
            pe.wait_ge(s("ada_biased"), n)
            for k in range(KC):
                mm = nc.tensor.transpose(bank(b, 2 * BANK)[:, k * P:(k + 1) * P], gate_rows[:, k * P:(k + 1) * P],
                                         ident[:, :])
            mm.then_inc(s("ada_turned"), 1)

        def ada_bias(dve, mem, n, rows_landed_, r0, nr, src):
            dve.wait_ge(s("ada_rows_landed"), 16 * rows_landed_)
            nc.vector.tensor_tensor(gate_rows[r0:r0 + nr, :], src, mem[2][r0:r0 + nr, :],
                                    ALU.add).then_inc(s("ada_biased"), 1)

        def ada_columns(dve, n, l, blocks, b):
            dve.wait_ge(s("ada_turned"), n)
            turned = bank(b, 2 * BANK).rearrange("p (k r) -> p r k", r=P)
            for i in blocks:
                sub, what = divmod(i, 3)
                for v in range(2):
                    src = turned[:, ada_row(l, i, v), :]
                    if what == 0:
                        nc.vector.tensor_copy(add_col[:, sub, v, :], src)
                    elif what == 1:
                        g = 16 * sub + 8 * l
                        nc.vector.scalar_tensor_tensor(out=mul_col[:, sub, v, :], in0=src, scalar=1.0,
                                                       in1=cols[:, g:g + 8], op0=ALU.add, op1=ALU.mult
                                                       )

        def ada_gates(dve, mem, n, r0, nr):
            dve.wait_ge(s("ada_turned"), n)
            nc.vector.tensor_tensor(gate_rows[r0:r0 + nr, :], gate_rows[r0:r0 + nr, :], mem[3][r0:r0 + nr, :],
                                    ALU.mult)

        def start_load(sp, q):
            if q == START_RING:
                sp.wait_ge(s("ada_mac"), 4)
            elif q > START_RING:
                sp.wait_ge(s("start_direct"), q - START_RING)
            i, k = divmod(2 * q, KC)
            sp.dma_start(start_w[q % START_RING][:, :, :],
                         ada_w[0, k * P:(k + 2) * P, i * D:(i + 1) * D].rearrange("(k p) n -> p k n", p=P)
                         ).then_inc(s(f"ada_landed{q % START_RING}"), 16)

        def start_vector(dve):
            for i in range(2):
                dve.wait_ge(s("ada_landed0"), 16 * (i + 1))
                for k in range(2):
                    if k:
                        dve.wait_ge(s("ada_mac"), 4 * i + 2)
                    ada_products(start_acc[i], start_w[0][:, k, :], k)
            dve.wait_ge(s("ada_sum"), 2)
            ada_bias(dve, (None, None, start_bias), 1, 2, 0, 4, psf[0:4, 4 * BANK:6 * BANK])
            ada_columns(dve, 1, 0, (0, 1), 4)
            close(dve, "dve")

        def start_tensor(pe):
            pe.wait_ge(s("setup_dve"), 9)
            for i in range(2):
                m = 2 * i
                for q in range(4 * i + 1, 4 * i + 4):
                    pe.wait_ge(s(f"ada_landed{q % START_RING}"), 16 * (q // START_RING + 1))
                    for k in range(2):
                        for half in range(2):
                            mm = nc.tensor.matmul(ps[0:32, 4 + half, :], cstat[:, 2 * (q % 4) + k, 2 - m:34 - m],
                                                  start_w[q % START_RING][:, k, half * BANK:(half + 1) * BANK],
                                                  start=q == 1 and k == 0, stop=False, skip_group_check=True)
                    mm.then_inc(s("start_direct"), 1)
                pe.wait_ge(s("ada_mac"), 4 * i + 4)
                for v in range(2):
                    for half in range(2):
                        mm = nc.tensor.matmul(ps[0:32, 4 + half, :], select[:, 32 - m - v:64 - m - v],
                                              start_acc[i][:, v, half * BANK:(half + 1) * BANK],
                                              start=False, stop=i == 1 and v == 1, skip_group_check=True)
                mm.then_inc(s("ada_sum"), 1)
            ada_turn(pe, 1, 4)
            close(pe, "pe")

        def start_scalar(act):
            for t in range(ALL_T):
                act.wait_ge(x_landed if t < LAT_T else ctx_landed, 16)
                if t:
                    act.wait_ge(s("mix0_xn"), t)
                nc.scalar.activation(xn[:, t, :], x[:, t, :], ACT.Square,
                                     accum_out=xsum[:, t:t + 1]).then_inc(s("mix0_sq"), 1)
                act.wait_ge(s("mix0_rms"), 2 * t + 2)
                nc.scalar.activation(xn[:, t, :], x[:, t, :], ACT.Copy,
                                     scale=xrms[:, t:t + 1]).then_inc(s("mix0_xn"), 1)
            close(act, "act")

        def start_pool(pool):
            pool.wait_ge(s("setup_dve"), SETUP_DVE)
            for t in range(ALL_T):
                x_rms(pool, "mix0", t)
            close(pool, "pool")

        def x_square(act, tag, after, nt, t):
            act.wait_ge(s(f"{after}_post"), post_count(nt, t, 3))
            nc.scalar.activation(xn[:, t, :], x[:, t, :], ACT.Square, accum_out=xsum[:, t:t + 1]).then_inc(s(f"{tag}_sq"), 1)

        def by_scalar(tag, nt, t):
            return tag == "mix1" and t % 2 == 1 and t < nt - 1

        def x_squares(act, tag, after, nt, t):
            if t:
                x_square(act, tag, after, nt, t - 1)
            if t >= 2 and by_scalar(tag, nt, t - 2):
                act.wait_ge(s(f"{tag}_rms"), 2 * (t - 2) + 2)
                nc.scalar.activation(xn[:, t - 2, :], x[:, t - 2, :], ACT.Copy,
                                     scale=xrms[:, t - 2:t - 1]).then_inc(s(f"{tag}_xn"), 1)

        def x_rms(pool, tag, t):
            pool.wait_ge(s(f"{tag}_sq"), t + 1)
            nc.gpsimd.tensor_scalar(xsum[:, t:t + 1], xsum[:, t:t + 1], 1.0 / D, EPS, ALU.mult,
                                    ALU.add).then_inc(s(f"{tag}_rms"), 1)
            pool.wait_ge(s(f"{tag}_rms"), 2 * t + 1)
            nc.gpsimd.tensor_tensor(xrms[:, t:t + 1], xsum[:, t:t + 1], minus_half[:, 0:1],
                                    ALU.pow).then_inc(s(f"{tag}_rms"), 1)

        def x_normed(dve, tag, t):
            dve.wait_ge(s(f"{tag}_rms"), 2 * t + 2)
            nc.vector.tensor_scalar(xn[:, t, :], x[:, t, :], xrms[:, t:t + 1], None, ALU.mult).then_inc(s(f"{tag}_xn"), 1)

        def norm_scalar(act, tag, before, sub, nt, b0, prefetch):
            after_phase(act, before)
            ns = 2 if nt == ALL_T else 1
            prefetch(act, range(0, 1))
            for k in range(KC):
                act.wait_ge(s(f"{tag}_turned"), k + 1)
                if k >= 2:
                    act.wait_ge(s(f"{tag}_split"), 2 * (k - 1))
                for v in range(ns):
                    c0, n = STREAMS[v]
                    nc.scalar.activation(h32[:, k % 2, c0:c0 + n], bank(b0 + 2 * (k % 2), 1024)[:, c0:c0 + n],
                                         ACT.Identity, bias=add_col[:, sub, v, k:k + 1],
                                         scale=mul_col[:, sub, v, k:k + 1]).then_inc(s(f"{tag}_h32"), 1)
                if k % 2:
                    prefetch(act, range(1 + k // 2, 2 + k // 2))
            close(act, "act")

        def norm_pool(pool, tag, before, nt, prefetch):
            after_phase(pool, before)
            prefetch(pool)
            close(pool, "pool")

        def late_vector(dve):
            dve.wait_ge(late_landed, 5 * 16)
            nc.vector.tensor_copy(ident_b[:, :], ident[:, :]).then_inc(s("late_dve"), 1)
            nc.vector.tensor_copy(mask_b[:, :, :], mask_f[:, :, :]).then_inc(s("late_dve"), 1)
            nc.vector.tensor_scalar(nsink[:, :], nsink[:, :], -1.0, None, ALU.mult).then_inc(s("late_dve"), 1)
            nc.vector.tensor_copy(pw_hi[:, :, :], pw[:, :, :]).then_inc(s("late_dve"), 1)
            dve.wait_ge(s("late_dve"), 4)
            nc.vector.tensor_tensor(pw_lo[:, :, :], pw[:, :, :], pw_hi[:, :, :].bitcast(F32),
                                    ALU.subtract).then_inc(s("late_dve"), 1)

        def norm_vector(dve, tag, before, nt):
            after_phase(dve, before)
            if tag == "mix0":
                late_vector(dve)
            ns = 2 if nt == ALL_T else 1
            T = nt * P
            for k in range(KC):
                dve.wait_ge(s(f"{tag}_h32"), ns * (k + 1))
                nc.vector.tensor_copy(hT_hi[:, k, 0:T], h32[:, k % 2, 0:T]).then_inc(s(f"{tag}_split"), 1)
                dve.wait_ge(s(f"{tag}_split"), 2 * k + 1)
                nc.vector.tensor_tensor(hT_lo[:, k, 0:T], h32[:, k % 2, 0:T], hT_hi[:, k, 0:T].bitcast(F32),
                                        ALU.subtract).then_inc(s(f"{tag}_split"), 1)
            close(dve, "dve")

        def norm_tensor(pe, tag, before, nt, b0, fill):
            after_phase(pe, before)
            ns = 2 if nt == ALL_T else 1
            for k in range(KC):
                if k >= 2:
                    pe.wait_ge(s(f"{tag}_h32"), ns * (k - 1))
                for t in range(nt):
                    if k == 0 and t == 0:
                        pe.wait_ge(s(f"{tag}_xn"), nt)
                    mm = nc.tensor.transpose(bank(b0 + 2 * (k % 2), 1024)[:, t * P:(t + 1) * P],
                                             xn[:, t, k * P:(k + 1) * P], ident[:, :])
                mm.then_inc(s(f"{tag}_turned"), 1)
                if k >= 2:
                    fill(k - 2)
            close(pe, "pe")
            fill(KC - 2)
            fill(KC - 1)
            pe.wait_ge(s(f"{tag}_h32"), ns * KC)

        def token_tiles(l):
            out = []
            for gi, (kind, _, w, nt, h0) in enumerate(PROJ[l]):
                if kind != "pool":
                    heads = w // HD if kind == "q" else w // HD // 2
                    out += [(gi, kind, t, heads, h0) for t in range(nt)]
            return out

        def rope_plan(l):
            base, n, tb, m = [], 0, [], 0
            for _, kind, _, heads, _ in token_tiles(l):
                base.append(n)
                tb.append(m)
                n += 6 + (2 if l else 0) + (kind == "kv")
                m += 2 if (l or kind == "q") else 1
            return base + [n], tb + [m]

        def proj_sync(sp, l):
            w = (ab_w_in, c_w_qkv)[l][0]
            m = 0
            for _, c0, width, _, _ in PROJ[l]:
                for u in range(4):
                    src = w[2 * u * P:(2 * u + 2) * P, c0:c0 + width].rearrange("(k p) n -> p k n", p=P)
                    load_unit(sp, f"proj{l}", m, src, 2 * width)
                    if l == 0 and m == 6:
                        after_phase(sp, 3)
                        ada_small_loads(sp, beside_proj, 0, (2, 3))
                        ada_loads(sp, beside_proj, 0, 2 * KC)
                    m += 1

        def unit_width(l, m):
            return 2 * PROJ[l][m // 4][2]

        def acc_free_steps(l, kind):
            return (2 if l else 2) + (kind == "kv")

        U_BANK = (6, 0, 2, 6)
        ACC_BANK = (0, 6)

        def proj_first(pe, l, tag):
            phase, (kind, _, width, _, _) = f"proj{l}", PROJ[l][0]

            def chunk(k):
                pe.wait_ge(s(f"{tag}_split"), 2 * (k + 1))
                if k % 2 == 0:
                    wait_split(pe, phase, k // 2)
                slot, c0 = unit_slot(phase, k // 2), (k % 2) * width
                if kind == "pool":
                    for t0_, w in STREAMS:
                        mm = mm3(bank(U_BANK[0], 1024)[:, t0_:t0_ + w], w_hi[:, slot, c0:c0 + P], w_lo[:, slot, c0:c0 + P],
                                 hT_hi[:, k, t0_:t0_ + w], hT_lo[:, k, t0_:t0_ + w], k == 0, k == KC - 1)
                else:
                    mm = mm3(bank(ACC_BANK[l], width), hT_hi[:, k, 0:P], hT_lo[:, k, 0:P],
                             w_hi[:, slot, c0:c0 + width], w_lo[:, slot, c0:c0 + width], k == 0, k == KC - 1)
                if k == KC - 1:
                    mm.then_inc(s("u_done" if kind == "pool" else f"acc_done{l}"), 1)
            return chunk

        def proj_tensor(pe, l):
            phase = f"proj{l}"
            base, tb = rope_plan(l)
            tiles = token_tiles(l)
            q_t = (q0T[:, :, :], qT[:, :].rearrange("p (h n) -> p h n", h=C_HEADS))[l]

            def turn(n):
                _, kind, _, heads, _ = tiles[n]
                blocks = heads if kind == "q" else 2 * heads
                pe.wait_ge(s(f"qk_steps{l}"), base[n + 1])
                if kind == "kv":
                    pe.wait_ge(s(f"k_dup{l}"), n + 1)
                for b in range(tb[n + 1] - tb[n]):
                    nb = tb[n] + b
                    if nb >= 2:
                        pe.wait_ge(s(f"turned_read{l}"), nb - 1)
                    for i in range(4):
                        mm = nc.tensor.transpose(bank(2 + nb % 2)[:, i * P:(i + 1) * P],
                                                 qks[:, (4 * b + i) * P:(4 * b + i + 1) * P].bitcast(F32), ident[:, :])
                    mm.then_inc(s(f"qk_turned{l}"), 1)

            m = n = 0
            for gi, (kind, _, width, nt, _) in enumerate(PROJ[l]):
                def wv(part, k, c0, w):
                    slot = unit_slot(phase, m + k // 2)
                    return part[:, slot, (k % 2) * width + c0:(k % 2) * width + c0 + w]

                if kind == "pool":
                    for f in range(1, 4):
                        if f == 3:
                            pe.wait_ge(s("u_read"), 2)
                        for k in range(KC):
                            for c0, w in STREAMS:
                                mm = mm3(bank(U_BANK[f], 1024)[:, c0:c0 + w], wv(w_hi, k, f * P, P), wv(w_lo, k, f * P, P),
                                         hT_hi[:, k, c0:c0 + w], hT_lo[:, k, c0:c0 + w], k == 0, k == KC - 1)
                            if f == 3 and k in (1, 3, 5):
                                mm.then_inc(used[phase], 1)
                        mm.then_inc(s("u_done"), 1)
                        if f == 2:
                            ada_sum(pe, beside_proj, 2)
                    pe.drain().then_inc(used[phase], 1)
                    pe.wait_ge(s("u_read"), 4)
                else:
                    for t in range(nt):
                        if n >= 2:
                            pe.wait_ge(s(f"qk_steps{l}"), base[n - 2] + acc_free_steps(l, tiles[n - 2][1]))
                        for k in range(KC) if gi or t else ():
                            if t == 0 and k % 2 == 0:
                                wait_split(pe, phase, m + k // 2)
                            tt = slice(t * P, (t + 1) * P)
                            mm = mm3(bank(ACC_BANK[l] + n % 2, width), hT_hi[:, k, tt], hT_lo[:, k, tt],
                                     wv(w_hi, k, 0, width), wv(w_lo, k, 0, width), k == 0, k == KC - 1)
                            if t == nt - 1 and k in (1, 3, 5):
                                mm.then_inc(used[phase], 1)
                        if gi or t:
                            mm.then_inc(s(f"acc_done{l}"), 1)
                        if l == 0 and n == 1:
                            pe.wait_ge(s("u_read"), 6)
                        if n >= 1:
                            turn(n - 1)
                        if l == 0 and n == 0:
                            ada_sum(pe, beside_proj, 3)
                        if l == 0 and n == 2:
                            ada_turn(pe, 2, 4)
                        n += 1
                    pe.drain().then_inc(used[phase], 1)
                m += 4
            def pool_products(windows):
                for f in windows:
                    pe.wait_ge(s("pool_d"), 2 * f + 2)
                    if f >= 2:
                        pe.wait_ge(s("pool_out"), 4 * (f - 1))
                    for v, (c0, w) in enumerate(STREAMS):
                        p0 = PADDED[v][0]
                        mm = mm3(bank(4 + 2 * (f % 2), 1024)[:, c0:c0 + w], pw_hi[:, f, :], pw_lo[:, f, :],
                                 d_hi[f % 2][:, p0:p0 + w], d_lo[f % 2][:, p0:p0 + w], True, True)
                    mm.then_inc(s("pool_mm"), 1)

            if l == 0:
                pool_products((0, 1))
            turn(n - 1)
            if l == 0:
                pool_products((2, 3))
            close(pe, "pe")

        def proj_prefetch(l):
            def act_part(act, units):
                for m in units:
                    if m < 4:
                        split_hi(act, f"proj{l}", m, unit_width(l, m), free=False)

            def pool_part(pool):
                for m in range(4):
                    split_lo(pool, f"proj{l}", m, unit_width(l, m))
            return act_part, pool_part

        def proj_scalar(act, l, before):
            phase = f"proj{l}"
            base, tb = rope_plan(l)
            tiles = token_tiles(l)
            q_t = (q0T[:, :, :], qT[:, :].rearrange("p (h n) -> p h n", h=C_HEADS))[l]
            k_t = (k0T, kT)[l]
            v_hl = (v0, v1)[l]

            def read_turned(n):
                _, kind, t, heads, h0 = tiles[n]
                for b in range(tb[n + 1] - tb[n]):
                    nb = tb[n] + b
                    act.wait_ge(s(f"qk_turned{l}"), nb + 1)
                    src = bank(2 + nb % 2).rearrange("p (i n) -> p i n", i=4)
                    tt = slice(t * P, (t + 1) * P)
                    if kind == "q":
                        dst = q_t[:, h0 + 4 * b:h0 + 4 * b + 4, tt]
                    else:
                        src = bank(2 + nb % 2).rearrange("p (j a n) -> p j a n", j=2, a=2)
                        dst = k_t[:, :, 2 * b:2 * b + 2, tt].rearrange("p a j n -> p j a n")
                    nc.scalar.activation(dst, src, ACT.Copy).then_inc(s(f"turned_read{l}"), 1)

            after_phase(act, before)
            m, n = 4, 0
            for gi, (kind, _, width, nt, _) in enumerate(PROJ[l]):
                if kind == "pool":
                    for f in range(4):
                        if f == 3:
                            for i in range(3):
                                split_hi(act, phase, m, unit_width(l, m))
                                m += 1
                        act.wait_ge(s("u_done"), f + 1)
                        act.wait_ge(s("u_zeroed"), 1)
                        for v, (c0, w) in enumerate(STREAMS):
                            p0 = PADDED[v][0]
                            nc.scalar.activation(ubuf[:, f, p0:p0 + w], bank(U_BANK[f], 1024)[:, c0:c0 + w],
                                                 ACT.Copy).then_inc(s("u_read"), 1)
                else:
                    for t in range(nt):
                        if gi < 2 and t == nt - 1:
                            split_hi(act, phase, m, unit_width(l, m))
                            m += 1
                        act.wait_ge(s(f"acc_done{l}"), n + 1)
                        heads = tiles[n][3]
                        if l:
                            if n:
                                act.wait_ge(s(f"qk_steps{l}"), base[n - 1] + 1 + (tiles[n - 1][1] == "kv"))
                            nc.scalar.activation(sq[:, 0:heads * HD], bank(ACC_BANK[l] + n % 2, heads * HD),
                                                 ACT.Square).then_inc(s("qk_sq"), 1)
                        if kind == "kv":
                            nc.scalar.activation(v_hl[:, t, :, 0, :], bank(ACC_BANK[l] + n % 2)[:, heads * HD:2 * heads * HD]
                                                 .rearrange("p (j d) -> p j d", d=HD),
                                                 ACT.Copy).then_inc(s(f"v_hi{l}"), 1)
                        if n:
                            read_turned(n - 1)
                        if gi < 2 and t == nt - 2:
                            for i in range(2):
                                split_hi(act, phase, m, unit_width(l, m))
                                m += 1
                        if gi < 2 and t == nt - 1:
                            split_hi(act, phase, m, unit_width(l, m))
                            m += 1
                        if kind == "kv":
                            act.wait_ge(s(f"qk_steps{l}"), base[n + 1])
                            kk = qks[:, 0:heads * 4 * HD].rearrange("p (i d n) -> p i d n", d=2, n=HD)
                            nc.scalar.activation(kk[:, :, 1, :], kk[:, :, 0, :].bitcast(F32),
                                                 ACT.Copy).then_inc(s(f"k_dup{l}"), 1)
                        n += 1
                if kind == "pool":
                    split_hi(act, phase, m, unit_width(l, m))
                    m += 1
            read_turned(n - 1)
            if l == 0:
                for f in range(4):
                    act.wait_ge(s("pool_mm"), f + 1)
                    for v, (c0, w) in enumerate(STREAMS):
                        nc.scalar.activation(hT_hi[:, f, c0:c0 + w], bank(4 + 2 * (f % 2), 1024)[:, c0:c0 + w],
                                             ACT.Copy, scale=cols[:, 48 + f:49 + f]).then_inc(s("pool_hi"), 1)
            close(act, "act")

        DIFFERENCE_AFTER = (0, 2, 7, 9)

        def window_sums(pool, windows):
            for f in windows:
                pool.wait_ge(s("u_read"), 2 * f + 2)
                src, reach = ubuf[:, f, :], 1
                for step in range(f + 1):
                    h = max(1, 2 ** step // 2)
                    dst = sums[:, step % 2, :]
                    lo, hi = reach, UBUF - reach
                    if step == 0:
                        a, b = src[:, lo - 1:hi - 1], src[:, lo:hi]
                    else:
                        a, b = src[:, lo - h:hi - h], src[:, lo + h:hi + h]
                    if step:
                        pool.wait_ge(s("win_sum"), f * (f + 1) // 2 + step)
                    elif f:
                        pool.wait_ge(s("pool_d32"), 3 * f)
                    nc.gpsimd.tensor_tensor(dst[:, lo:hi], a, b, ALU.add).then_inc(s("win_sum"), 1)
                    src = dst
                    reach += max(1, 2 ** step)

        def proj_pool(pool, l, before):
            phase = f"proj{l}"
            after_phase(pool, before)
            m, n = 4, 0
            tiles = token_tiles(l)
            base, _ = rope_plan(l)
            for gi, (kind, _, width, nt, _) in enumerate(PROJ[l]):
                if kind == "pool":
                    nc.gpsimd.memset(ubuf[:, :, :], 0.0).then_inc(s("u_zeroed"), 1)
                    for i in range(4):
                        split_lo(pool, phase, m, unit_width(l, m))
                        m += 1
                    window_sums(pool, (0, 1))
                elif l:
                    for t in range(nt):
                        if gi < 2 and t == nt - 1:
                            for i in range(3):
                                split_lo(pool, phase, m, unit_width(l, m))
                                m += 1
                        pool.wait_ge(s(f"qk_steps{l}"), base[n] + 1 + (kind == "kv"))
                        heads = tiles[n][3]
                        nc.gpsimd.tensor_scalar(qk_ms[:, 0:heads], qk_ss[:, 0:heads], 1.0 / HD, EPS, ALU.mult,
                                                ALU.add).then_inc(s("qk_rms"), 1)
                        pool.wait_ge(s("qk_rms"), 2 * n + 1)
                        nc.gpsimd.tensor_tensor(qk_r[:, 0:heads], qk_ms[:, 0:heads], minus_half[:, 0:heads],
                                                ALU.pow).then_inc(s("qk_rms"), 1)
                        n += 1
                if kind != "pool" and gi < 2:
                    while m < 4 * (gi + 2):
                        split_lo(pool, phase, m, unit_width(l, m))
                        m += 1
            if l == 0:
                window_sums(pool, (2, 3))
            close(pool, "pool")

        def proj_vector(dve, l, before):
            base, _ = rope_plan(l)
            tiles = token_tiles(l)
            v_hl = (v0, v1)[l]
            steps = s(f"qk_steps{l}")
            after_phase(dve, before)
            if l:
                dve.wait_ge(s("gain_landed"), 2 * 16)
                nc.vector.tensor_scalar(qk_gain[:, 0, :], qk_gain[:, 0, :], SCALE, None, ALU.mult).then_inc(s("qk_tab"), 1)
                dve.wait_ge(s("qk_tab"), 1)
                for i in range(4):
                    nc.vector.tensor_tensor(qk_tab[:, i, :, :], rope[:, i % 2, :, :],
                                            qk_gain[:, i // 2, :].unsqueeze(1).broadcast_to([P, ALL_T, HD]),
                                            ALU.mult).then_inc(s("qk_tab"), 1)
                dve.wait_ge(s("qk_tab"), 5)
            else:
                ada_macs(dve, beside_proj, (2, 3))
            for n, (gi, kind, t, heads, h0) in enumerate(tiles):
                W = heads * HD
                src = bank(ACC_BANK[l] + n % 2, W).rearrange("p (h d) -> p h d", d=HD)
                at = base[n]
                if n:
                    dve.wait_ge(steps, at)
                if kind == "kv":
                    dve.wait_ge(s(f"v_hi{l}"), n + 1)
                    nc.vector.tensor_tensor(v_hl[:, t, :, 1, :], bank(ACC_BANK[l] + n % 2)[:, W:2 * W]
                                            .rearrange("p (j d) -> p j d", d=HD),
                                            v_hl[:, t, :, 0, :].bitcast(F32), ALU.subtract).then_inc(steps, 1)
                    at += 1
                else:
                    dve.wait_ge(s(f"acc_done{l}"), n + 1)
                if l:
                    dve.wait_ge(s("qk_sq"), n + 1)
                    nc.vector.reduce_sum(qk_ss[:, 0:heads], sq[:, 0:W].rearrange("p (h d) -> p h d", d=HD),
                                         AX_X).then_inc(steps, 1)
                    dve.wait_ge(s("qk_rms"), 2 * n + 2)
                    nrm = qkn[:, 0:W].rearrange("p (h d) -> p h d", d=HD)
                    nc.vector.tensor_tensor(nrm, src, qk_r[:, 0:heads].unsqueeze(2).broadcast_to([P, heads, HD]),
                                            ALU.mult).then_inc(steps, 1)
                    at += 2
                    dve.wait_ge(steps, at)
                    src = nrm
                    tab = [qk_tab[:, 2 * (kind == "kv") + i, t, :] for i in range(2)]
                else:
                    tab = [rope[:, i, t, :] for i in range(2)]
                a = qka[:, 0:W].rearrange("p (h d) -> p h d", d=HD)
                b = qkb[:, 0:W].rearrange("p (h d) -> p h d", d=HD)
                for dst, tb_ in zip((a, b), tab):
                    nc.vector.tensor_tensor(dst, src, tb_.unsqueeze(1).broadcast_to([P, heads, HD]),
                                            ALU.mult).then_inc(steps, 1)
                at += 2
                dve.wait_ge(steps, at)
                half = HD // 2
                nc.vector.tensor_tensor(a[:, :, 0:half], a[:, :, 0:half], b[:, :, half:HD],
                                        ALU.subtract).then_inc(steps, 1)
                nc.vector.tensor_tensor(a[:, :, half:HD], a[:, :, half:HD], b[:, :, 0:half],
                                        ALU.add).then_inc(steps, 1)
                at += 2
                dve.wait_ge(steps, at)
                if n:
                    dve.wait_ge(s(f"qk_turned{l}"), rope_plan(l)[1][n])
                if kind == "q":
                    v = qks[:, 0:2 * W].rearrange("p (h a d) -> p h a d", a=2, d=HD)
                    hi, lo = v[:, :, 0, :], v[:, :, 1, :]
                else:
                    v = qks[:, 0:4 * W].rearrange("p (h a c d) -> p h a c d", a=2, c=2, d=HD)
                    hi, lo = v[:, :, 0, 0, :], v[:, :, 1, 0, :]
                nc.vector.tensor_copy(hi, a).then_inc(steps, 1)
                dve.wait_ge(steps, at + 1)
                nc.vector.tensor_tensor(lo, a, hi.bitcast(F32), ALU.subtract).then_inc(steps, 1)
                assert at + 2 == base[n + 1]
                if l == 0 and n == 0:
                    dve.wait_ge(s("ada_sum"), 4)
                    ada_bias(dve, beside_proj, 2, 5, 32, 4, psf[32:36, 4 * BANK:6 * BANK])
                if l == 0 and n == 2:
                    ada_columns(dve, 2, 0, (2, 3), 4)
                    ada_gates(dve, beside_proj, 2, 32, 2)
                if l == 0 and n in DIFFERENCE_AFTER:
                    pool_difference(dve, DIFFERENCE_AFTER.index(n))
                if l == 0 and n == len(tiles) - 2:
                    pool_split(dve, 0)
                    pool_split(dve, 1)
            if l == 0:
                for f in (2, 3):
                    dve.wait_ge(s("pool_mm"), f - 1)
                    pool_split(dve, f)
                for f in range(4):
                    pool_lo(dve, f)
            close(dve, "dve")

        def pool_difference(dve, f):
            acc = sums[:, f % 2, :]
            dve.wait_ge(s("win_sum"), (f + 1) * (f + 2) // 2)
            for v, (p0, w) in enumerate(PADDED):
                e = acc[:, p0:p0 + w]
                ends = e.rearrange("p (a n) -> p a n", n=PAD)[:, 0:w // PAD:w // PAD - 1, :]
                nc.vector.tensor_tensor(ends, ends, edge[:, f, :, :], ALU.mult).then_inc(s("pool_d32"), 1)
            dve.wait_ge(s("pool_d32"), 3 * f + 2)
            lo = PADDED[0][0]
            nc.vector.scalar_tensor_tensor(out=ubuf[:, f, lo:UBUF - PAD], in0=acc[:, lo:UBUF - PAD],
                                           scalar=1.0 / POOL_WINDOWS[f], in1=ubuf[:, f, lo:UBUF - PAD],
                                           op0=ALU.mult, op1=ALU.subtract).then_inc(s("pool_d32"), 1)

        def pool_split(dve, f):
            dve.wait_ge(s("pool_d32"), 3 * (3 if f == 1 else f) + 3)
            nc.vector.tensor_copy(d_hi[f % 2], ubuf[:, f, :]).then_inc(s("pool_d"), 1)
            dve.wait_ge(s("pool_d"), 2 * f + 1)
            nc.vector.tensor_tensor(d_lo[f % 2], ubuf[:, f, :], d_hi[f % 2].bitcast(F32),
                                    ALU.subtract).then_inc(s("pool_d"), 1)

        def pool_lo(dve, f):
            dve.wait_ge(s("pool_hi"), 2 * f + 2)
            for c0, w in STREAMS:
                nc.vector.scalar_tensor_tensor(out=hT_lo[:, f, c0:c0 + w], in0=bank(4 + 2 * (f % 2), 1024)[:, c0:c0 + w],
                                               scalar=cols[:, 48 + f:49 + f], in1=hT_hi[:, f, c0:c0 + w].bitcast(F32),
                                               op0=ALU.mult, op1=ALU.subtract).then_inc(s("pool_out"), 2)

        def attn_setup(l):
            groups = attention_groups(l)
            first = [0]
            for g in groups:
                first.append(first[-1] + len(g[2]))
            return groups, attention_steps(groups, INTERLEAVE[l]), first

        mx, negm, den, rden, esink = (small[:, i, :] for i in range(5))

        def attn_tensor(pe, l, before):
            groups, steps, first = attn_setup(l)
            q_t = (q0T[:, :, :], qT[:, :].rearrange("p (h n) -> p h n", h=C_HEADS))[l]
            k_t = (k0T, kT)[l]
            v_hl = (v0, v1)[l]
            per = 2 if l == 0 else 1
            after_phase(pe, before)
            for kind, g, i in steps:
                j, n, keys, masks = groups[g]
                if kind == "S":
                    h = 4 * g + i
                    if h >= 2:
                        pe.wait_ge(s(f"exp_done{l}"), per * (h - 2) + 1)
                    sc = bank(2 * (h % 2), 1024)
                    lhs = q_t[:, GROUP * j + i, n * P:(n + 1) * P]
                    pieces = key_pieces(keys)
                    for part in range(2):
                        for p0, k0, w in pieces:
                            mm = nc.tensor.matmul(sc[:, p0:p0 + w], lhs, k_t[:, part, j, k0:k0 + w],
                                                  start=part == 0 and p0 % BANK == 0, stop=part == 1,
                                                  skip_group_check=True)
                    for c, t in enumerate(keys):
                        if t in masks:
                            mm = nc.tensor.matmul(sc[:, c * P:(c + 1) * P], ident_b[:, :], mask_b[:, masks[t], :],
                                                  start=False, stop=True, skip_group_check=True)
                    mm.then_inc(s(f"scores{l}"), 1)
                elif kind == "T":
                    cg = first[g] + i
                    pe.wait_ge(s(f"prob_norm{l}"), 4 * g + 4)
                    if cg >= 2:
                        pe.wait_ge(s(f"pT_lo{l}"), cg - 1)
                    for h in range(GROUP):
                        mm = nc.tensor.transpose(bank(4 + cg % 2)[:, h * P:(h + 1) * P],
                                                 prob[:, g % 2, h, i * P:(i + 1) * P], ident[:, :])
                    mm.then_inc(s(f"prob_turned{l}"), 1)
                elif kind == "V":
                    cg = first[g] + i
                    pe.wait_ge(s(f"pT_lo{l}"), cg + 1)
                    if i == 0 and g >= 2:
                        pe.wait_ge(s(f"o_sum{l}"), 2 * (g - 1))
                    vt = v_hl[:, keys[i], j, :, :].rearrange("p a d -> p (a d)")
                    nc.tensor.matmul(bank(6 + g % 2), vt, pT_hi[:, cg % PT, :], start=i == 0, stop=False,
                                     skip_group_check=True)
                    mm = nc.tensor.matmul(bank(6 + g % 2), vt, pT_lo[:, cg % PT, :], start=False,
                                          stop=i == len(keys) - 1, skip_group_check=True)
                    mm.then_inc(s(f"pv{l}"), 1)
            close(pe, "pe")

        def attn_scalar(act, l, before):
            groups, steps, first = attn_setup(l)
            after_phase(act, before)
            per = 3 if l == 0 else 2
            for kind, g, i in steps:
                j, n, keys, masks = groups[g]
                h = 4 * g + i
                if kind == "E":
                    act.wait_ge(s(f"smax{l}"), h + 1)
                    W = len(keys) * P
                    nc.scalar.activation(prob[:, g % 2, i, 0:W], bank(2 * (h % 2), 1024)[:, 0:W], ACT.Exp,
                                         bias=negm[:, h:h + 1], scale=SCALE if l == 0 else 1.0,
                                         accum_out=den[:, h:h + 1]).then_inc(s(f"exp_done{l}"), 1)
                    if l == 0:
                        nc.scalar.activation(esink[:, h:h + 1], nsink[:, GROUP * j + i:GROUP * j + i + 1], ACT.Exp,
                                             bias=negm[:, h:h + 1], scale=-1.0).then_inc(s(f"exp_done{l}"), 1)
                elif kind == "T":
                    cg = first[g] + i
                    act.wait_ge(s(f"prob_turned{l}"), cg + 1)
                    if cg >= PT:
                        act.wait_ge(s(f"pv{l}"), cg - PT + 1)
                    nc.scalar.activation(pT_hi[:, cg % PT, :], bank(4 + cg % 2), ACT.Copy).then_inc(s(f"pT_hi{l}"), 1)
                    if cg == first[-1] - 1:
                        split_hi(act, f"out{l}", 0, 1024, free=False)
                elif kind == "O":
                    act.wait_ge(s(f"pv{l}"), first[g + 1])
                    if g >= 2:
                        act.wait_ge(s(f"o_split{l}"), 2 * (g - 1))
                    for odd in range(2):
                        other = 64 * (1 - odd)
                        src = ps[other:other + HD, 6 + g % 2, :].rearrange("p (a b n) -> p a b n", a=2, b=2)
                        nc.scalar.activation(o_tmp[64 * odd:64 * odd + 64, g % 2, :, :], src[:, :, odd, :],
                                             ACT.Copy).then_inc(s(f"o_read{l}"), 1)
            close(act, "act")

        def attn_vector(dve, l, before):
            groups, steps, first = attn_setup(l)
            after_phase(dve, before)
            nden = 2 if l == 0 else 1

            def denominator(h):
                dve.wait_ge(s(f"exp_done{l}"), nden * h + nden)
                d = den
                if l == 0:
                    nc.vector.tensor_tensor(rden[:, h:h + 1], den[:, h:h + 1], esink[:, h:h + 1],
                                            ALU.add).then_inc(s(f"rden{l}"), 1)
                    dve.wait_ge(s(f"rden{l}"), 2 * h + 1)
                    d = rden
                nc.vector.reciprocal(rden[:, h:h + 1], d[:, h:h + 1]).then_inc(s(f"rden{l}"), 1)

            for kind, g, i in steps:
                j, n, keys, masks = groups[g]
                h = 4 * g + i
                if kind == "S":
                    dve.wait_ge(s(f"scores{l}"), h + 1)
                    sc = bank(2 * (h % 2), 1024)[:, 0:len(keys) * P]
                    if l == 0:
                        nc.vector.reduce_max(mx[:, h:h + 1], sc, AX_X).then_inc(s("smax_raw"), 1)
                        dve.wait_ge(s("smax_raw"), h + 1)
                        nc.vector.scalar_tensor_tensor(out=negm[:, h:h + 1], in0=mx[:, h:h + 1], scalar=-SCALE,
                                                       in1=nsink[:, GROUP * j + i:GROUP * j + i + 1],
                                                       op0=ALU.mult, op1=ALU.min).then_inc(s("smax0"), 1)
                    else:
                        nc.vector.tensor_reduce(negm[:, h:h + 1], sc, AX_X, ALU.max, negate=True).then_inc(s("smax1"), 1)
                elif kind == "D":
                    denominator(h)
                elif kind == "T":
                    cg = first[g] + i
                    dve.wait_ge(s(f"pT_hi{l}"), cg + 1)
                    nc.vector.tensor_tensor(pT_lo[:, cg % PT, :], bank(4 + cg % 2), pT_hi[:, cg % PT, :].bitcast(F32),
                                            ALU.subtract).then_inc(s(f"pT_lo{l}"), 1)
                    if cg == first[-1] - 1:
                        split_lo(dve, f"out{l}", 0, 1024, by=nc.vector)
                elif kind == "O":
                    dve.wait_ge(s(f"o_read{l}"), 2 * g + 2)
                    for odd in range(2):
                        rows = slice(64 * odd, 64 * odd + 64)
                        src = ps[rows, 6 + g % 2, :].rearrange("p (a b n) -> p a b n", a=2, b=2)
                        nc.vector.tensor_tensor(o_tmp[rows, g % 2, :, :], o_tmp[rows, g % 2, :, :], src[:, :, odd, :],
                                                ALU.add).then_inc(s(f"o_sum{l}"), 1)
                    if g == len(groups) - 1:
                        dve.wait_ge(s(f"o_split{l}"), 2 * g)
                        split_output(dve, l, groups, g)
            close(dve, "dve")

        def split_output(eng, l, groups, g):
            j, n = groups[g][0:2]
            c_first = 4 if l == 0 else 0
            eng.wait_ge(s(f"o_sum{l}"), 2 * g + 2)
            cc = slice(c_first + 2 * j, c_first + 2 * j + 2)
            tt = slice(n * P, (n + 1) * P)
            eng.tensor_copy(hT_hi[:, cc, tt], o_tmp[:, g % 2, :, :]).then_inc(s(f"o_split{l}"), 1)
            eng.wait_ge(s(f"o_split{l}"), 2 * g + 1)
            eng.tensor_tensor(hT_lo[:, cc, tt], o_tmp[:, g % 2, :, :], hT_hi[:, cc, tt].bitcast(F32),
                              ALU.subtract).then_inc(s(f"o_split{l}"), 1)

        def attn_pool(pool, l, before):
            groups, steps, first = attn_setup(l)
            after_phase(pool, before)
            per = 2 if l == 0 else 1
            for kind, g, i in steps:
                j, n, keys, masks = groups[g]
                if kind == "D":
                    h = 4 * g + i
                    pool.wait_ge(s(f"rden{l}"), per * (h + 1))
                    pr = prob[:, g % 2, i, 0:len(keys) * P]
                    nc.gpsimd.tensor_scalar(pr, pr, rden[:, h:h + 1], 1.0, ALU.mult,
                                            ALU.mult).then_inc(s(f"prob_norm{l}"), 1)
                elif kind == "O" and g < len(groups) - 1:
                    split_output(pool, l, groups, g)
            close(pool, "pool")

        def gate_tensor(pe, l, tag, sub, halves):
            for i in halves:
                v, half = divmod(i, 2)
                row = ada_row(l, (2, 5)[sub], v)
                if i >= 2:
                    pe.wait_ge(s(f"{tag}_gate"), i - 1)
                nc.tensor.matmul(bank(6 + i % 2), ident[:, row:row + 1].broadcast_to([P, P]),
                                 gate_rows[:, half * BANK:(half + 1) * BANK],
                                 start=True, stop=True, skip_group_check=True).then_inc(s(f"{tag}_gate_mm"), 1)

        def gate_scalar(act, tag, halves):
            for i in halves:
                v, half = divmod(i, 2)
                act.wait_ge(s(f"{tag}_gate_mm"), i + 1)
                nc.scalar.activation(gate[:, v, half * BANK:(half + 1) * BANK], bank(6 + i % 2),
                                     ACT.Copy).then_inc(s(f"{tag}_gate"), 1)

        def first_half_scalar(act, tag, t, acc, y0_, sqj_):
            nc.scalar.activation(y0_[:, t, :], acc, ACT.Copy).then_inc(s(f"{tag}_y0"), 1)

        def square_scalar(act, tag, half, t, nt, src, sqj_):
            i = half * nt + t
            if i >= 2:
                act.wait_ge(s(f"{tag}_ysq"), i - 1)
            nc.scalar.activation(sqj_[:, i % 2, :], src, ACT.Square,
                                 accum_out=ssum[:, half, t:t + 1]).then_inc(s(f"{tag}_ysq"), 1)

        def post_pool(pool, tag, nt, then):
            for t in range(nt):
                pool.wait_ge(s(f"{tag}_ysq"), nt + t + 1)
                nc.gpsimd.tensor_tensor(ssum[:, 0, t:t + 1], ssum[:, 0, t:t + 1], ssum[:, 1, t:t + 1],
                                        ALU.add).then_inc(s(f"{tag}_yr"), 1)
                pool.wait_ge(s(f"{tag}_yr"), 3 * t + 1)
                nc.gpsimd.tensor_scalar(ssum[:, 0, t:t + 1], ssum[:, 0, t:t + 1], 1.0 / D, EPS, ALU.mult,
                                        ALU.add).then_inc(s(f"{tag}_yr"), 1)
                pool.wait_ge(s(f"{tag}_yr"), 3 * t + 2)
                nc.gpsimd.tensor_tensor(rms[:, t:t + 1], ssum[:, 0, t:t + 1], minus_half[:, 0:1],
                                        ALU.pow).then_inc(s(f"{tag}_yr"), 1)
                if then and t:
                    x_rms(pool, then, t - 1)
            if then:
                x_rms(pool, then, nt - 1)

        def post_count(nt, t, step):
            return nt + 3 * t + step

        def first_half_vector(dve, tag, nt, y0_):
            post = s(f"{tag}_post")
            dve.wait_ge(s(f"{tag}_gate"), 2 * (2 if nt == ALL_T else 1))
            for t in range(nt):
                dve.wait_ge(s(f"{tag}_ysq"), t + 1)
                nc.vector.tensor_tensor(y0_[:, t, :], y0_[:, t, :], gate[:, int(t >= LAT_T), 0:BANK],
                                        ALU.mult).then_inc(post, 1)

        def post_vector(dve, tag, nt, acc_of, y0_, temps, then):
            post = s(f"{tag}_post")
            for t in range(nt):
                y1 = temps[t % 2][:, :]
                dve.wait_ge(s(f"{tag}_ysq"), nt + t + 1)
                if t >= 2:
                    dve.wait_ge(post, post_count(nt, t - 2, 3))
                nc.vector.tensor_tensor(y1, acc_of(t), gate[:, int(t >= LAT_T), BANK:D], ALU.mult).then_inc(post, 1)
                dve.wait_ge(s(f"{tag}_yr"), 3 * t + 3)
                dve.wait_ge(post, post_count(nt, t, 1))
                for half, y in enumerate((y0_[:, t, :], y1)):
                    xv = x[:, t, half * BANK:(half + 1) * BANK]
                    nc.vector.scalar_tensor_tensor(out=xv, in0=y, scalar=rms[:, t:t + 1], in1=xv,
                                                   op0=ALU.mult, op1=ALU.add).then_inc(post, 1)
                if then and t and not by_scalar(then, nt, t - 1):
                    x_normed(dve, then, t - 1)
            if then:
                x_normed(dve, then, nt - 1)

        def out_prefetch_scalar(act, l):
            for m in range(1, 4):
                split_hi(act, f"out{l}", m, 1024, free=False)

        def out_sync(sp, l):
            w = (ab_w_out, c_w_out)[l][0]
            n = 2 * KC
            for m in range(8):
                half, u = divmod(m, 4)
                load_unit(sp, f"out{l}", m, w[2 * u * P:(2 * u + 2) * P, half * BANK:(half + 1) * BANK]
                          .rearrange("(k p) n -> p k n", p=P), 1024)
                if l == 0 and 2 <= m < 7:
                    if m == 2:
                        after_phase(sp, 5)
                    more = 2 if m < 6 else 8
                    ada_loads(sp, beside_out, n, n + more)
                    n += more
                    if m == 2:
                        ada_small_loads(sp, beside_out, 0, (4, 5))

        def out_tensor(pe, l, before, nt):
            phase, tag = f"out{l}", f"mixpost{l}"
            after_phase(pe, before)
            for half in range(2):
                for t in range(nt):
                    n = half * nt + t
                    if n >= 4:
                        if n - 4 < nt:
                            pe.wait_ge(s(f"{tag}_y0"), n - 3)
                        else:
                            pe.wait_ge(s(f"{tag}_post"), post_count(nt, n - 4 - nt, 2))
                    for k in range(KC):
                        m = 4 * half + k // 2
                        if t == 0 and k % 2 == 0:
                            wait_split(pe, phase, m)
                        slot, c0 = unit_slot(phase, m), (k % 2) * BANK
                        tt = slice(t * P, (t + 1) * P)
                        mm = mm3(bank(n % 4), hT_hi[:, k, tt], hT_lo[:, k, tt], w_hi[:, slot, c0:c0 + BANK],
                                 w_lo[:, slot, c0:c0 + BANK], k == 0, k == KC - 1)
                        if t == nt - 1 and k in (1, 3, 5):
                            mm.then_inc(used[phase], 1)
                    mm.then_inc(s(f"{tag}_acc"), 1)
                    if n == 0:
                        gate_tensor(pe, l, tag, 0, range(4 if nt == ALL_T else 2))
                    if l == 0 and n == 3:
                        ada_sum(pe, beside_out, 4)
                    elif l == 0 and n == 6:
                        ada_sum(pe, beside_out, 5)
                    elif l == 0 and n == 7:
                        ada_turn(pe, 3, 4)
                pe.drain().then_inc(used[phase], 1)
            close(pe, "pe")

        def out_scalar(act, l, before, nt):
            phase, tag = f"out{l}", f"mixpost{l}"
            after_phase(act, before)
            out_prefetch_scalar(act, l)
            gate_scalar(act, tag, range(4 if nt == ALL_T else 2))
            for t in range(nt):
                if t == nt - 1:
                    for m in range(4, 7):
                        split_hi(act, phase, m, 1024)
                act.wait_ge(s(f"{tag}_acc"), t + 1)
                first_half_scalar(act, tag, t, bank(t % 4), y0, sqj)
                act.wait_ge(s(f"{tag}_y0"), t + 1)
                square_scalar(act, tag, 0, t, nt, y0[:, t, :], sqj)
            split_hi(act, phase, 7, 1024)
            for t in range(nt):
                act.wait_ge(s(f"{tag}_acc"), nt + t + 1)
                square_scalar(act, tag, 1, t, nt, bank((nt + t) % 4), sqj)
                x_squares(act, f"ffn{l}", tag, nt, t)
            x_squares(act, f"ffn{l}", tag, nt, nt)
            close(act, "act")

        def out_pool(pool, l, before, nt):
            after_phase(pool, before)
            if l == 0:
                for m in range(4, 8):
                    split_lo(pool, "out0", m, 1024)
            post_pool(pool, f"mixpost{l}", nt, f"ffn{l}")
            close(pool, "pool")

        def out_vector(dve, l, before, nt):
            after_phase(dve, before)
            for m in range(1, 4):
                split_lo(dve, f"out{l}", m, 1024, by=nc.vector)
            if l == 0:
                ada_macs(dve, beside_out, (4, 5))
            else:
                for m in range(4, 8):
                    split_lo(dve, f"out{l}", m, 1024, by=nc.vector)
            if l == 0:
                dve.wait_ge(s("ada_sum"), 6)
                dve.wait_ge(s("mixpost0_gate_mm"), 4)
                ada_bias(dve, beside_out, 3, 8, 64, 4, psf[64:68, 4 * BANK:6 * BANK])
                ada_columns(dve, 3, 0, (4, 5), 4)
                ada_gates(dve, beside_out, 3, 64, 4)
            first_half_vector(dve, f"mixpost{l}", nt, y0)
            post_vector(dve, f"mixpost{l}", nt, lambda t: bank((nt + t) % 4), y0, (t0, t1), f"ffn{l}")
            close(dve, "dve")

        TURN = 6
        TURNS = 2 * FT // TURN

        def up_sync(sp, l):
            def turn(i, with_ada):
                for m in range(TURN):
                    c0 = (m // 2) * P + (m % 2) * DFF
                    src = ffn_w_up[l][:, bass.ds(i * (3 * P) + c0, P)].rearrange("(k p) n -> p k n", p=P)
                    load_unit(sp, f"up{l}", m, src, 1024, i, TURN)
                    if with_ada and m >= 2:
                        if m == 2:
                            after_phase(sp, 6)
                        for k in (2 * m - 4, 2 * m - 3):
                            ada_load(sp, 4 * KC + k, beside_up, 1, slice(k * P, (k + 1) * P), bass.ds(i * D, D), i)

            with sp.Fori(0, TURNS - 1) as i:
                turn(i, l == 0)
            turn(TURNS - 1, False)

        def up_prefetch(l):
            def act_part(act, units):
                for m in units:
                    if m < 3:
                        split_hi(act, f"up{l}", m, 1024, free=False)

            def pool_part(pool):
                for m in range(3):
                    split_lo(pool, f"up{l}", m, 1024)
            return act_part, pool_part

        def up_first(pe, l, nt, tag):
            def chunk(k):
                pe.wait_ge(s(f"{tag}_split"), 2 * (k + 1))
                if k == 0:
                    wait_split(pe, f"up{l}", 0)
                kk = slice(k * P, (k + 1) * P)
                for c0, w in STREAMS[:1 if nt == LAT_T else 2]:
                    mm = mm3(bank(0, 1024)[:, c0:c0 + w], w_hi[:, 0, kk], w_lo[:, 0, kk],
                             hT_hi[:, k, c0:c0 + w], hT_lo[:, k, c0:c0 + w], k == 0, k == KC - 1)
                if k == KC - 1:
                    mm.then_inc(used[f"up{l}"], 1)
            return chunk

        def up_tensor(pe, l, nt):
            phase = f"up{l}"
            streams = STREAMS[:1 if nt == LAT_T else 2]
            if l == 0:
                for half in range(2):
                    nc.tensor.matmul(ps[96:128, 6 + half, :], select[:, 0:32],
                                     rope[:, :, :, :].rearrange("p a t n -> p (a t n)")[:, 0:BANK],
                                     start=True, stop=True, skip_group_check=True)

            def turn(i, with_ada, first=0, ada_streams=1):
                for m in range(first, TURN):
                    wait_split(pe, phase, m, i, TURN)
                    pe.wait_ge(s(f"taps{l}"), i * TURN + (m + 1))
                    slot = unit_slot(phase, m)
                    acc = bank(2 * (m % 3), 1024)
                    for k in range(KC):
                        kk = slice(k * P, (k + 1) * P)
                        for c0, w in streams:
                            mm = mm3(acc[:, c0:c0 + w], w_hi[:, slot, kk], w_lo[:, slot, kk],
                                     hT_hi[:, k, c0:c0 + w], hT_lo[:, k, c0:c0 + w], k == 0, k == KC - 1)
                    mm.then_inc(used[phase], 1)
                if with_ada:
                    pe.wait_ge(s("ada_mac"), i * (2 * KC) + (START_MACS + 10 * KC))
                    pe.wait_ge(s("ada_selector"), i * 2 + 2)
                    for v in range(ada_streams):
                        for half in range(2):
                            mm = nc.tensor.matmul(ps[96:128, 6 + half, :], select_v[:, v, :],
                                                  beside_up[0][:, v, half * BANK:(half + 1) * BANK],
                                                  start=False, stop=True, skip_group_check=True)
                    mm.then_inc(s("ada_sum"), 1)

            turn(0, l == 0, first=1, ada_streams=2)
            if l == 0:
                turn(1, True, ada_streams=2)
            with pe.Fori(2 if l == 0 else 1, TURNS - 1) as i:
                turn(i, l == 0)
            turn(TURNS - 1, False)
            close(pe, "pe")

        def up_scalar(act, l, before, nt):
            phase = f"up{l}"
            T = nt * P
            after_phase(act, before)
            act.sem_inc(s(f"gated{l}"), 1)
            act.sem_inc(s(f"gelu{l}"), 1)

            def turn(i, last):
                for m in range(TURN):
                    b = m % 2
                    col = i * 3 + (m // 2 + b * FT)
                    act.wait_ge(used[phase], i * TURN + (m + 1))
                    act.wait_ge(s(f"gated{l}") if b else s(f"gelu{l}"), i * 3 + (m // 2 + 1))
                    nc.scalar.activation((conv_a, conv_b)[b][:, 0:T], bank(2 * (m % 3), 1024)[:, 0:T], ACT.Identity,
                                         bias=convb[:, l, bass.ds(col, 1)],
                                         scale=convw[l][:, 1, bass.ds(col, 1)]).then_inc(s(f"center{l}"), 1)
                    if not (last and m >= TURN - 3):
                        split_hi(act, phase, m + 3, 1024, i, TURN)
                    else:
                        split_hi(act, f"down{l}", m - (TURN - 3), BANK, free=False)
                    if not b:
                        act.wait_ge(s(f"taps{l}"), i * TURN + (m + 4))
                        act.wait_ge(s(f"gated{l}"), i * 3 + (m // 2 + 1))
                        nc.scalar.activation(gelu[:, 0:T], conv_a[:, 0:T], ACT.Gelu_apprx_tanh).then_inc(s(f"gelu{l}"), 1)

            with act.Fori(0, TURNS - 1) as i:
                turn(i, False)
            turn(TURNS - 1, True)
            for m in range(3):
                down_activation(act, l, nt, m, 0)
            close(act, "act")

        def up_pool(pool, l, before):
            after_phase(pool, before)
            with pool.Fori(0, TURNS - 1) as i:
                for m in range(3, 3 + TURN):
                    split_lo(pool, f"up{l}", m, 1024, i, TURN)
            for m in range(3, TURN):
                split_lo(pool, f"up{l}", m + TURN * (TURNS - 1), 1024)
            for m in range(3):
                split_lo(pool, f"down{l}", m, BANK)
            close(pool, "pool")

        def up_vector(dve, l, before, nt):
            streams = STREAMS[:1 if nt == LAT_T else 2]
            T = nt * P
            ns = len(streams)
            after_phase(dve, before)
            dve.sem_inc(s(f"taps{l}"), 3)

            def turn(i, with_ada):
                if with_ada:
                    dve.wait_ge(s("ada_sum"), i + 6)
                    for v in range(2):
                        nc.vector.tensor_copy(select_v[:, v, :], select[:, bass.ds(i * 2 + (22 - v), 32)]
                                              ).then_inc(s("ada_selector"), 1)
                for m in range(TURN):
                    b = m % 2
                    col = i * 3 + (m // 2 + b * FT)
                    dve.wait_ge(s(f"center{l}"), i * TURN + (m + 1))
                    cv = (conv_a, conv_b)[b]
                    acc = bank(2 * (m % 3), 1024)
                    for c0, w in streams:
                        nc.vector.scalar_tensor_tensor(out=cv[:, c0 + 1:c0 + w], in0=acc[:, c0:c0 + w - 1],
                                                       scalar=convw[l][:, 0, bass.ds(col, 1)], in1=cv[:, c0 + 1:c0 + w],
                                                       op0=ALU.mult, op1=ALU.add).then_inc(s(f"tap0_{l}"), 1)
                    for v, (c0, w) in enumerate(streams):
                        dve.wait_ge(s(f"tap0_{l}"), i * (TURN * ns) + (m * ns + v + 1))
                        op = nc.vector.scalar_tensor_tensor(out=cv[:, c0:c0 + w - 1], in0=acc[:, c0 + 1:c0 + w],
                                                            scalar=convw[l][:, 2, bass.ds(col, 1)], in1=cv[:, c0:c0 + w - 1],
                                                            op0=ALU.mult, op1=ALU.add)
                        if v == ns - 1:
                            op.then_inc(s(f"taps{l}"), 1)
                    if b:
                        dve.wait_ge(s(f"taps{l}"), i * TURN + (m + 4))
                        dve.wait_ge(s(f"gelu{l}"), i * 3 + (m // 2 + 2))
                        nc.vector.tensor_tensor(act_g[:, bass.ds(i * 3 + m // 2, 1), 0:T].rearrange("p a n -> p (a n)"),
                                                gelu[:, 0:T], conv_b[:, 0:T], ALU.mult).then_inc(s(f"gated{l}"), 1)
                    if l == 0 and not with_ada and m == 1:
                        dve.wait_ge(s("ada_sum"), 12)
                        nc.vector.tensor_copy(gate_rows[96:128, :], psf[96:128, 6 * BANK:8 * BANK])
                    if with_ada and m < 4:
                        for k in (2 * m, 2 * m + 1):
                            ada_mac(dve, beside_up, 4 * KC + k, k, i)

            with dve.Fori(0, TURNS - 1) as i:
                turn(i, l == 0)
            turn(TURNS - 1, False)
            close(dve, "dve")

        DTURNS = FT // 3

        def down_sync(sp, l):
            for half in range(2):
                if l == 0 and half:
                    after_phase(sp, 8)
                    ada_small_loads(sp, beside_up, 1, range(6))
                with sp.Fori(0, DTURNS) as i:
                    for m in range(3):
                        src = ffn_w_down[l][bass.ds(i * (3 * P) + m * P, P), half * BANK:(half + 1) * BANK]
                        load_unit(sp, f"down{l}", half * FT + m, src, BANK, i, 3)

        def down_tensor(pe, l, before, nt):
            phase, tag = f"down{l}", f"ffnpost{l}"
            after_phase(pe, before)
            gate_tensor(pe, l, tag, 1, (0, 1))

            def unit(i, m, half, first, last, tiles):
                slot = unit_slot(phase, m)
                for t in tiles:
                    if half and first:
                        pe.wait_ge(s(f"{tag}_y0"), t + 1)
                    tt = slice(t * P, (t + 1) * P)
                    mm = mm3(bank(t), g_hi[:, slot, tt], g_lo[:, slot, tt], w_hi[:, slot, 0:BANK],
                             w_lo[:, slot, 0:BANK], first, last)
                return mm

            def ready(i, m, half):
                wait_split(pe, phase, half * FT + m, i, 3)
                pe.wait_ge(s(f"g_lo{l}"), i * 3 + (half * FT + m + 1))

            for half in range(2):
                for m in range(3):
                    ready(0, m, half)
                    unit(0, m, half, m == 0, False, range(nt)).then_inc(used[phase], 1)
                if half == 0 and nt == ALL_T:
                    gate_tensor(pe, l, tag, 1, (2, 3))
                if l == 0 and half == 1:
                    pe.wait_ge(s(f"{tag}_gate"), 4)
                    ada_turn(pe, 4, 6)
                with pe.Fori(1, DTURNS - 1) as i:
                    for m in range(3):
                        ready(i, m, half)
                        unit(i, m, half, False, False, range(nt)).then_inc(used[phase], 1)
                if half == 0:
                    ready(DTURNS - 1, 0, half)
                    unit(DTURNS - 1, 0, half, False, False, range(nt)).then_inc(used[phase], 1)
                for t in range(nt):
                    for m in range(1 - half, 3):
                        if t == 0:
                            ready(DTURNS - 1, m, half)
                        mm = unit(DTURNS - 1, m, half, False, m == 2, (t,))
                        if half == 0 and m == 1 and t == nt - 1:
                            mm.then_inc(used[phase], 1)
                    mm.then_inc(s(f"{tag}_acc"), 1)
                pe.drain().then_inc(used[phase], 3 if half else 1)
            close(pe, "pe")

        def down_split(act, l, nt, half, m, i=0):
            split_hi(act, f"down{l}", half * FT + m, BANK, i, 3)
            down_activation(act, l, nt, m, i)

        def down_activation(act, l, nt, m, i):
            T = nt * P
            nc.scalar.activation(g_hi[:, m, 0:T], act_g[:, bass.ds(i * 3 + m, 1), 0:T].rearrange("p a n -> p (a n)"),
                                 ACT.Copy).then_inc(s(f"g_hi{l}"), 1)

        def down_scalar(act, l, before, nt):
            tag = f"ffnpost{l}"
            after_phase(act, before)
            for half in range(2):
                if half == 0:
                    gate_scalar(act, tag, (0, 1))
                with act.Fori(1, DTURNS) as i:
                    for m in range(3):
                        down_split(act, l, nt, half, m, i)
                if half == 0:
                    down_split(act, l, nt, 1, 0, 0)
                for t in range(nt):
                    act.wait_ge(s(f"{tag}_acc"), half * nt + t + 1)
                    if half == 0:
                        first_half_scalar(act, tag, t, bank(t), y0d, sqjd)
                    else:
                        square_scalar(act, tag, 1, t, nt, bank(t), sqjd)
                        if l == 0:
                            x_squares(act, "mix1", tag, nt, t)
                if half == 0:
                    for m in range(1, 3):
                        down_split(act, l, nt, 1, m, 0)
                    if nt == ALL_T:
                        gate_scalar(act, tag, (2, 3))
                    for t in range(nt):
                        act.wait_ge(s(f"{tag}_y0"), t + 1)
                        square_scalar(act, tag, 0, t, nt, y0d[:, t, :], sqjd)
            if l == 0:
                x_squares(act, "mix1", tag, nt, nt)
            close(act, "act")

        def down_pool(pool, l, before, nt):
            after_phase(pool, before)
            for half in range(2):
                with pool.Fori(1 - half, DTURNS) as i:
                    for m in range(3):
                        split_lo(pool, f"down{l}", half * FT + m, BANK, i, 3)
            post_pool(pool, f"ffnpost{l}", nt, None if l else "mix1")
            close(pool, "pool")

        def down_vector(dve, l, before, nt):
            T = nt * P
            after_phase(dve, before)
            def split_activations(half, first, last):
                with dve.Fori(first, last) as i:
                    for m in range(3):
                        dve.wait_ge(s(f"g_hi{l}"), i * 3 + (half * FT + m + 1))
                        nc.vector.tensor_tensor(g_lo[:, m, 0:T],
                                                act_g[:, bass.ds(i * 3 + m, 1), 0:T].rearrange("p a n -> p (a n)"),
                                                g_hi[:, m, 0:T].bitcast(F32), ALU.subtract).then_inc(s(f"g_lo{l}"), 1)

            split_activations(0, 0, DTURNS)
            if l == 0:
                dve.wait_ge(s("ffnpost0_gate_mm"), 4)
                ada_bias(dve, beside_up, 4, 16, 96, 12, gate_rows[96:108, :])
            split_activations(1, 0, DTURNS // 2)
            if l == 0:
                ada_columns(dve, 4, 1, range(6), 6)
                ada_gates(dve, beside_up, 4, 96, 12)
            first_half_vector(dve, f"ffnpost{l}", nt, y0d)
            split_activations(1, DTURNS // 2, DTURNS)
            post_vector(dve, f"ffnpost{l}", nt, bank, y0d, (t0d, t1d), None if l else "mix1")
            close(dve, "dve")

        block = es.enter_context(nc.Block())
        NT = {0: ALL_T, 1: LAT_T}

        @block.sync
        def _(sp):
            setup_sync(sp)
            for q in range(1, 4):
                start_load(sp, q)
            x_sync(sp)
            ada_small_loads(sp, (None, None, start_bias), 0, (0, 1))
            for q in range(4, 8):
                start_load(sp, q)
            late_sync(sp)
            for l in range(2):
                proj_sync(sp, l)
                out_sync(sp, l)
                up_sync(sp, l)
                down_sync(sp, l)
                if l == 0:
                    for i, g in enumerate((c_q_g, c_k_g)):
                        sp.dma_start(qk_gain[:, i, :], g[0].partition_broadcast(P)).then_inc(s("gain_landed"), 16)
            for t in range(LAT_T):
                sp.wait_ge(s("ffnpost1_post"), post_count(LAT_T, t, 3))
                sp.dma_start(out[0, t * P:(t + 1) * P, :], x[:, t, :]).then_inc(store_done, 16)
            sp.wait_ge(store_done, 16 * LAT_T)

        @block.tensor
        def _(pe):
            setup_tensor(pe)
            after_phase(pe, 1)
            start_tensor(pe)
            for l in range(2):
                b = 7 * l
                norm_tensor(pe, f"mix{l}", b + 2, ALL_T, 0, proj_first(pe, l, f"mix{l}"))
                proj_tensor(pe, l)
                attn_tensor(pe, l, b + 4)
                out_tensor(pe, l, b + 5, NT[l])
                norm_tensor(pe, f"ffn{l}", b + 6, NT[l], 4, up_first(pe, l, NT[l], f"ffn{l}"))
                up_tensor(pe, l, NT[l])
                down_tensor(pe, l, b + 8, NT[l])

        @block.scalar
        def _(act):
            setup_scalar(act)
            start_scalar(act)
            for l in range(2):
                b = 7 * l
                norm_scalar(act, f"mix{l}", b + 2, 0, ALL_T, 0, proj_prefetch(l)[0])
                proj_scalar(act, l, b + 3)
                attn_scalar(act, l, b + 4)
                out_scalar(act, l, b + 5, NT[l])
                norm_scalar(act, f"ffn{l}", b + 6, 1, NT[l], 4, up_prefetch(l)[0])
                up_scalar(act, l, b + 7, NT[l])
                down_scalar(act, l, b + 8, NT[l])

        @block.gpsimd
        def _(pool):
            close(pool, "pool")
            start_pool(pool)
            for l in range(2):
                b = 7 * l
                norm_pool(pool, f"mix{l}", b + 2, ALL_T, proj_prefetch(l)[1])
                proj_pool(pool, l, b + 3)
                attn_pool(pool, l, b + 4)
                out_pool(pool, l, b + 5, NT[l])
                norm_pool(pool, f"ffn{l}", b + 6, NT[l], up_prefetch(l)[1])
                up_pool(pool, l, b + 7)
                down_pool(pool, l, b + 8, NT[l])

        @block.vector
        def _(dve):
            setup_vector(dve)
            after_phase(dve, 1)
            start_vector(dve)
            for l in range(2):
                b = 7 * l
                norm_vector(dve, f"mix{l}", b + 2, ALL_T)
                proj_vector(dve, l, b + 3)
                attn_vector(dve, l, b + 4)
                out_vector(dve, l, b + 5, NT[l])
                norm_vector(dve, f"ffn{l}", b + 6, NT[l])
                up_vector(dve, l, b + 7, NT[l])
                down_vector(dve, l, b + 8, NT[l])


def shape_constants():
    import numpy as np

    ident = np.eye(P, dtype=np.float32)
    grid_w, n_freq = 64, HD // 4
    pos = np.arange(SEQ)
    freqs = np.float32(10000.0) ** (-np.arange(n_freq, dtype=np.float32) / np.float32(n_freq))
    ang = np.concatenate([(pos // grid_w).astype(np.float32)[:, None] * freqs,
                          (pos % grid_w).astype(np.float32)[:, None] * freqs], axis=-1)
    rope = np.zeros((2, TOK, HD), np.float32)
    rope[0] = 1.0
    rope[0, :SEQ] = np.tile(np.cos(ang), 2)
    rope[1, :SEQ] = np.tile(np.sin(ang), 2)
    q, k = np.arange(P)[:, None], np.arange(P)[None, :]
    mask = np.zeros((2, P, P), np.float32)
    mask[0][k < q] = -1e30
    mask[1][k > q] = -1e30
    edge = np.ones((4, 2, PAD), np.float32)
    for g, w in enumerate(POOL_WINDOWS):
        for i in range(PAD):
            edge[g, 0, i] = w / (min(i, w // 2) + w // 2)
            edge[g, 1, PAD - 1 - i] = w / (w // 2 + min(i + 1, w // 2))
    return {"ident": ident, "rope": rope, "mask": mask, "edge": edge}


_INS = ["x", "c", "ctx", "c_ctx", "ada_w", "ada_b", "mix_pre_g", "mix_post_g", "ffn_pre_g", "ffn_post_g",
        "ab_w_in", "ab_w_out", "pool_w", "pool_scale", "sink_logit", "c_w_qkv", "c_w_out", "c_q_g", "c_k_g",
        "ffn_w_up", "ffn_conv_w", "ffn_conv_b", "ffn_w_down"]


def kernel(**inputs):
    import numpy as np
    import concourse.bacc as bacc
    from concourse.bass_utils import run_bass_kernel_spmd as run

    nc = bacc.Bacc("TRN2", target_bir_lowering=False, num_devices=1, dynamic_dma_scratch_size=1024)
    arrays = {f"in_{n}_dram": np.ascontiguousarray(inputs[n]) for n in _INS}
    arrays.update({f"const_{n}_dram": a for n, a in shape_constants().items()})
    args = [nc.dram_tensor(n, a.shape, mybir.dt.from_np(a.dtype), kind="ExternalInput").ap()
            for n, a in arrays.items()]
    args.append(nc.dram_tensor("out_dram", (1, SEQ, D), F32, kind="ExternalOutput").ap())
    hybrid_backbone_kernel(nc, *args)
    r = run(nc, [arrays], core_ids=[0])
    return r.results[0]["out_dram"]
```
